# Optimizing a Trainium2 kernel written in Bass

```python
import jax, jax.numpy as jnp
from jax import lax
import numpy as np

D_MODEL = 1024
BATCH = 1
SEQ = 1024
DEPTH = 1
DEC_BATCH = 8
DEC_SEQ = 1
PAST_LEN = 2048
PAGE_SIZE = 128

HEAD_DIM = 64
N_HEADS = 8
N_KV_HEADS = 2
GQA_GROUP = N_HEADS // N_KV_HEADS
ATTN_DIM = N_HEADS * HEAD_DIM
KV_DIM = N_KV_HEADS * HEAD_DIM
WINDOW = 128
BLOCK = WINDOW
CONV_DIM = D_MODEL - ATTN_DIM
CONV_GROUPS = 8
CONV_WIDTH = 3
MIX_DIM = ATTN_DIM + CONV_DIM
OFF_Q = 0
OFF_K = OFF_Q + ATTN_DIM
OFF_V = OFF_K + KV_DIM
OFF_B = OFF_V + KV_DIM
OFF_C = OFF_B + CONV_DIM
OFF_H = OFF_C + CONV_DIM
IN_PROJ_DIM = OFF_H + CONV_DIM
N_EXPERT_GROUPS = 4
EXPERTS_PER_GROUP = 4
N_EXPERTS = N_EXPERT_GROUPS * EXPERTS_PER_GROUP
TOP_K_FINE = 2
D_EXPERT = 256
RMS_EPS = 1e-5
NEG_INF = -1e30

kernel_name = "hymba_swa_sink_shortconv_hiermoe_step"

def rmsnorm(x, g):
    xf = x.astype(jnp.float32)
    y = xf * lax.rsqrt(jnp.mean(xf * xf, axis=-1, keepdims=True) + RMS_EPS)
    return (y * g.astype(jnp.float32)).astype(x.dtype)

def group_rmsnorm(x, g, n_groups):
    shp = x.shape
    xf = x.astype(jnp.float32).reshape(shp[:-1] + (n_groups, shp[-1] // n_groups))
    y = xf * lax.rsqrt(jnp.mean(xf * xf, axis=-1, keepdims=True) + RMS_EPS)
    return (y.reshape(shp) * g.astype(jnp.float32)).astype(x.dtype)

def sink_attention(q, k, v, valid, sinks):
    scores = jnp.einsum('...qkgd,...ckd->...kgqc', q, k).astype(jnp.float32) * (HEAD_DIM ** -0.5)
    scores = jnp.where(valid, scores, NEG_INF)
    sink = sinks.astype(jnp.float32).reshape(N_KV_HEADS, GQA_GROUP, 1, 1)
    m = jnp.maximum(scores.max(axis=-1, keepdims=True), sink)
    e = jnp.exp(scores - m)
    p = e / (e.sum(axis=-1, keepdims=True) + jnp.exp(sink - m))
    return jnp.einsum('...kgqc,...ckd->...qkgd', p.astype(v.dtype), v)

def banded_window_attention(q, k, v, sinks):
    n, s = q.shape[0], q.shape[1]
    nb = s // BLOCK
    qb = q.reshape(n, nb, BLOCK, N_KV_HEADS, GQA_GROUP, HEAD_DIM)

    def band(t):
        tb = t.reshape(n, nb, BLOCK, N_KV_HEADS, HEAD_DIM)
        prev = jnp.concatenate([jnp.zeros_like(tb[:, :1]), tb[:, :-1]], axis=1)
        return jnp.concatenate([prev, tb], axis=2)

    blk = jnp.arange(nb)[:, None, None]
    a = jnp.arange(BLOCK)[None, :, None]
    c = jnp.arange(2 * BLOCK)[None, None, :]
    diff = BLOCK + a - c
    key_pos = (blk - 1) * BLOCK + c
    valid = (diff >= 0) & (diff <= WINDOW) & (key_pos >= 0)
    out = sink_attention(qb, band(k), band(v), valid[None, :, None, None], sinks)
    return out.reshape(n, s, N_KV_HEADS, GQA_GROUP, HEAD_DIM)

def cached_window_attention(q, k, v, k_hist, v_hist, sinks):
    t = q.shape[1]
    wb = k_hist.shape[1]
    k_all = jnp.concatenate([k_hist, k], axis=1)
    v_all = jnp.concatenate([v_hist, v], axis=1)
    diff = wb + jnp.arange(t)[:, None] - jnp.arange(wb + t)[None, :]
    valid = (diff >= 0) & (diff <= WINDOW)
    out = sink_attention(q, k_all, v_all, valid[None, None, None], sinks)
    return out, k_all[:, -wb:], v_all[:, -wb:]

def causal_short_conv(u, u_hist, conv_w):
    t = u.shape[1]
    full = jnp.concatenate([u_hist, u], axis=1)
    z = sum(conv_w[j] * full[:, j:j + t] for j in range(CONV_WIDTH))
    return z, full[:, -(CONV_WIDTH - 1):]

def hierarchical_moe(xt, w_group, b_group, w_fine, b_fine, w_gate, w_up, w_down):
    nt = xt.shape[0]
    coarse = (xt @ w_group + b_group).astype(jnp.float32)
    p_group = jax.nn.softmax(coarse, axis=-1)
    g_sel = jnp.argmax(coarse, axis=-1)
    p_sel = jnp.take_along_axis(p_group, g_sel[:, None], axis=1)
    fine = (xt @ w_fine + b_fine).astype(jnp.float32).reshape(nt, N_EXPERT_GROUPS, EXPERTS_PER_GROUP)
    fine_sel = jnp.take_along_axis(fine, g_sel[:, None, None], axis=1)[:, 0]
    top_p, top_i = lax.top_k(jax.nn.softmax(fine_sel, axis=-1), TOP_K_FINE)
    top_p = top_p / top_p.sum(axis=-1, keepdims=True)
    expert_id = g_sel[:, None] * EXPERTS_PER_GROUP + top_i
    gates = jnp.einsum('nk,nke->ne', p_sel * top_p,
                       jax.nn.one_hot(expert_id, N_EXPERTS, dtype=jnp.float32)).astype(xt.dtype)
    hg = jnp.einsum('nd,edf->nef', xt, w_gate)
    hu = jnp.einsum('nd,edf->nef', xt, w_up)
    act = jax.nn.silu(hg) * hu * gates[:, :, None]
    return jnp.einsum('nef,efd->nd', act, w_down)

def layer_forward(x, k_hist, v_hist, u_hist, norm1_g, w_in, conv_w, sinks, attn_out_g, conv_out_g,
                  w_out, norm2_g, w_group, b_group, w_fine, b_fine, w_gate, w_up, w_down):
    n, t, _ = x.shape
    xn = rmsnorm(x, norm1_g)
    proj = xn @ w_in
    q = proj[..., OFF_Q:OFF_K].reshape(n, t, N_KV_HEADS, GQA_GROUP, HEAD_DIM)
    k = proj[..., OFF_K:OFF_V].reshape(n, t, N_KV_HEADS, HEAD_DIM)
    v = proj[..., OFF_V:OFF_B].reshape(n, t, N_KV_HEADS, HEAD_DIM)
    gate_b = proj[..., OFF_B:OFF_C]
    gate_c = proj[..., OFF_C:OFF_H]
    h = proj[..., OFF_H:IN_PROJ_DIM]
    if k_hist is None:
        attn = banded_window_attention(q, k, v, sinks)
        keep = min(WINDOW, t)
        new_k, new_v = k[:, t - keep:], v[:, t - keep:]
        u_hist = jnp.zeros((n, CONV_WIDTH - 1, CONV_DIM), x.dtype)
    else:
        attn, new_k, new_v = cached_window_attention(q, k, v, k_hist, v_hist, sinks)
    attn = attn.reshape(n, t, ATTN_DIM)
    z, new_u = causal_short_conv(gate_c * h, u_hist, conv_w)
    conv_out = gate_b * z
    mixed = jnp.concatenate([group_rmsnorm(attn, attn_out_g, N_HEADS),
                             group_rmsnorm(conv_out, conv_out_g, CONV_GROUPS)], axis=-1)
    x = x + mixed @ w_out
    xn2 = rmsnorm(x, norm2_g).reshape(n * t, D_MODEL)
    x = x + hierarchical_moe(xn2, w_group, b_group, w_fine, b_fine, w_gate, w_up, w_down).reshape(n, t, D_MODEL)
    return x, new_k, new_v, new_u

def setup_inputs(seed: int = 0) -> dict:
    key = jax.random.key(seed)
    ks = jax.random.split(key, 24)

    def nrm(k, shape, scale):
        return jax.random.normal(k, shape, jnp.float32) * scale

    win = min(WINDOW, PAST_LEN)
    return {
        "x_prompt": nrm(ks[0], (BATCH, SEQ, D_MODEL), 1.0),
        "x_sample": nrm(ks[1], (DEC_BATCH, DEC_SEQ, D_MODEL), 1.0),
        "cache_k_win": nrm(ks[2], (DEPTH, DEC_BATCH, win, N_KV_HEADS, HEAD_DIM), 1.0),
        "cache_v_win": nrm(ks[3], (DEPTH, DEC_BATCH, win, N_KV_HEADS, HEAD_DIM), 1.0),
        "state_conv": nrm(ks[4], (DEPTH, DEC_BATCH, CONV_WIDTH - 1, CONV_DIM), 1.0),
        "norm1_g": 1.0 + nrm(ks[5], (DEPTH, D_MODEL), 0.02),
        "w_in": nrm(ks[6], (DEPTH, D_MODEL, IN_PROJ_DIM), D_MODEL ** -0.5),
        "conv_w": nrm(ks[7], (DEPTH, CONV_WIDTH, CONV_DIM), CONV_WIDTH ** -0.5),
        "sinks": nrm(ks[8], (DEPTH, N_HEADS), 1.0),
        "attn_out_g": 1.0 + nrm(ks[9], (DEPTH, ATTN_DIM), 0.02),
        "conv_out_g": 1.0 + nrm(ks[10], (DEPTH, CONV_DIM), 0.02),
        "w_out": nrm(ks[11], (DEPTH, MIX_DIM, D_MODEL), MIX_DIM ** -0.5),
        "norm2_g": 1.0 + nrm(ks[12], (DEPTH, D_MODEL), 0.02),
        "w_group": nrm(ks[13], (DEPTH, D_MODEL, N_EXPERT_GROUPS), D_MODEL ** -0.5),
        "b_group": nrm(ks[14], (DEPTH, N_EXPERT_GROUPS), 0.01),
        "w_fine": nrm(ks[15], (DEPTH, D_MODEL, N_EXPERTS), D_MODEL ** -0.5),
        "b_fine": nrm(ks[16], (DEPTH, N_EXPERTS), 0.01),
        "w_gate": nrm(ks[17], (DEPTH, N_EXPERTS, D_MODEL, D_EXPERT), D_MODEL ** -0.5),
        "w_up": nrm(ks[18], (DEPTH, N_EXPERTS, D_MODEL, D_EXPERT), D_MODEL ** -0.5),
        "w_down": nrm(ks[19], (DEPTH, N_EXPERTS, D_EXPERT, D_MODEL), D_EXPERT ** -0.5),
        "final_g": 1.0 + nrm(ks[20], (D_MODEL,), 0.02),
    }

def reference(x_prompt, x_sample, cache_k_win, cache_v_win, state_conv, norm1_g, w_in, conv_w, sinks,
              attn_out_g, conv_out_g, w_out, norm2_g, w_group, b_group, w_fine, b_fine, w_gate, w_up,
              w_down, final_g):
    yp, ys = x_prompt, x_sample
    kp_l, vp_l, up_l, ks_l, vs_l, us_l = [], [], [], [], [], []
    for l in range(DEPTH):
        lp = (norm1_g[l], w_in[l], conv_w[l], sinks[l], attn_out_g[l], conv_out_g[l], w_out[l],
              norm2_g[l], w_group[l], b_group[l], w_fine[l], b_fine[l], w_gate[l], w_up[l], w_down[l])
        yp, kp, vp, up = layer_forward(yp, None, None, None, *lp)
        ys, ksm, vsm, usm = layer_forward(ys, cache_k_win[l], cache_v_win[l], state_conv[l], *lp)
        kp_l.append(kp); vp_l.append(vp); up_l.append(up)
        ks_l.append(ksm); vs_l.append(vsm); us_l.append(usm)
    y_prompt = rmsnorm(yp, final_g)
    y_sample = rmsnorm(ys, final_g)
    return (y_prompt, y_sample, jnp.stack(kp_l), jnp.stack(vp_l), jnp.stack(up_l),
            jnp.stack(ks_l), jnp.stack(vs_l), jnp.stack(us_l))


_drawn_inputs = setup_inputs


def setup_inputs(seed=0):
    import zlib

    import numpy as np

    out = dict(_drawn_inputs(seed))
    spreads = {}
    factors = {}
    for name, (base, spread) in spreads.items():
        noise = np.random.default_rng([zlib.crc32(name.encode()), seed]).standard_normal(out[name].shape)
        drawn = base * np.exp(spread * noise) if base else spread * noise
        out[name] = __import__('jax').numpy.asarray(drawn.astype(out[name].dtype))
    for name, factor in factors.items():
        out[name] = (out[name] * factor).astype(out[name].dtype)
    return out
```

```python
from contextlib import ExitStack

import concourse.bass as bass
from concourse import mybir
from concourse.bass import ds

P = 128
D = 1024
KC = D // P
SEQ = 1024
NS = 8
NT = SEQ + NS
TILES = SEQ // P
ALLT = TILES + 1
HD = 64
NH = 8
NKV = 2
ATT = NH * HD
AC = ATT // P
CONV = D - ATT
CC = CONV // P
OFF_K = ATT
OFF_V = OFF_K + NKV * HD
OFF_B = OFF_V + NKV * HD
OFF_C = OFF_B + CONV
OFF_H = OFF_C + CONV
QKV = 6
NG = 4
EG = 4
NE = NG * EG
FE = 256
FC = FE // P
NR = NG + NE
SLOT_TILES = (2 * NT + NE * (P - 1)) // P
NB = 3
RUN = NT // NB
WB = 3
EPS = 1e-5
MASKED = -1e30
LOWEST = -3e38
NOWHERE = 999.0

F32 = mybir.dt.float32
I32 = mybir.dt.int32
ALU = mybir.AluOpType
ACT = mybir.ActivationFunctionType
AX = mybir.AxisListType.X


class Steps:

    def __init__(self, eng, sem):
        self.eng, self.sem, self.base, self.n = eng, sem, 0, 0

    def then(self, ins):
        ins.then_inc(self.sem, 1)
        self.n += 1
        self.eng.wait_ge(self.sem, self.base + self.n)

    def loop(self, lo, hi, per, body):
        start = self.n
        with self.eng.Fori(lo, hi) as i:
            self.base = (i - lo) * per
            body(i)
        assert self.n == start + per, f"{self.n - start} steps, not {per}"
        self.base, self.n = 0, start + per * (hi - lo)


def hybrid_layer_step(nc, x_prompt, x_sample, cache_k_win, cache_v_win, state_conv, norm1_g, w_in,
                      conv_w, sinks, attn_out_g, conv_out_g, w_out, norm2_g, w_group, b_group,
                      w_fine, b_fine, w_gate, w_up, w_down, final_g,
                      y_prompt, y_sample, new_k_prompt, new_v_prompt, new_conv_prompt,
                      new_k_sample, new_v_sample, new_conv_sample):
    xp, x_smp = x_prompt[0], x_sample[:, 0, :]
    w_in_v = w_in[0].rearrange("(c p) f -> p c f", p=P)
    w_out_v = w_out[0].rearrange("(c p) f -> p c f", p=P)
    w_gate_rows = w_gate[0].rearrange("e (p c) f -> (e p) (c f)", p=P)
    w_up_rows = w_up[0].rearrange("e (p c) f -> (e p) (c f)", p=P)
    w_down_rows = w_down[0].rearrange("e (p c) n -> (e p) (c n)", p=P)
    xn2_d = nc.dram_tensor("xn2_rows", [NT, D], F32, kind="Internal").ap()
    y_d = nc.dram_tensor("y_slots", [SLOT_TILES * P, D], F32, kind="Internal").ap()

    ctx = ExitStack()
    with ctx:
        def sem(name):
            return ctx.enter_context(nc.semaphore(name))

        def sems(name, n):
            return [sem(f"{name}{i}") for i in range(n)]

        def alloc(stack, name, shape, dt=F32):
            return stack.enter_context(nc.sbuf_tensor("b_" + name, shape, dt))

        def sb(name, shape, dt=F32):
            return alloc(ctx, name, shape, dt)

        bank = ctx.enter_context(nc.psum_tensor("banks", [P, 8, 512], F32))

        ident = sb("ident", [P, P])
        ones = sb("ones", [P, P])
        earlier = sb("earlier", [P, P])
        group_mean = sb("group_mean", [P, 2])
        exponent = sb("exponent", [P, 2 * ALLT])
        epsilon = sb("epsilon", [P, 1])
        rev4 = sb("rev4", [P, ALLT, EG])
        valid = sb("valid", [P, ALLT])
        nowhere = sb("nowhere", [P, 2, ALLT])
        iota_row = sb("iota_row", [P, P])
        iota_p = sb("iota_p", [P, 1])
        steps128 = sb("steps128", [P, ALLT])
        token_no = sb("token_no", [P, ALLT])
        half_mask = sb("half_mask", [NH, P])
        g1 = sb("g1", [P, KC])
        ga = sb("ga", [P, AC])
        ga_s = sb("ga_s", [NH, HD])
        cwg = sb("cwg", [P, CC, 4])
        sink_in = sb("sink_in", [P, NH])
        nsink = sb("nsink", [P, NH])
        sink_in_s = sb("sink_in_s", [NH, 1])
        nsink_s = sb("nsink_s", [NH, 1])
        w_r = sb("w_r", [P, KC, NR])
        b_r = sb("b_r", [P, NR])

        mixedT = sb("mixedT", [P, KC, NT])
        ms = [sb(f"ms{i}", [P, ALLT]) for i in range(3)]
        rstd = [sb(f"rstd{i}", [P, ALLT]) for i in range(3)]
        junk = sb("junk", [P, D])
        kv_rows = sb("kv_rows", [P, 2, P])
        kvs_rows = sb("kvs_rows", [NS, 2, P])
        u_rows = sb("u_rows", [2 + NS, CONV])

        first = ExitStack()
        xnT = alloc(first, "xnT", [P, KC, NT])
        w_chunk = [alloc(first, f"w_chunk{i}", [P, KC, P]) for i in range(WB)]
        x_in = [alloc(first, f"x_in{i}", [P, D]) for i in range(2)]
        x_sc = [alloc(first, f"x_sc{i}", [P, D]) for i in range(2)]
        qkvT = alloc(first, "qkvT", [P, QKV, NT])
        v_tok = alloc(first, "v_tok", [P, ALLT, P])
        hcb = alloc(first, "hcb", [P, 3, NT])
        uT = alloc(first, "uT", [P, 2 + NT])
        zT = alloc(first, "zT", [P, NT])
        sqT = alloc(first, "sqT", [P, ALLT * P])
        u_last = alloc(first, "u_last", [P, CC, 2 + NS])
        histT = alloc(first, "histT", [P, CC, 2 * NS])
        hist = alloc(first, "hist", [2 * NS, CONV])
        cw = alloc(first, "cw", [P, 4])
        cms = alloc(first, "cms", [P, 2 * ALLT])
        crs = alloc(first, "crs", [P, 2 * ALLT])
        crs_row = sqT
        band_mask = alloc(first, "band_mask", [P, TILES, 2 * P])
        qs = alloc(first, "qs", [P, AC, P])
        kb = alloc(first, "kb", [P, 2 * P])
        prob = [alloc(first, f"prob{i}", [P, NH, 2 * P]) for i in range(2)]
        pTs = alloc(first, "pTs", [P, NH, 2, P])
        mx = alloc(first, "mx", [P, NH])
        nm = [alloc(first, f"nm{i}", [P, NH]) for i in range(2)]
        sd = [alloc(first, f"sd{i}", [P, NH]) for i in range(2)]
        es = [alloc(first, f"es{i}", [P, NH]) for i in range(2)]
        den = [alloc(first, f"den{i}", [P, NH]) for i in range(2)]
        rden = alloc(first, "rden", [P, NH])
        at_o = alloc(first, "at_o", [P, ATT])
        at_sq = alloc(first, "at_sq", [P, ATT])
        at_n = alloc(first, "at_n", [P, ATT])
        at_ms = alloc(first, "at_ms", [P, NH])
        at_r = alloc(first, "at_r", [P, NH])
        ck = x_in[0][:, :].rearrange("p (n f) -> p n f", n=NS)
        cv = x_in[1][:, :].rearrange("p (n f) -> p n f", n=NS)
        kTs = x_sc[0][:, :].rearrange("p (n t) -> p n t", n=NS)
        qbd = alloc(first, "qbd", [P, NS, NH])
        s_sc = prob[0][0:NH, :, :].rearrange("p a b -> p (a b)")[:, 0:NS * (P + 1)].rearrange("p (n t) -> p n t", n=NS)
        s_p = prob[1][0:NH, :, :].rearrange("p a b -> p (a b)")[:, 0:NS * (P + 1)].rearrange("p (n t) -> p n t", n=NS)
        s_o2 = pTs[0:NH, :, :, :].rearrange("p a b c -> p (a b c)")[:, 0:NS * P].rearrange("p (n f) -> p n f", n=NS)
        s_o = at_o[0:NH, :].rearrange("p (n d) -> p n d", n=NS)
        s_sq = at_sq[0:NH, :].rearrange("p (n d) -> p n d", n=NS)
        s_n = at_n[0:NH, :].rearrange("p (n d) -> p n d", n=NS)
        s_mx, s_nm, s_es, s_dn, s_ms, s_r = [alloc(first, f"s_small{i}", [NH, NS]) for i in range(6)]
        s_pT = alloc(first, "s_pT", [P, NS, NH])
        s_z = alloc(first, "s_z", [NS, NS, NH])
        first.close()

        second = ExitStack()
        w_o = alloc(second, "w_o", [P, KC, D])
        x2 = alloc(second, "x2", [P, ALLT, D])
        g2 = alloc(second, "g2", [P, D])
        gf = alloc(second, "gf", [P, D])
        mix_st = [alloc(second, f"mix_st{i}", [P, KC, P]) for i in range(2)]
        xn2 = [alloc(second, f"xn2_{i}", [P, D]) for i in range(2)]
        xn2T = alloc(second, "xn2T", [P, KC, P])
        logits = alloc(second, "logits", [P, ALLT, NR])
        w_gu = [alloc(second, f"w_gu{i}", [P, 2, KC, FE]) for i in range(2)]
        w_dn = [alloc(second, f"w_dn{i}", [P, FC, D]) for i in range(2)]
        r9 = [alloc(second, f"r9_{i}", [P, ALLT]) for i in range(8)]
        r4 = [alloc(second, f"r4_{i}", [P, ALLT, EG]) for i in range(5)]
        count = alloc(second, "count", [P, NE])
        tiles_of = alloc(second, "tiles_of", [P, NE])
        scan = [alloc(second, f"scan{i}", [P, NE]) for i in range(2)]
        start128 = alloc(second, "start128", [P, NE])
        slot_f = alloc(second, "slot_f", [P, 2, ALLT])
        slot_i = alloc(second, "slot_i", [P, 2, ALLT], I32)
        row_i = alloc(second, "row_i", [P, 2, ALLT], I32)
        tile_i = alloc(second, "tile_i", [P, 2, ALLT], I32)
        row_f = alloc(second, "row_f", [P, 2, ALLT])
        tile_f = alloc(second, "tile_f", [P, 2, ALLT])
        gate = alloc(second, "gate", [P, 2, ALLT])
        slot_gate = alloc(second, "slot_gate", [P, SLOT_TILES])
        slot_tok = alloc(second, "slot_tok", [P, SLOT_TILES], I32)
        tile_ex = alloc(second, "tile_ex", [P, SLOT_TILES])
        w_row = alloc(second, "w_row", [P, SLOT_TILES], I32)
        tok_i = [alloc(second, f"tok_i{i}", [P, 1], I32) for i in range(2)]
        wrow_i = [alloc(second, f"wrow_i{i}", [P, 1], I32) for i in range(2)]
        pair_a = [alloc(second, f"pair_a{i}", [P, 1], I32) for i in range(2)]
        pair_b = [alloc(second, f"pair_b{i}", [P, 1], I32) for i in range(2)]
        silu = [alloc(second, f"silu{i}", [P, FE]) for i in range(2)]
        hid = [alloc(second, f"hid{i}", [P, FC, P]) for i in range(2)]
        hidT = [alloc(second, f"hidT{i}", [P, FC, P]) for i in range(2)]
        second.close()
        free_at = [0]
        mixed_flat = mixedT[:, :, :].rearrange("p c t -> p (c t)")

        def carve(n):
            free_at[0] += n
            assert free_at[0] <= KC * NT
            return mixed_flat[:, free_at[0] - n:free_at[0]]

        y_sb = [carve(D) for _ in range(2)]
        prod16 = carve(ALLT * NE).rearrange("p (t e) -> p t e", t=ALLT)
        pick = carve(2 * ALLT * NE).rearrange("p (k t e) -> p k t e", k=2, t=ALLT)
        both = carve(ALLT * NE).rearrange("p (t e) -> p t e", t=ALLT)
        before = carve((ALLT + 1) * NE).rearrange("p (t e) -> p t e", e=NE)
        place16 = carve(ALLT * NE).rearrange("p (t e) -> p t e", t=ALLT)
        cmp9 = carve(NE * ALLT).rearrange("p (e t) -> p e t", e=NE)
        row_hot = carve(2 * ALLT * P).rearrange("p (j q) -> p j q", q=P)
        tile_hot = carve(2 * ALLT * SLOT_TILES).rearrange("p (j u) -> p j u", u=SLOT_TILES)
        payload = carve(2 * ALLT * 2 * SLOT_TILES).rearrange("p (j v u) -> p j v u", v=2, u=SLOT_TILES)
        cmp16 = row_hot.rearrange("p j q -> p (j q)")[:, 0:SLOT_TILES * NE].rearrange("p (u e) -> p u e", e=NE)
        xg = [m[:, :, :].rearrange("p c t -> p (c t)") for m in mix_st]
        xgT = [x[:, :].rearrange("p (c t) -> p c t", c=KC) for x in xn2]
        pair_rows = [[xg[i], xn2[i][:, :]] for i in range(2)]

        const_made, const_in, late_const_in, sinks_ready = sem("const_made"), sem("const_in"), sem("late_const_in"), sem("sinks_ready")
        x_arrived = sems("x_arrived", 2)
        ms1_ready, eps1_added, rstd1_ready = sem("ms1_ready"), sem("eps1_added"), sem("rstd1_ready")
        x_scaled, x_turned, xnT_ready = sem("x_scaled"), sem("x_turned"), sem("xnT_ready")
        w_arrived = sems("w_arrived", WB)
        run_done, run_out = sem("run_done"), sem("run_out")
        hist_arrived, hist_turned, hist_ready = sem("hist_arrived"), sem("hist_turned"), sem("hist_ready")
        v_turned, v_ready, kv_turned, kv_rows_ready = sem("v_turned"), sem("v_ready"), sem("kv_turned"), sem("kv_rows_ready")
        staged, scores_done, scores_read = sem("staged"), sem("scores_done"), sem("scores_read")
        nm_ready, sd_ready, exp_ready = sem("nm_ready"), sem("sd_ready"), sem("exp_ready")
        p_turned, pT_ready, pv_done = sem("p_turned"), sem("pT_ready"), sem("pv_done")
        at_ms_ready, at_r_ready, at_n_ready = sem("at_ms_ready"), sem("at_r_ready"), sem("at_n_ready")
        at_turned, atT_ready = sem("at_turned"), sem("atT_ready")
        u_ready, sq_ready, cms_done, cms_ready, crs_ready = sem("u_ready"), sem("sq_ready"), sem("cms_done"), sem("cms_ready"), sem("crs_ready")
        crs_row_ready, crs_turned, conv_ready = sem("crs_row_ready"), sem("crs_turned"), sem("conv_ready")
        u_turned, u_rows_ready = sem("u_turned"), sem("u_rows_ready")
        cache_arrived, ck_turned, kTs_ready, qbd_ready = sem("cache_arrived"), sem("ck_turned"), sem("kTs_ready"), sem("qbd_ready")
        s_scored, s_shifted, s_exp_ready, s_turned, s_pT_ready = sem("s_scored"), sem("s_shifted"), sem("s_exp_ready"), sem("s_turned"), sem("s_pT_ready")
        s_pv_done, s_ms_ready, s_r_ready, s_n_ready, s_n_turned, s_mixed = sem("s_pv_done"), sem("s_ms_ready"), sem("s_r_ready"), sem("s_n_ready"), sem("s_n_turned"), sem("s_mixed")
        w_o_arrived, x_again, mix_staged, out_done, x2_ready = sem("w_o_arrived"), sem("x_again"), sem("mix_staged"), sem("out_done"), sem("x2_ready")
        ms2_ready, eps2_added, rstd2_ready, xn2_ready = sem("ms2_ready"), sem("eps2_added"), sem("rstd2_ready"), sem("xn2_ready")
        xn2_stored = sems("xn2_stored", 2)
        xn2_turned, xn2T_ready, routed, logits_ready = sem("xn2_turned"), sem("xn2T_ready"), sem("routed"), sem("logits_ready")
        r_shifted, r_exp_ready, picks_ready, places_done = sem("r_shifted"), sem("r_exp_ready"), sem("picks_ready"), sem("places_done")
        table_in_ready, table_done, slots_ready = sem("table_in_ready"), sem("table_done"), sem("slots_ready")
        tok_staged, x_gathered, gu_gathered, dn_gathered = sem("tok_staged"), sems("x_gathered", 2), sems("gu_gathered", 2), sems("dn_gathered", 2)
        xg_turned, xgT_ready, h_done, silu_ready, hid_ready = sem("xg_turned"), sem("xgT_ready"), sem("h_done"), sem("silu_ready"), sem("hid_ready")
        hid_turned, hidT_ready, y_done = sem("hid_turned"), sem("hidT_ready"), sem("y_done")
        y_left_ready, y_right_ready, y_stored = sem("y_left_ready"), sem("y_right_ready"), sems("y_stored", 2)
        pair_staged, pair_gathered, x3_ready = sem("pair_staged"), sems("pair_gathered", 2), sem("x3_ready")
        ms3_ready, eps3_added, rstd3_ready, out_ready = sem("ms3_ready"), sem("eps3_added"), sem("rstd3_ready"), sem("out_ready")
        out_stored, rows_stored = sems("out_stored", 2), sem("rows_stored")
        dve_step, act_held, pool_held = sem("dve_step"), sem("act_held"), sem("pool_held")

        ctx.enter_context(nc.allow_non_contiguous_dma(reason="gains and sinks are a few KB"))
        block = ctx.enter_context(nc.Block())

        def rows_of(t):
            return NS if isinstance(t, int) and t == TILES else P

        def cols(t):
            return slice(t * P, t * P + rows_of(t)) if isinstance(t, int) else ds(t * P, P)

        def col(t, n=1):
            return slice(t, t + n) if isinstance(t, int) else ds(t, n)

        @block.sync
        def _(sp):
            def load_x(t, k):
                n = rows_of(t)
                src = x_smp if n == NS else xp[cols(t), :]
                sp.dma_start(x_in[k][0:n, :], src).then_inc(x_arrived[k], 16)

            def load_w(buf, c0):
                sp.dma_start(w_chunk[buf][:, :, :], w_in_v[:, :, ds(c0, P)]).then_inc(w_arrived[buf], 16)

            def load_wq(j):
                for g in range(NKV):
                    sp.dma_start(w_chunk[j % WB][:, :, g * HD:(g + 1) * HD],
                                 w_in_v[:, :, (4 * g + j) * HD:(4 * g + j + 1) * HD]).then_inc(w_arrived[j % WB], 16)

            load_x(0, 0)
            load_x(1, 1)
            sp.dma_start(g1[:, :], norm1_g[0].rearrange("(c p) -> p c", p=P)).then_inc(const_in, 16)
            sp.dma_start(ga[:, :], attn_out_g[0].rearrange("(c p) -> p c", p=P)).then_inc(const_in, 16)
            sp.dma_start(ga_s[:, :], attn_out_g[0].rearrange("(h d) -> h d", h=NH)).then_inc(const_in, 16)
            for j in range(3):
                sp.dma_start(cwg[:, :, j], conv_w[0, j].rearrange("(c p) -> p c", p=P)).then_inc(const_in, 16)
            sp.dma_start(cwg[:, :, 3], conv_out_g[0].rearrange("(c p) -> p c", p=P)).then_inc(const_in, 16)
            for g in range(NKV):
                dst = sink_in[:, :].rearrange("p (h g j) -> p g h j", h=2, g=NKV)[:, g, :, :]
                src = sinks[0:1, 4 * g:4 * g + 4].rearrange("o (h j) -> o h j", h=2).broadcast_to([P, 2, 2])
                sp.dma_start(dst, src).then_inc(const_in, 16)
            sp.dma_start(sink_in_s[:, :], sinks[0].rearrange("(h o) -> h o", o=1)).then_inc(const_in, 16)
            sp.dma_start(hist[:, :], state_conv[0].rearrange("n j f -> (n j) f")).then_inc(hist_arrived, 16)

            for j in range(WB):
                load_wq(j)
            def x_pair(i):
                for k in range(2):
                    sp.wait_ge(x_scaled, 2 * i + (k - 1))
                    load_x(2 * i + k, k)
            with sp.Fori(1, TILES // 2) as i:
                x_pair(i)
            sp.wait_ge(x_scaled, TILES - 1)
            load_x(TILES, 0)
            sp.wait_ge(x_scaled, ALLT)
            sp.dma_start(ck, cache_k_win[0].rearrange("n t g d -> t n (g d)")).then_inc(cache_arrived, 16)
            sp.dma_start(cv, cache_v_win[0].rearrange("n t g d -> t n (g d)")).then_inc(cache_arrived, 16)
            sp.wait_ge(run_done, NB)
            load_wq(3)
            sp.wait_ge(run_done, 2 * NB)
            load_w(1, OFF_K)
            sp.wait_ge(run_done, 3 * NB)
            load_w(2, OFF_V)
            with sp.Fori(0, CC) as i:
                for x, off in enumerate((OFF_H, OFF_C, OFF_B)):
                    sp.wait_ge(run_done, i * (3 * NB) + NB * (QKV + x + 1 - WB))
                    load_w(x, i * P + off)
            sp.wait_ge(run_done, NB * (QKV + 3 * CC))
            sp.dma_start(w_o[:, :, :], w_out_v).then_inc(w_o_arrived, 16)
            sp.wait_ge(kv_rows_ready, 3)
            sp.dma_start(new_k_prompt[0, 0].rearrange("t g d -> t (g d)"), kv_rows[:, 0, :]).then_inc(rows_stored, 16)
            sp.dma_start(new_v_prompt[0, 0].rearrange("t g d -> t (g d)"), kv_rows[:, 1, :]).then_inc(rows_stored, 16)
            for j, (new, old) in enumerate(((new_k_sample, cache_k_win), (new_v_sample, cache_v_win))):
                new_v = new[0].rearrange("n t g d -> n t (g d)")
                sp.dma_start(new_v[:, P - 1, :], kvs_rows[:, j, :]).then_inc(rows_stored, 16)
                sp.dma_start(new_v[:, 0:P - 1, :], old[0].rearrange("n t g d -> n t (g d)")[:, 1:P, :]).then_inc(rows_stored, 16)
            sp.dma_start(new_conv_sample[0, :, 0, :], state_conv[0, :, 1, :]).then_inc(rows_stored, 16)
            sp.wait_ge(u_rows_ready, 1)
            sp.dma_start(new_conv_prompt[0, 0], u_rows[0:2, :]).then_inc(rows_stored, 16)
            sp.dma_start(new_conv_sample[0, :, 1, :], u_rows[2:2 + NS, :]).then_inc(rows_stored, 16)
            sp.wait_ge(s_mixed, 2)
            sp.dma_start(x2[:, 0:TILES, :], xp.rearrange("(t p) d -> p t d", p=P)).then_inc(x_again, 16)
            sp.dma_start(x2[0:NS, TILES, :], x_smp).then_inc(x_again, 16)
            sp.dma_start(g2[:, :], norm2_g[0:1, :].broadcast_to([P, D])).then_inc(late_const_in, 16)
            sp.dma_start(gf[:, :], final_g.rearrange("(o d) -> o d", o=1).broadcast_to([P, D])).then_inc(late_const_in, 16)
            sp.dma_start(w_r[:, :, 0:NG], w_group[0].rearrange("(p c) n -> p c n", p=P)).then_inc(late_const_in, 16)
            sp.dma_start(w_r[:, :, NG:NR], w_fine[0].rearrange("(p c) n -> p c n", p=P)).then_inc(late_const_in, 16)
            sp.dma_start(b_r[:, 0:NG], b_group[0:1, :].broadcast_to([P, NG])).then_inc(late_const_in, 16)
            sp.dma_start(b_r[:, NG:NR], b_fine[0:1, :].broadcast_to([P, NE])).then_inc(late_const_in, 16)
            def store_xn2(t, k):
                sp.wait_ge(xn2_ready, t + 1)
                sp.dma_start(xn2_d[cols(t), :], xn2[k][0:rows_of(t), :]).then_inc(xn2_stored[k], 16)
            with sp.Fori(0, TILES // 2) as i:
                for k in range(2):
                    store_xn2(i * 2 + k, k)
            store_xn2(TILES, 0)
            with sp.Fori(0, SLOT_TILES // 2) as i:
                for k in range(2):
                    u = i * 2 + k
                    sp.wait_ge(y_left_ready, u + 1)
                    sp.wait_ge(y_right_ready, u + 1)
                    sp.dma_start(y_d[ds(u * P, P), :], y_sb[k]).then_inc(y_stored[k], 16)
            def store_out(t, k):
                n = rows_of(t)
                dst = y_sample[:, 0, :] if n == NS else y_prompt[0][cols(t), :]
                sp.wait_ge(out_ready, t + 1)
                sp.dma_start(dst, y_sb[k][0:n, :]).then_inc(out_stored[k], 16)
            with sp.Fori(0, TILES // 2) as i:
                for k in range(2):
                    store_out(i * 2 + k, k)
            store_out(TILES, 0)
            sp.wait_ge(out_stored[0], 16 * (TILES // 2 + 1))
            sp.wait_ge(out_stored[1], 16 * (TILES // 2))
            sp.wait_ge(rows_stored, 16 * 9)

        @block.gpsimd
        def _(pool):
            made = Steps(pool, const_made)

            def select(out, in_, pattern, base, cm, fill, op=ALU.is_ge):
                made.then(pool.affine_select(out=out, in_=in_, compare_op=op, fill=fill, base=base,
                                             pattern=pattern, channel_multiplier=cm))

            def iota(out, pattern, base, cm):
                made.then(pool.iota(out, pattern=pattern, base=base, channel_multiplier=cm,
                                    allow_small_or_imprecise_dtypes=True))

            made.then(pool.memset(ident[:, :], 0.0))
            select(ident[:, :], ident[:, :], [[-1, P]], 0, 1, 1.0, ALU.not_equal)
            made.then(pool.memset(epsilon[:, :], EPS))
            made.then(pool.memset(exponent[:, :], -0.5))

            def rsqrt(n, t, ready, added, out_ready_, rows):
                pool.wait_ge(ready, t + 1)
                pool.sem_inc(pool_held, 1)
                pool.tensor_tensor(ms[n][0:rows, col(t)], ms[n][0:rows, col(t)], epsilon[0:rows, :], ALU.add).then_inc(added, 1)
                pool.wait_ge(added, t + 1)
                pool.sem_inc(pool_held, 1)
                pool.tensor_tensor(rstd[n][0:rows, col(t)], ms[n][0:rows, col(t)], exponent[0:rows, 0:1], ALU.pow).then_inc(out_ready_, 1)

            with pool.Fori(0, TILES) as t:
                rsqrt(0, t, ms1_ready, eps1_added, rstd1_ready, P)
            rsqrt(0, TILES, ms1_ready, eps1_added, rstd1_ready, NS)

            made.then(pool.memset(ones[:, :], 1.0))
            select(earlier[:, :], ones[:, :], [[1, P]], -1, -1, 0.0)
            made.then(pool.memset(group_mean[:, :], 1.0 / HD))
            select(group_mean[:, :], group_mean[:, :], [[-HD, 2]], 0, 1, 0.0)
            select(group_mean[:, :], group_mean[:, :], [[HD, 2]], HD - 1, -1, 0.0)
            made.then(pool.memset(uT[:, 0:2], 0.0))
            made.then(pool.memset(v_tok[:, 0, :], 0.0))
            made.then(pool.memset(qbd[:, :, :], 0.0))
            made.then(pool.memset(band_mask[:, :, :], 0.0))
            select(band_mask[:, :, :], band_mask[:, :, :], [[0, TILES], [1, 2 * P]], 0, -1, MASKED)
            select(band_mask[:, :, :], band_mask[:, :, :], [[0, TILES], [-1, 2 * P]], P, 1, MASKED)
            made.then(pool.memset(band_mask[:, 0, 0:P], MASKED))
            made.then(pool.memset(half_mask[:, :], 1.0))
            select(half_mask[:, :].rearrange("h (g d) -> h g d", g=NKV), half_mask[:, :].rearrange("h (g d) -> h g d", g=NKV),
                   [[-4, NKV], [0, HD]], 0, 1, 0.0)
            select(half_mask[:, :].rearrange("h (g d) -> h g d", g=NKV), half_mask[:, :].rearrange("h (g d) -> h g d", g=NKV),
                   [[4, NKV], [0, HD]], 3, -1, 0.0)
            iota(rev4[:, :, :], [[0, ALLT], [-1, EG]], EG, 0)
            made.then(pool.memset(valid[:, :], 1.0))
            select(valid[:, :], valid[:, :], [[-P, ALLT]], NT - 1, -1, 0.0)
            made.then(pool.memset(nowhere[:, :, :], 0.0))
            select(nowhere[:, :, :], nowhere[:, :, :], [[0, 2], [-P, ALLT]], NT - 1, -1, NOWHERE)
            iota(iota_row[:, :], [[1, P]], 0, 0)
            iota(iota_p[:, :], [[0, 1]], 0, 1)
            iota(steps128[:, :], [[P, ALLT]], 0, 0)
            iota(token_no[:, :], [[P, ALLT]], 0, 1)
            assert made.n == CONST_ALL, made.n

            def at_power(t):
                pool.wait_ge(at_ms_ready, t + 1)
                pool.tensor_tensor(at_r[:, :], at_ms[:, :], exponent[:, 0:NH], ALU.pow).then_inc(at_r_ready, 1)

            def conv_power(i):
                pool.wait_ge(cms_ready, i + 1)
                pool.tensor_tensor(crs[:, :], cms[:, :], exponent[:, :], ALU.pow).then_inc(crs_ready, 1)

            at_power(0)
            at_power(1)
            with pool.Fori(1, CC) as i:
                at_power(i * 2)
                conv_power(i - 1)
                at_power(i * 2 + 1)
            conv_power(CC - 1)
            pool.wait_ge(s_ms_ready, 1)
            pool.tensor_tensor(s_r[:, :], s_ms[:, :], exponent[0:NH, 0:NS], ALU.pow).then_inc(s_r_ready, 1)
            with pool.Fori(0, TILES) as t:
                rsqrt(1, t, ms2_ready, eps2_added, rstd2_ready, P)
            rsqrt(1, TILES, ms2_ready, eps2_added, rstd2_ready, NS)

            def at_row(idx):
                return bass.IndirectOffsetOnAxis(ap=idx, axis=0)

            def gather_x_gu(u, k):
                pool.tensor_copy(tok_i[k][:, :], slot_tok[:, col(u)]).then_inc(tok_staged, 1)
                pool.tensor_copy(wrow_i[k][:, :], w_row[:, col(u)]).then_inc(tok_staged, 1)
                pool.wait_ge(tok_staged, u * 2 + 2)
                pool.sem_inc(pool_held, 1)
                pool.indirect_dma_start(xg[k], None, xn2_d, at_row(tok_i[k][:, :])).then_inc(x_gathered[k], 16)
                pool.indirect_dma_start(w_gu[k][:, 0, :, :].rearrange("p c f -> p (c f)"), None, w_gate_rows,
                                        at_row(wrow_i[k][:, :])).then_inc(gu_gathered[k], 16)
                pool.indirect_dma_start(w_gu[k][:, 1, :, :].rearrange("p c f -> p (c f)"), None, w_up_rows,
                                        at_row(wrow_i[k][:, :])).then_inc(gu_gathered[k], 16)

            def gather_dn(u, k):
                pool.indirect_dma_start(w_dn[k][:, :, :].rearrange("p c f -> p (c f)"), None, w_down_rows,
                                        at_row(wrow_i[k][:, :])).then_inc(dn_gathered[k], 16)

            pool.wait_ge(slots_ready, 1)
            pool.wait_ge(xn2_stored[0], 16 * (TILES // 2 + 1))
            pool.wait_ge(xn2_stored[1], 16 * (TILES // 2))
            for k in range(2):
                gather_x_gu(k, k)
                gather_dn(k, k)
            with pool.Fori(1, SLOT_TILES // 2) as i:
                for k in range(2):
                    u = i * 2 + k
                    pool.wait_ge(dn_gathered[k], i * 16)
                    pool.wait_ge(xg_turned, u - 1)
                    pool.wait_ge(h_done, u - 1)
                    pool.sem_inc(pool_held, 1)
                    gather_x_gu(u, k)
                    pool.wait_ge(y_done, u * 2 - 2)
                    pool.sem_inc(pool_held, 1)
                    gather_dn(u, k)

            def gather_pair(t, k, rows):
                pool.tensor_copy(pair_a[k][:, :], slot_i[:, 0, col(t)]).then_inc(pair_staged, 1)
                pool.tensor_copy(pair_b[k][:, :], slot_i[:, 1, col(t)]).then_inc(pair_staged, 1)
                pool.wait_ge(pair_staged, t * 2 + 2)
                pool.sem_inc(pool_held, 1)
                for dst, idx in zip(pair_rows[k], (pair_a[k], pair_b[k])):
                    pool.indirect_dma_start(dst[0:rows, :], None, y_d, at_row(idx[0:rows, :])).then_inc(pair_gathered[k], 16)

            pool.wait_ge(y_stored[0], 16 * (SLOT_TILES // 2))
            pool.wait_ge(y_stored[1], 16 * (SLOT_TILES // 2))
            gather_pair(0, 0, P)
            gather_pair(1, 1, P)
            for t, _ in enumerate(range(2)):
                rsqrt(2, t, ms3_ready, eps3_added, rstd3_ready, P)
            with pool.Fori(1, TILES // 2) as i:
                for k in range(2):
                    t = i * 2 + k
                    pool.wait_ge(x3_ready, t - 1)
                    pool.sem_inc(pool_held, 1)
                    gather_pair(t, k, P)
                    rsqrt(2, t, ms3_ready, eps3_added, rstd3_ready, P)
            pool.wait_ge(x3_ready, TILES - 1)
            gather_pair(TILES, 0, NS)
            rsqrt(2, TILES, ms3_ready, eps3_added, rstd3_ready, NS)

        @block.scalar
        def _(act):
            def squares(n, t, src, ready, rows):
                if not isinstance(t, int) or t >= 1:
                    act.wait_ge(ready, t)
                    act.sem_inc(act_held, 1)
                act.activation(junk[0:rows, :], src, ACT.Square, scale=D ** -0.5,
                               accum_out=ms[n][0:rows, col(t)]).then_inc(ready, 1)

            for k in range(2):
                act.wait_ge(x_arrived[k], 16)
                squares(0, k, x_in[k][:, :], ms1_ready, P)
            with act.Fori(1, TILES // 2) as i:
                for k in range(2):
                    act.wait_ge(x_arrived[k], i * 16 + 16)
                    squares(0, i * 2 + k, x_in[k][:, :], ms1_ready, P)
            act.wait_ge(x_arrived[0], 16 * (TILES // 2 + 1))
            squares(0, TILES, x_in[0][0:NS, :], ms1_ready, NS)

            def projection_out(m, dst):
                for n in range(NB):
                    act.wait_ge(run_done, m * NB + (n + 1))
                    act.copy(dst[:, n * RUN:(n + 1) * RUN], bank[:, 5 + n, 0:RUN]).then_inc(run_out, 1)

            for m in range(QKV):
                projection_out(m, qkvT[:, m, :])

            def exps(t, k):
                act.wait_ge(nm_ready, t + 1)
                for h in range(NH):
                    act.activation(prob[k][:, h, :], prob[k][:, h, :], ACT.Exp, bias=nm[k][:, h:h + 1],
                                   accum_out=den[k][:, h:h + 1])
                act.wait_ge(sd_ready, t + 1)
                act.activation(es[k][:, :], sd[k][:, :], ACT.Exp).then_inc(exp_ready, 1)

            def probs_out(t, k):
                if not isinstance(t, int) or t >= 1:
                    act.wait_ge(pv_done, t)
                for q in range(4):
                    act.wait_ge(p_turned, t * 4 + (q + 1))
                    act.copy(pTs[:, 2 * q:2 * q + 2, :, :].rearrange("p a b c -> p (a b c)"), bank[:, 2 + q % 2, :]).then_inc(pT_ready, 1)

            exps(0, 0)

            def pair(i, last=False):
                t0 = i * 2
                probs_out(t0, 0)
                exps(t0 + 1, 1)
                if not isinstance(i, int) or i >= 1:
                    act.wait_ge(u_ready, i)
                projection_out(i * 3 + QKV, hcb[:, 0, :])
                projection_out(i * 3 + (QKV + 1), hcb[:, 1, :])
                probs_out(t0 + 1, 1)
                if not last:
                    exps(t0 + 2, 0)
                if not isinstance(i, int) or i >= 1:
                    act.wait_ge(sq_ready, i)
                projection_out(i * 3 + (QKV + 2), hcb[:, 2, :])

            pair(0)
            with act.Fori(1, CC - 1) as i:
                pair(i)
            pair(CC - 1, True)

            act.wait_ge(ck_turned, 1)
            act.copy(kTs, bank[:, 0:2, :].rearrange("p b (n t) -> p (b n) t", t=P)).then_inc(kTs_ready, 1)
            act.wait_ge(s_shifted, 1)
            act.activation(s_p, s_sc, ACT.Exp).then_inc(s_exp_ready, 1)
            act.activation(s_es[:, :], s_es[:, :], ACT.Exp).then_inc(s_exp_ready, 1)

            def stage(t, k):
                n = rows_of(t)
                if not isinstance(t, int) or t >= 2:
                    act.wait_ge(out_done, t - 1)
                act.sem_inc(act_held, 1)
                act.copy(mix_st[k][:, :, 0:n], mixedT[:, :, cols(t)]).then_inc(mix_staged, 1)

            def norm2(t, k):
                n = rows_of(t)
                act.wait_ge(x2_ready, t + 1)
                squares(1, t, x2[0:n, t, :] if isinstance(t, int) else x2[:, ds(t, 1), :].rearrange("p o d -> p (o d)"), ms2_ready, n)
                act.wait_ge(xn2_turned, t + 1)
                act.copy(xn2T[:, :, 0:n], bank[:, 4:6, :].rearrange("p b (c t) -> p (b c) t", t=P)[:, :, 0:n]).then_inc(xn2T_ready, 1)

            act.wait_ge(s_mixed, 2)
            stage(0, 0)
            for t in range(2):
                stage(t + 1, (t + 1) % 2)
                norm2(t, t % 2)
            with act.Fori(1, TILES // 2 - 1) as i:
                for k in range(2):
                    stage(i * 2 + (k + 1), (k + 1) % 2)
                    norm2(i * 2 + k, k)
            for t in range(TILES - 2, ALLT):
                if t < TILES:
                    stage(t + 1, (t + 1) % 2)
                norm2(t, t % 2)

            act.wait_ge(r_shifted, 2)
            act.activation(r4[4][:, :, :], r4[4][:, :, :], ACT.Exp).then_inc(r_exp_ready, 1)
            act.activation(r9[5][:, :], r9[5][:, :], ACT.Exp).then_inc(r_exp_ready, 1)

            def x_out(u, k):
                act.wait_ge(xg_turned, u + 1)
                act.copy(xgT[k], bank[:, 0:2, :].rearrange("p b (c t) -> p (b c) t", t=P)).then_inc(xgT_ready, 1)

            def silus(u, k):
                act.wait_ge(h_done, u + 1)
                act.activation(silu[k][:, :], bank[:, 2 + k, 0:FE], ACT.Silu).then_inc(silu_ready, 1)

            def hid_out(u, k):
                act.wait_ge(hid_turned, u + 1)
                act.copy(hidT[k][:, :, :], bank[:, 4, 0:FE].rearrange("p (c t) -> p c t", c=FC)).then_inc(hidT_ready, 1)

            def y_out(u, k):
                if not isinstance(u, int) or u >= 2:
                    act.wait_ge(y_stored[k], u // 2 * 16 if isinstance(u, int) else (u - k) * 8)
                act.wait_ge(y_done, u * 2 + 1)
                act.copy(y_sb[k][:, 0:512], bank[:, 5, :]).then_inc(y_left_ready, 1)

            def tile(u, k):
                hid_out(u, k)
                if not isinstance(u, int) or u + 1 < SLOT_TILES:
                    silus(u + 1, 1 - k)
                if not isinstance(u, int) or u + 2 < SLOT_TILES:
                    x_out(u + 2, k)
                y_out(u, k)

            x_out(0, 0)
            silus(0, 0)
            x_out(1, 1)
            tile(0, 0)
            tile(1, 1)
            with act.Fori(1, SLOT_TILES // 2 - 1) as i:
                for k in range(2):
                    tile(i * 2 + k, k)
            tile(SLOT_TILES - 2, 0)
            tile(SLOT_TILES - 1, 1)

            def norm3(t):
                n = rows_of(t)
                act.wait_ge(x3_ready, t + 1)
                squares(2, t, x2[0:n, t, :] if isinstance(t, int) else x2[:, ds(t, 1), :].rearrange("p o d -> p (o d)"), ms3_ready, n)

            norm3(0)
            with act.Fori(1, TILES) as t:
                norm3(t)
            norm3(TILES)

        @block.tensor
        def _(pe):
            def late(t, least=1):
                return not isinstance(t, int) or t >= least

            def turn_x(t, k):
                n = rows_of(t)
                pe.wait_ge(x_scaled, t + 1)
                if late(t, 2):
                    pe.wait_ge(xnT_ready, t - 1)
                for c in range(KC):
                    mm = pe.transpose(bank[:, 2 * k + c // 4, (c % 4) * P:(c % 4) * P + n], x_sc[k][0:n, c * P:(c + 1) * P], ident[0:n, 0:n])
                mm.then_inc(x_turned, 1)

            pe.wait_ge(const_made, 2)
            for t in range(2):
                turn_x(t, t)
            with pe.Fori(1, TILES // 2) as i:
                for k in range(2):
                    turn_x(i * 2 + k, k)
            turn_x(TILES, 0)

            pe.wait_ge(hist_arrived, 16)
            for c in range(CC):
                mm = pe.transpose(bank[:, 4, c * 2 * NS:(c + 1) * 2 * NS], hist[:, c * P:(c + 1) * P], ident[0:2 * NS, 0:2 * NS])
            mm.then_inc(hist_turned, 1)

            def project(m, buf, arrived):
                pe.wait_ge(w_arrived[buf], arrived)
                for n in range(NB):
                    if late(m):
                        pe.wait_ge(run_out, m * NB + (n + 1 - NB))
                    for c in range(KC):
                        mm = pe.matmul(bank[:, 5 + n, 0:RUN], w_chunk[buf][:, c, :], xnT[:, c, n * RUN:(n + 1) * RUN],
                                       start=c == 0, stop=c == KC - 1)
                    mm.then_inc(run_done, 1)

            pe.wait_ge(xnT_ready, ALLT)
            for m in range(QKV):
                project(m, m % WB, (32, 32, 32, 64, 48, 48)[m])

            pe.wait_ge(run_out, NB * QKV)
            for b in range(TILES):
                mm = pe.transpose(bank[:, b // 4, (b % 4) * P:(b % 4 + 1) * P], qkvT[:, 5, b * P:(b + 1) * P], ident[:, :])
            mm.then_inc(v_turned, 1)
            pe.wait_ge(hist_ready, 1)
            pe.transpose(bank[:, 4, 0:P], qkvT[:, 4, SEQ - P:SEQ], ident[:, :])
            for j in range(2):
                mm = pe.transpose(bank[0:NS, 4, (1 + j) * P:(2 + j) * P], qkvT[:, 4 + j, SEQ:NT], ident[:, :])
            mm.then_inc(kv_turned, 1)

            def scores(t):
                for half in range(2):
                    pe.wait_ge(staged, t * 2 + 2)
                    if late(t) or half:
                        pe.wait_ge(scores_read, t * 2 + half)
                    for j in range(2):
                        for g in range(NKV):
                            mm = pe.matmul(bank[:, g, j * 2 * P:(j + 1) * 2 * P], qs[g * HD:(g + 1) * HD, 2 * half + j, :],
                                           kb[g * HD:(g + 1) * HD, :], start=True, stop=True)
                    mm.then_inc(scores_done, 1)

            def weigh(t, k):
                pe.wait_ge(exp_ready, t + 1)
                for q in range(4):
                    if late(t) or q >= 2:
                        pe.wait_ge(pT_ready, t * 4 + (q - 1))
                    for x in range(2):
                        for c in range(2):
                            mm = pe.transpose(bank[:, 2 + q % 2, (2 * x + c) * P:(2 * x + c + 1) * P],
                                              prob[k][:, 2 * q + x, c * P:(c + 1) * P], ident[:, :])
                    mm.then_inc(p_turned, 1)
                if late(t):
                    pe.wait_ge(atT_ready, t)
                pe.wait_ge(pT_ready, t * 4 + 4)
                for h in range(NH):
                    g = h // 2 % 2
                    for c in range(2):
                        v = v_tok[:, t + c, g * HD:(g + 1) * HD] if isinstance(t, int) else \
                            v_tok[:, :, :].rearrange("p b f -> p (b f)")[:, ds(t * P + (c * P + g * HD), HD)]
                        mm = pe.matmul(bank[:, 4, h * HD:(h + 1) * HD], pTs[:, h, c, :], v, start=c == 0, stop=c == 1)
                mm.then_inc(pv_done, 1)

            def turn_attention(t):
                pe.wait_ge(at_n_ready, t + 1)
                for c in range(AC):
                    first_h = (c % 2) * 4 + (c // 2) * 2
                    mm = pe.transpose(bank[:, 4, c * P:(c + 1) * P], at_n[:, first_h * HD:first_h * HD + P], ident[:, :])
                mm.then_inc(at_turned, 1)

            last_tokens = NT - P

            def conv_means(i):
                pe.wait_ge(sq_ready, i + 1)
                for t in range(ALLT):
                    at = t * P if t < TILES else last_tokens
                    mm = pe.matmul(bank[:, 2, 2 * t:2 * t + 2], sqT[:, at:at + P], group_mean[:, :], start=True, stop=True)
                mm.then_inc(cms_done, 1)

            def conv_scales(i, t1):
                pe.wait_ge(crs_row_ready, i + 1)
                pe.wait_ge(scores_read, t1 * 2 + 2)
                for t in range(ALLT):
                    out = bank[:, t // 4, (t % 4) * P:(t % 4 + 1) * P] if t < TILES else bank[:, 2, P:2 * P]
                    mm = pe.transpose(out, crs_row[:, t * P:(t + 1) * P], ident[:, :])
                mm.then_inc(crs_turned, 1)

            def pair(i, last=False):
                t0 = i * 2
                weigh(t0, 0)
                scores(t0 + 1)
                if late(i):
                    conv_means(i - 1)
                project(i * 3 + QKV, 0, i * 16 + 80)
                if late(i):
                    conv_scales(i - 1, t0 + 1)
                project(i * 3 + (QKV + 1), 1, i * 16 + 64)
                turn_attention(t0)
                if late(i):
                    pe.wait_ge(conv_ready, i * 2)
                weigh(t0 + 1, 1)
                if not last:
                    scores(t0 + 2)
                project(i * 3 + (QKV + 2), 2, i * 16 + 64)
                turn_attention(t0 + 1)

            pe.wait_ge(const_made, CONST_ALL)
            pe.wait_ge(v_ready, 1)
            scores(0)
            pe.wait_ge(kv_rows_ready, 3)
            pair(0)
            with pe.Fori(1, CC - 1) as i:
                pair(i)
            pair(CC - 1, True)
            conv_means(CC - 1)
            conv_scales(CC - 1, TILES - 1)
            for c in range(CC):
                mm = pe.transpose(bank[0:2 + NS, 3, c * P:(c + 1) * P], u_last[:, c, :], ident[:, :])
            mm.then_inc(u_turned, 1)

            pe.wait_ge(cache_arrived, 32)
            pe.wait_ge(conv_ready, 2 * CC)
            for n in range(NS):
                mm = pe.transpose(bank[:, n // 4, (n % 4) * P:(n % 4 + 1) * P], ck[:, n, :], ident[:, :])
            mm.then_inc(ck_turned, 1)
            pe.wait_ge(kTs_ready, 1)
            pe.wait_ge(qbd_ready, 2)
            pe.wait_ge(u_rows_ready, 1)
            pe.wait_ge(atT_ready, TILES)
            for n in range(NS):
                pe.matmul(bank[0:NH, 2 + n // 4, (n % 4) * P:(n % 4 + 1) * P], qbd[:, n, :], kTs[:, n, :], start=True, stop=True)
                mm = pe.matmul(bank[0:NH, 4, n:n + 1], qbd[:, n, :], qkvT[:, 4, SEQ + n:SEQ + n + 1], start=True, stop=True)
            mm.then_inc(s_scored, 1)
            pe.wait_ge(s_exp_ready, 2)
            for n in range(NS):
                pe.transpose(bank[:, 0, n * NH:(n + 1) * NH], s_p[:, n, 0:P], ident[0:NH, 0:NH])
            pe.transpose(bank[0:NS, 1, 0:NH], s_p[:, :, P], ident[0:NH, 0:NH]).then_inc(s_turned, 1)
            pe.wait_ge(s_pT_ready, 2)
            for n in range(NS):
                out = bank[0:NH, 2 + n // 4, (n % 4) * P:(n % 4 + 1) * P]
                pe.matmul(out, s_pT[:, n, :], cv[:, n, :], start=True, stop=False)
                mm = pe.matmul(out, s_z[:, n, :], kvs_rows[:, 1, :], start=False, stop=True)
            mm.then_inc(s_pv_done, 1)
            pe.wait_ge(s_n_ready, 1)
            for n in range(NS):
                mm = pe.transpose(bank[0:HD, 0, n * NH:(n + 1) * NH], s_n[:, n, :], ident[0:NH, 0:NH])
            mm.then_inc(s_n_turned, 1)

            def project_out(t, k):
                n = rows_of(t)
                pe.wait_ge(mix_staged, t + 1)
                if late(t, 2):
                    pe.wait_ge(x2_ready, t - 1)
                for half in range(2):
                    for c in range(KC):
                        mm = pe.matmul(bank[0:n, 2 * k + half, :], mix_st[k][:, c, 0:n], w_o[:, c, half * 512:(half + 1) * 512],
                                       start=c == 0, stop=c == KC - 1)
                mm.then_inc(out_done, 1)

            def route(t, k):
                n = rows_of(t)
                pe.wait_ge(xn2_ready, t + 1)
                for c in range(KC):
                    mm = pe.transpose(bank[:, 4 + c // 4, (c % 4) * P:(c % 4) * P + n], xn2[k][0:n, c * P:(c + 1) * P], ident[0:n, 0:n])
                mm.then_inc(xn2_turned, 1)
                pe.wait_ge(xn2T_ready, t + 1)
                if late(t):
                    pe.wait_ge(logits_ready, t)
                for c in range(KC):
                    mm = pe.matmul(bank[0:n, 7, 0:NR], xn2T[:, c, 0:n], w_r[:, c, :], start=c == 0, stop=c == KC - 1)
                mm.then_inc(routed, 1)

            pe.wait_ge(w_o_arrived, 16)
            pe.wait_ge(late_const_in, 16 * 6)
            project_out(0, 0)
            for t in range(2):
                project_out(t + 1, (t + 1) % 2)
                route(t, t % 2)
            with pe.Fori(1, TILES // 2 - 1) as i:
                for k in range(2):
                    project_out(i * 2 + (k + 1), (k + 1) % 2)
                    route(i * 2 + k, k)
            for t in range(TILES - 2, ALLT):
                if t < TILES:
                    project_out(t + 1, (t + 1) % 2)
                route(t, t % 2)

            pe.wait_ge(picks_ready, 1)
            pe.matmul(bank[:, 0, 0:ALLT * NE], earlier[:, :], both.rearrange("p t e -> p (t e)"), start=True, stop=False)
            pe.matmul(bank[:, 0, 0:ALLT * NE], ones[:, :], before[:, 0:ALLT, :].rearrange("p t e -> p (t e)"), start=False, stop=True)
            pe.matmul(bank[:, 1, 0:NE], ones[:, :], before[:, ALLT, :], start=True, stop=True).then_inc(places_done, 1)
            pe.wait_ge(table_in_ready, 1)
            for j in range(2 * ALLT):
                mm = pe.matmul(bank[:, 2, 0:2 * SLOT_TILES], row_hot[:, j, :], payload[:, j, :, :].rearrange("p v u -> p (v u)"),
                               start=j == 0, stop=j == 2 * ALLT - 1)
            mm.then_inc(table_done, 1)

            def turn_tokens(u, k, arrived):
                pe.wait_ge(x_gathered[k], arrived)
                if late(u):
                    pe.wait_ge(xgT_ready, u)
                for c in range(KC):
                    mm = pe.transpose(bank[:, c // 4, (c % 4) * P:(c % 4 + 1) * P], xg[k][:, c * P:(c + 1) * P], ident[:, :])
                mm.then_inc(xg_turned, 1)

            def gate_and_up(u, k, arrived):
                pe.wait_ge(gu_gathered[k], arrived)
                pe.wait_ge(xgT_ready, u + 1)
                if late(u, 2):
                    pe.wait_ge(hid_ready, u - 1)
                for c in range(KC):
                    mm = pe.matmul(bank[:, 2 + k, :].rearrange("p (v f) -> p v f", v=2), xgT[k][:, c, :], w_gu[k][:, :, c, :], start=c == 0, stop=c == KC - 1)
                mm.then_inc(h_done, 1)

            def turn_hidden(u, k):
                pe.wait_ge(hid_ready, u + 1)
                if late(u):
                    pe.wait_ge(hidT_ready, u)
                for c in range(FC):
                    mm = pe.transpose(bank[:, 4, c * P:(c + 1) * P], hid[k][:, c, :], ident[:, :])
                mm.then_inc(hid_turned, 1)

            def down(u, k, arrived):
                pe.wait_ge(dn_gathered[k], arrived)
                pe.wait_ge(hidT_ready, u + 1)
                for half in range(2):
                    if late(u):
                        pe.wait_ge((y_left_ready, y_right_ready)[half], u)
                    for c in range(FC):
                        mm = pe.matmul(bank[:, 5 + half, :], hidT[k][:, c, :], w_dn[k][:, c, half * 512:(half + 1) * 512],
                                       start=c == 0, stop=c == FC - 1)
                    mm.then_inc(y_done, 1)

            def tile(u, i, k):
                turn_hidden(u, k)
                if late(u + 1, 0) and not (isinstance(u, int) and u + 1 >= SLOT_TILES):
                    gate_and_up(u + 1, 1 - k, (i + k) * 32 + 32)
                if not (isinstance(u, int) and u + 2 >= SLOT_TILES):
                    turn_tokens(u + 2, k, i * 16 + 32)
                down(u, k, i * 16 + 16)

            turn_tokens(0, 0, 16)
            gate_and_up(0, 0, 32)
            turn_tokens(1, 1, 16)
            tile(0, 0, 0)
            tile(1, 0, 1)
            with pe.Fori(1, SLOT_TILES // 2 - 1) as i:
                for k in range(2):
                    tile(i * 2 + k, i, k)
            tile(SLOT_TILES - 2, SLOT_TILES // 2 - 1, 0)
            tile(SLOT_TILES - 1, SLOT_TILES // 2 - 1, 1)

        @block.vector
        def _(dve):
            st = Steps(dve, dve_step)

            def bc(ap, n):
                return ap.unsqueeze(2).broadcast_to([ap.shape[0], ap.shape[1], n])

            def late(t, least=1):
                return not isinstance(t, int) or t >= least

            dve.wait_ge(const_in, 16 * 10)
            st.then(dve.tensor_scalar(nsink[:, :], sink_in[:, :], -1.0, None, ALU.mult))
            st.then(dve.tensor_scalar(nsink_s[:, :], sink_in_s[:, :], -1.0, None, ALU.mult))

            def scale_x(t, k):
                n = rows_of(t)
                if late(t, 2):
                    dve.wait_ge(x_turned, t - 1)
                dve.wait_ge(rstd1_ready, t + 1)
                dve.tensor_scalar(x_sc[k][0:n, :], x_in[k][0:n, :], rstd[0][0:n, col(t)], None, ALU.mult).then_inc(x_scaled, 1)

            def xT_out(t, k):
                n = rows_of(t)
                dve.wait_ge(x_turned, t + 1)
                dve.tensor_tensor(xnT[:, :, cols(t)], bank[:, 2 * k:2 * k + 2, :].rearrange("p b (c t) -> p (b c) t", t=P)[:, :, 0:n],
                                  bc(g1[:, :], n), ALU.mult).then_inc(xnT_ready, 1)

            scale_x(0, 0)
            scale_x(1, 1)
            xT_out(0, 0)
            with dve.Fori(1, TILES // 2) as i:
                for k in range(2):
                    scale_x(i * 2 + k, k)
                    xT_out(i * 2 + (k - 1), 1 - k)
            scale_x(TILES, 0)
            xT_out(TILES - 1, 1)
            xT_out(TILES, 0)

            dve.wait_ge(hist_turned, 1)
            dve.tensor_copy(histT[:, :, :], bank[:, 4, 0:CC * 2 * NS].rearrange("p (c n) -> p c n", c=CC)).then_inc(hist_ready, 1)

            dve.wait_ge(v_turned, 1)
            dve.tensor_copy(kv_rows[:, 1, :], bank[:, 1, 3 * P:4 * P]).then_inc(kv_rows_ready, 1)
            dve.tensor_copy(v_tok[:, 1:ALLT, :], bank[:, 0:2, :].rearrange("p b (c t) -> p (b c) t", t=P)).then_inc(v_ready, 1)
            dve.wait_ge(kv_turned, 1)
            dve.tensor_copy(kv_rows[:, 0, :], bank[:, 4, 0:P]).then_inc(kv_rows_ready, 1)
            dve.tensor_copy(kvs_rows[:, :, :], bank[0:NS, 4, P:3 * P].rearrange("p (j f) -> p j f", j=2)).then_inc(kv_rows_ready, 1)
            dve.wait_ge(const_made, CONST_ALL)
            dve.wait_ge(run_out, NB * QKV)
            for g in range(NKV):
                h = slice(g * HD, (g + 1) * HD)
                dve.tensor_scalar(qbd[h, :, 4 * g:4 * g + 4], qkvT[h, 0:4, SEQ:NT].rearrange("p j n -> p n j"),
                                  HD ** -0.5, None, ALU.mult).then_inc(qbd_ready, 1)

            kT_flat = qkvT[:, :, :].rearrange("p c t -> p (c t)")

            def stage(t):
                if late(t):
                    dve.wait_ge(scores_done, t * 2)
                dve.tensor_scalar(qs[:, :, :], qkvT[:, 0:4, cols(t)], HD ** -0.5, None, ALU.mult).then_inc(staged, 1)
                at = 4 * NT - P + t * P if isinstance(t, int) else t * P + (4 * NT - P)
                dve.tensor_scalar(kb[:, :], kT_flat[:, ds(at, 2 * P)], 1.0, None, ALU.mult).then_inc(staged, 1)

            def soften(t, k):
                mask = band_mask[:, t, :] if isinstance(t, int) else band_mask[:, ds(t, 1), :].rearrange("p o c -> p (o c)")
                for half in range(2):
                    dve.wait_ge(scores_done, t * 2 + (half + 1))
                    dve.tensor_tensor(prob[k][:, 4 * half:4 * half + 4, :], bank[:, 0:2, :].rearrange("p b (x c) -> p (b x) c", x=2),
                                      mask.unsqueeze(1).broadcast_to([P, 4, 2 * P]), ALU.add).then_inc(scores_read, 1)
                dve.wait_ge(scores_read, t * 2 + 2)
                st.then(dve.tensor_reduce(mx[:, :], prob[k][:, :, :], AX, ALU.max))
                dve.scalar_tensor_tensor(out=nm[k][:, :], in0=mx[:, :], scalar=-1.0, in1=nsink[:, :], op0=ALU.mult, op1=ALU.min).then_inc(nm_ready, 1)
                dve.wait_ge(nm_ready, t + 1)
                dve.tensor_tensor(sd[k][:, :], nm[k][:, :], nsink[:, :], ALU.subtract).then_inc(sd_ready, 1)

            def norm_heads(t, k):
                dve.wait_ge(exp_ready, t + 1)
                st.then(dve.tensor_tensor(den[k][:, :], den[k][:, :], es[k][:, :], ALU.add))
                st.then(dve.reciprocal(rden[:, :], den[k][:, :]))
                dve.wait_ge(pv_done, t + 1)
                o = at_o[:, :].rearrange("p (h d) -> p h d", d=HD)
                st.then(dve.tensor_tensor(o, bank[:, 4, :].rearrange("p (h d) -> p h d", d=HD), bc(rden[:, :], HD), ALU.mult))
                st.then(dve.tensor_tensor(at_sq[:, :], at_o[:, :], at_o[:, :], ALU.mult))
                st.then(dve.tensor_reduce(at_ms[:, :], at_sq[:, :].rearrange("p (h d) -> p h d", d=HD), AX, ALU.add))
                dve.tensor_scalar(at_ms[:, :], at_ms[:, :], 1.0 / HD, EPS, ALU.mult, ALU.add).then_inc(at_ms_ready, 1)
                dve.wait_ge(at_r_ready, t + 1)
                dve.tensor_tensor(at_n[:, :].rearrange("p (h d) -> p h d", d=HD), o, bc(at_r[:, :], HD), ALU.mult).then_inc(at_n_ready, 1)

            def attention_out(t):
                dve.wait_ge(at_turned, t + 1)
                dve.tensor_tensor(mixedT[:, 0:AC, cols(t)], bank[:, 4, :].rearrange("p (c t) -> p c t", t=P), bc(ga[:, :], P), ALU.mult).then_inc(atT_ready, 1)

            def taps(i):
                dve.wait_ge(run_out, i * (3 * NB) + NB * (QKV + 2))
                cwi = cwg[:, i, :] if isinstance(i, int) else cwg[:, ds(i, 1), :].rearrange("p o j -> p (o j)")
                st.then(dve.tensor_scalar(cw[:, :], cwi, 1.0, None, ALU.mult))
                dve.tensor_tensor(uT[:, 2:2 + NT], hcb[:, 0, :], hcb[:, 1, :], ALU.mult).then_inc(u_ready, 1)
                dve.wait_ge(u_ready, i + 1)
                st.then(dve.tensor_scalar(zT[:, 0:SEQ], uT[:, 0:SEQ], cw[:, 0:1], None, ALU.mult))
                for j in (1, 2):
                    st.then(dve.scalar_tensor_tensor(out=zT[:, 0:SEQ], in0=uT[:, j:j + SEQ], scalar=cw[:, j:j + 1], in1=zT[:, 0:SEQ],
                                                     op0=ALU.mult, op1=ALU.add))
                h = (histT[:, i, :] if isinstance(i, int) else histT[:, ds(i, 1), :].rearrange("p o n -> p (o n)")).rearrange("p (n j) -> p n j", j=2)
                z = zT[:, SEQ:NT]
                st.then(dve.tensor_scalar(z, h[:, :, 0], cw[:, 0:1], None, ALU.mult))
                st.then(dve.scalar_tensor_tensor(out=z, in0=h[:, :, 1], scalar=cw[:, 1:2], in1=z, op0=ALU.mult, op1=ALU.add))
                st.then(dve.scalar_tensor_tensor(out=z, in0=uT[:, 2 + SEQ:2 + NT], scalar=cw[:, 2:3], in1=z, op0=ALU.mult, op1=ALU.add))
                last = u_last[:, i, :] if isinstance(i, int) else u_last[:, ds(i, 1), :].rearrange("p o n -> p (o n)")
                st.then(dve.tensor_scalar(last, uT[:, SEQ:2 + NT], 1.0, None, ALU.mult))

            def gated(i):
                dve.wait_ge(run_out, i * (3 * NB) + NB * (QKV + 3))
                st.then(dve.tensor_tensor(zT[:, :], zT[:, :], hcb[:, 2, :], ALU.mult))
                dve.tensor_tensor(sqT[:, 0:NT], zT[:, :], zT[:, :], ALU.mult).then_inc(sq_ready, 1)

            def conv_rstd(i):
                dve.wait_ge(cms_done, i + 1)
                dve.tensor_scalar(cms[:, :], bank[:, 2, 0:2 * ALLT], EPS, None, ALU.add).then_inc(cms_ready, 1)
                dve.wait_ge(crs_ready, i + 1)
                dve.tensor_copy(crs_row[:, :].rearrange("p (m d) -> p m d", d=HD), bc(crs[:, :], HD)).then_inc(crs_row_ready, 1)

            def conv_out(i):
                dve.wait_ge(crs_turned, i + 1)
                at = mixedT[:, AC + i, :] if isinstance(i, int) else mixedT[:, ds(i + AC, 1), :].rearrange("p o t -> p (o t)")
                dve.scalar_tensor_tensor(out=at[:, 0:SEQ].rearrange("p (b t) -> p b t", b=2), in0=bank[:, 0:2, :], scalar=cw[:, 3:4],
                                         in1=zT[:, 0:SEQ].rearrange("p (b t) -> p b t", b=2), op0=ALU.mult, op1=ALU.mult).then_inc(conv_ready, 1)
                dve.scalar_tensor_tensor(out=at[:, SEQ:NT], in0=bank[:, 2, 2 * P - NS:2 * P], scalar=cw[:, 3:4], in1=zT[:, SEQ:NT],
                                         op0=ALU.mult, op1=ALU.mult).then_inc(conv_ready, 1)

            def pair(i, last=False):
                t0 = i * 2
                stage(t0 + 1)
                soften(t0 + 1, 1)
                norm_heads(t0, 0)
                if late(i):
                    conv_rstd(i - 1)
                    conv_out(i - 1)
                attention_out(t0)
                if not last:
                    stage(t0 + 2)
                    soften(t0 + 2, 0)
                norm_heads(t0 + 1, 1)
                taps(i)
                gated(i)
                attention_out(t0 + 1)

            stage(0)
            soften(0, 0)
            pair(0)
            st.loop(1, CC - 1, 2 + 10 + 8 + 1, pair)
            pair(CC - 1, True)
            conv_rstd(CC - 1)
            conv_out(CC - 1)
            dve.wait_ge(u_turned, 1)
            dve.tensor_copy(u_rows[:, :], bank[0:2 + NS, 3, :]).then_inc(u_rows_ready, 1)

            dve.wait_ge(s_scored, 1)
            st.then(dve.tensor_copy(s_sc[:, :, 0:P], bank[0:NH, 2:4, :].rearrange("p b (n t) -> p (b n) t", t=P)))
            st.then(dve.tensor_copy(s_sc[:, :, P], bank[0:NH, 4, 0:NS]))
            st.then(dve.tensor_reduce(s_mx[:, :], s_sc, AX, ALU.max))
            st.then(dve.scalar_tensor_tensor(out=s_nm[:, :], in0=s_mx[:, :], scalar=-1.0, in1=nsink_s[:, :].broadcast_to([NH, NS]),
                                             op0=ALU.mult, op1=ALU.min))
            st.then(dve.tensor_tensor(s_es[:, :], s_nm[:, :], nsink_s[:, :].broadcast_to([NH, NS]), ALU.subtract))
            dve.tensor_tensor(s_sc, s_sc, bc(s_nm[:, :], P + 1), ALU.add).then_inc(s_shifted, 1)
            dve.wait_ge(s_exp_ready, 2)
            st.then(dve.tensor_reduce(s_dn[:, :], s_p, AX, ALU.add))
            st.then(dve.tensor_tensor(s_dn[:, :], s_dn[:, :], s_es[:, :], ALU.add))
            st.then(dve.reciprocal(s_dn[:, :], s_dn[:, :]))
            dve.wait_ge(s_turned, 1)
            dve.tensor_copy(s_pT[:, :, :], bank[:, 0, 0:NS * NH].rearrange("p (n h) -> p n h", h=NH)).then_inc(s_pT_ready, 1)
            dve.tensor_tensor(s_z[:, :, :], bank[0:NS, 1, 0:NH].unsqueeze(1).broadcast_to([NS, NS, NH]), bc(ident[0:NS, 0:NS], NH),
                              ALU.mult).then_inc(s_pT_ready, 1)
            dve.wait_ge(s_pv_done, 1)
            st.then(dve.tensor_tensor(s_o2, bank[0:NH, 2:4, :].rearrange("p b (n f) -> p (b n) f", f=P),
                                      half_mask[:, :].unsqueeze(1).broadcast_to([NH, NS, P]), ALU.mult))
            st.then(dve.tensor_tensor(s_o, s_o2[:, :, 0:HD], s_o2[:, :, HD:P], ALU.add))
            st.then(dve.tensor_tensor(s_o, s_o, bc(s_dn[:, :], HD), ALU.mult))
            st.then(dve.tensor_tensor(s_sq, s_o, s_o, ALU.mult))
            st.then(dve.tensor_reduce(s_ms[:, :], s_sq, AX, ALU.add))
            dve.tensor_scalar(s_ms[:, :], s_ms[:, :], 1.0 / HD, EPS, ALU.mult, ALU.add).then_inc(s_ms_ready, 1)
            dve.wait_ge(s_r_ready, 1)
            st.then(dve.tensor_tensor(s_n, s_o, bc(s_r[:, :], HD), ALU.mult))
            dve.tensor_tensor(s_n, s_n, ga_s[:, :].unsqueeze(1).broadcast_to([NH, NS, HD]), ALU.mult).then_inc(s_n_ready, 1)
            dve.wait_ge(s_n_turned, 1)
            turned = bank[0:HD, 0, 0:NS * NH].rearrange("p (n c x) -> p c n x", n=NS, x=2)
            for x in range(2):
                dve.tensor_copy(mixedT[x * HD:(x + 1) * HD, 0:AC, SEQ:NT], turned[:, :, :, x]).then_inc(s_mixed, 1)

            dve.wait_ge(s_mixed, 2)
            st.then(dve.memset(logits[:, :, :], 0.0))
            dve.wait_ge(x_again, 32)
            dve.wait_ge(late_const_in, 16 * 6)

            def x2_of(t):
                return x2[0:rows_of(t), t, :] if isinstance(t, int) else x2[:, ds(t, 1), :].rearrange("p o d -> p (o d)")

            def residual(t, k, free):
                n = rows_of(t)
                dve.wait_ge(out_done, t + 1)
                dve.tensor_tensor(x2_of(t), bank[0:n, 2 * k:2 * k + 2, :].rearrange("p b d -> p (b d)"), x2_of(t), ALU.add).then_inc(x2_ready, 1)
                dve.wait_ge(rstd2_ready, t + 1)
                if late(t, 2):
                    dve.wait_ge(xn2_stored[k], free)
                dve.scalar_tensor_tensor(out=xn2[k][0:n, :].rearrange("p (c q) -> p q c", c=KC), in0=x2_of(t).rearrange("p (q c) -> p q c", c=KC),
                                         scalar=rstd[1][0:n, col(t)], in1=g2[0:n, :].rearrange("p (q c) -> p q c", c=KC),
                                         op0=ALU.mult, op1=ALU.mult).then_inc(xn2_ready, 1)
                dve.wait_ge(routed, t + 1)
                lt = logits[0:n, t, :] if isinstance(t, int) else logits[:, ds(t, 1), :].rearrange("p o r -> p (o r)")
                dve.tensor_tensor(lt, bank[0:n, 7, 0:NR], b_r[0:n, :], ALU.add).then_inc(logits_ready, 1)

            residual(0, 0, 0)
            residual(1, 1, 0)
            with dve.Fori(1, TILES // 2) as i:
                for k in range(2):
                    residual(i * 2 + k, k, i * 16)
            residual(TILES, 0, 16 * (TILES // 2))

            dve.wait_ge(logits_ready, ALLT)

            def first_of_max(vals, top, hot, a, b):
                st.then(dve.tensor_reduce(top, vals, AX, ALU.max))
                st.then(dve.tensor_tensor(a, vals, bc(top, EG), ALU.is_equal))
                st.then(dve.tensor_tensor(a, a, rev4[:, :, :], ALU.mult))
                st.then(dve.tensor_reduce(b, a, AX, ALU.max))
                st.then(dve.tensor_tensor(hot, a, bc(b, EG), ALU.is_equal))

            top_c, tmp9, top1, top2, denom, ratio, psel, one_r = [r[:, :] for r in r9]
            hot_g, hot_1, fine, tmp4, shifted = [r[:, :, :] for r in r4]
            coarse = logits[:, :, 0:NG]
            first_of_max(coarse, top_c, hot_g, tmp4, tmp9)
            dve.tensor_tensor(shifted, coarse, bc(top_c, NG), ALU.subtract).then_inc(r_shifted, 1)
            g_e = "p t (g j) -> p t g j"
            st.then(dve.tensor_tensor(prod16.rearrange(g_e, g=NG), logits[:, :, NG:NR].rearrange(g_e, g=NG),
                                      hot_g.unsqueeze(3).broadcast_to([P, ALLT, NG, EG]), ALU.mult))
            st.then(dve.tensor_reduce(fine, prod16.rearrange("p t (g j) -> p t j g", g=NG), AX, ALU.add))
            first_of_max(fine, top1, hot_1, tmp4, tmp9)

            def picked(k, hot):
                st.then(dve.tensor_tensor(pick[:, k, :, :].rearrange(g_e, g=NG), hot_g.unsqueeze(3).broadcast_to([P, ALLT, NG, EG]),
                                          hot.unsqueeze(2).broadcast_to([P, ALLT, NG, EG]), ALU.mult))
                st.then(dve.tensor_tensor(pick[:, k, :, :], pick[:, k, :, :], bc(valid[:, :], NE), ALU.mult))

            picked(0, hot_1)
            st.then(dve.scalar_tensor_tensor(out=fine, in0=hot_1, scalar=LOWEST, in1=fine, op0=ALU.mult, op1=ALU.add))
            first_of_max(fine, top2, hot_1, tmp4, tmp9)
            dve.tensor_tensor(ratio, top2, top1, ALU.subtract).then_inc(r_shifted, 1)
            picked(1, hot_1)
            st.then(dve.tensor_tensor(both, pick[:, 0, :, :], pick[:, 1, :, :], ALU.add))
            st.then(dve.memset(before[:, 0, :], 0.0))
            for t in range(ALLT):
                ins = dve.tensor_tensor(before[:, t + 1, :], before[:, t, :], both[:, t, :], ALU.add)
                if t < ALLT - 1:
                    st.then(ins)
            ins.then_inc(picks_ready, 1)
            dve.wait_ge(r_exp_ready, 2)
            st.then(dve.tensor_reduce(denom, shifted, AX, ALU.add))
            st.then(dve.tensor_scalar(one_r, ratio, 1.0, None, ALU.add))
            st.then(dve.tensor_tensor(denom, denom, one_r, ALU.mult))
            st.then(dve.reciprocal(gate[:, 0, :], denom))
            st.then(dve.tensor_tensor(gate[:, 1, :], gate[:, 0, :], ratio, ALU.mult))

            dve.wait_ge(places_done, 1)
            st.then(dve.tensor_copy(count[:, :], bank[:, 1, 0:NE]))
            st.then(dve.tensor_tensor(cmp9, bc(count[:, :], ALLT), steps128[:, :].unsqueeze(1).broadcast_to([P, NE, ALLT]), ALU.is_gt))
            st.then(dve.tensor_reduce(tiles_of[:, :], cmp9, AX, ALU.add))
            src = tiles_of
            for n, sh in enumerate((1, 2, 4, 8)):
                dst = scan[n % 2]
                st.then(dve.tensor_copy(dst[:, 0:sh], src[:, 0:sh]))
                st.then(dve.tensor_tensor(dst[:, sh:NE], src[:, sh:NE], src[:, 0:NE - sh], ALU.add))
                src = dst
            ends = src
            st.then(dve.tensor_tensor(start128[:, :], ends[:, :], tiles_of[:, :], ALU.subtract))
            st.then(dve.tensor_scalar(start128[:, :], start128[:, :], float(P), None, ALU.mult))
            st.then(dve.tensor_tensor(place16, bank[:, 0, 0:ALLT * NE].rearrange("p (t e) -> p t e", e=NE),
                                      start128[:, :].unsqueeze(1).broadcast_to([P, ALLT, NE]), ALU.add))
            for k in range(2):
                st.then(dve.tensor_tensor(prod16, pick[:, k, :, :], place16, ALU.mult))
                st.then(dve.tensor_reduce(slot_f[:, k, :], prod16, AX, ALU.add))
            st.then(dve.tensor_copy(slot_i[:, :, :], slot_f[:, :, :]))
            st.then(dve.tensor_scalar(row_i[:, :, :], slot_i[:, :, :], P - 1, None, ALU.bitwise_and))
            st.then(dve.tensor_scalar(tile_i[:, :, :], slot_i[:, :, :], 7, None, ALU.logical_shift_right))
            st.then(dve.tensor_copy(tile_f[:, :, :], tile_i[:, :, :]))
            st.then(dve.tensor_tensor(row_f[:, :, :], row_i[:, :, :], nowhere[:, :, :], ALU.add))
            kt = "p k t -> p (k t)"
            st.then(dve.tensor_tensor(row_hot, bc(row_f[:, :, :].rearrange(kt), P), iota_row[:, :].unsqueeze(1).broadcast_to([P, 2 * ALLT, P]), ALU.is_equal))
            st.then(dve.tensor_tensor(tile_hot, bc(tile_f[:, :, :].rearrange(kt), SLOT_TILES),
                                      iota_row[:, 0:SLOT_TILES].unsqueeze(1).broadcast_to([P, 2 * ALLT, SLOT_TILES]), ALU.is_equal))
            st.then(dve.tensor_tensor(payload[:, :, 1, :], tile_hot, bc(gate[:, :, :].rearrange(kt), SLOT_TILES), ALU.mult))
            for k in range(2):
                j = slice(k * ALLT, (k + 1) * ALLT)
                ins = dve.tensor_tensor(payload[:, j, 0, :], tile_hot[:, j, :], bc(token_no[:, :], SLOT_TILES), ALU.mult)
                if k == 0:
                    st.then(ins)
            ins.then_inc(table_in_ready, 1)
            dve.wait_ge(table_done, 1)
            st.then(dve.tensor_copy(slot_tok[:, :], bank[:, 2, 0:SLOT_TILES]))
            st.then(dve.tensor_copy(slot_gate[:, :], bank[:, 2, SLOT_TILES:2 * SLOT_TILES]))
            st.then(dve.tensor_tensor(cmp16, ends[:, :].unsqueeze(1).broadcast_to([P, SLOT_TILES, NE]), bc(iota_row[:, 0:SLOT_TILES], NE), ALU.is_le))
            st.then(dve.tensor_reduce(tile_ex[:, :], cmp16, AX, ALU.add))
            st.then(dve.tensor_scalar(tile_ex[:, :], tile_ex[:, :], float(NE - 1), float(P), ALU.min, ALU.mult))
            dve.tensor_scalar(w_row[:, :], tile_ex[:, :], iota_p[:, 0:1], None, ALU.add).then_inc(slots_ready, 1)

            def hidden(u, k):
                dve.wait_ge(silu_ready, u + 1)
                qc = "p (q c) -> p q c"
                dve.scalar_tensor_tensor(out=hid[k][:, :, :].rearrange("p c q -> p q c"), in0=bank[:, 2 + k, FE:2 * FE].rearrange(qc, c=FC),
                                         scalar=slot_gate[:, col(u)], in1=silu[k][:, :].rearrange(qc, c=FC), op0=ALU.mult, op1=ALU.mult).then_inc(hid_ready, 1)

            def y_out(u, k):
                if late(u, 2):
                    dve.wait_ge(y_stored[k], u // 2 * 16 if isinstance(u, int) else (u - k) * 8)
                dve.wait_ge(y_done, u * 2 + 2)
                dve.tensor_copy(y_sb[k][:, 512:D], bank[:, 6, :]).then_inc(y_right_ready, 1)

            hidden(0, 0)
            hidden(1, 1)
            y_out(0, 0)
            hidden(2, 0)
            y_out(1, 1)
            with dve.Fori(1, SLOT_TILES // 2 - 1) as i:
                hidden(i * 2 + 1, 1)
                y_out(i * 2, 0)
                hidden(i * 2 + 2, 0)
                y_out(i * 2 + 1, 1)
            hidden(SLOT_TILES - 1, 1)
            y_out(SLOT_TILES - 2, 0)
            y_out(SLOT_TILES - 1, 1)

            def add_pair(t, k, arrived):
                n = rows_of(t)
                dve.wait_ge(pair_gathered[k], arrived)
                st.then(dve.tensor_tensor(x2_of(t), x2_of(t), pair_rows[k][0][0:n, :], ALU.add))
                dve.tensor_tensor(x2_of(t), x2_of(t), pair_rows[k][1][0:n, :], ALU.add).then_inc(x3_ready, 1)

            def last_norm(t, k, free):
                n = rows_of(t)
                dve.wait_ge(rstd3_ready, t + 1)
                if late(t, 2):
                    dve.wait_ge(out_stored[k], free)
                dve.scalar_tensor_tensor(out=y_sb[k][0:n, :], in0=x2_of(t), scalar=rstd[2][0:n, col(t)], in1=gf[0:n, :],
                                         op0=ALU.mult, op1=ALU.mult).then_inc(out_ready, 1)

            dve.wait_ge(y_stored[0], 16 * (SLOT_TILES // 2))
            dve.wait_ge(y_stored[1], 16 * (SLOT_TILES // 2))
            add_pair(0, 0, 32)
            add_pair(1, 1, 32)
            last_norm(0, 0, 0)
            last_norm(1, 1, 0)

            def sum_pair(i):
                for k in range(2):
                    add_pair(i * 2 + k, k, i * 32 + 32)
                    last_norm(i * 2 + k, k, i * 16)

            st.loop(1, TILES // 2, 2, sum_pair)
            add_pair(TILES, 0, 32 * (TILES // 2 + 1))
            last_norm(TILES, 0, 16 * (TILES // 2))


CONST_ALL = 28


_INS = ["x_prompt", "x_sample", "cache_k_win", "cache_v_win", "state_conv", "norm1_g", "w_in", "conv_w", "sinks",
        "attn_out_g", "conv_out_g", "w_out", "norm2_g", "w_group", "b_group", "w_fine", "b_fine", "w_gate", "w_up",
        "w_down", "final_g"]
_OUTS = [(1, SEQ, D), (NS, 1, D), (1, 1, P, NKV, HD), (1, 1, P, NKV, HD), (1, 1, 2, CONV),
         (1, NS, P, NKV, HD), (1, NS, P, NKV, HD), (1, NS, 2, CONV)]


def kernel(**inputs):
    import numpy as _np
    import concourse.bacc as _bacc
    from concourse import mybir as _mybir
    from concourse.bass_utils import run_bass_kernel_spmd as _run

    nc = _bacc.Bacc("TRN2", target_bir_lowering=False, num_devices=1)
    arrays, args = {}, []
    for name in _INS:
        a = _np.ascontiguousarray(inputs[name])
        arrays[f"in_{name}_dram"] = a
        args.append(nc.dram_tensor(f"in_{name}_dram", a.shape, _mybir.dt.from_np(a.dtype), kind="ExternalInput").ap())
    for i, shape in enumerate(_OUTS):
        args.append(nc.dram_tensor(f"out_{i}_dram", shape, _mybir.dt.float32, kind="ExternalOutput").ap())
    hybrid_layer_step(nc, *args)
    r = _run(nc, [arrays], core_ids=[0])
    return tuple(r.results[0][f"out_{i}_dram"] for i in range(len(_OUTS)))
```

```python
from contextlib import ExitStack

import concourse.bass as bass
from concourse import mybir
from concourse.bass import ds

P = 128
D = 1024
KC = D // P
SEQ = 1024
NS = 8
NT = SEQ + NS
TILES = SEQ // P
ALLT = TILES + 1
HD = 64
NH = 8
NKV = 2
ATT = NH * HD
AC = ATT // P
CONV = D - ATT
CC = CONV // P
OFF_K = ATT
OFF_V = OFF_K + NKV * HD
OFF_B = OFF_V + NKV * HD
OFF_C = OFF_B + CONV
OFF_H = OFF_C + CONV
QKV = 6
NG = 4
EG = 4
NE = NG * EG
FE = 256
FC = FE // P
NR = NG + NE
SLOT_TILES = (2 * NT + NE * (P - 1)) // P
LEAST_TILES = 2 * NT // P
FILL = SLOT_TILES - LEAST_TILES
PLANNED = SLOT_TILES + 2
EW = 3 * KC * FE
EB = 3
PL_BUF = 0
PL_ARRIVED = PL_BUF + PLANNED
PL_EXPERT = PL_ARRIVED + PLANNED
PL_FREED = PL_EXPERT + NE
PL_TILES = PL_FREED + NE
PL_EXPERTS = PL_TILES + 1
PL_STORED = PL_EXPERTS + 1
PL_ALL = PL_STORED + 2
NB = 3
RUN = NT // NB
WB = 3
CHUNKS = QKV + 3 * CC
XB = 4
LB = 3
EPS = 1e-5
MASKED = -1e30
LOWEST = -3e38
NOWHERE = 999.0

F32 = mybir.dt.float32
F32R = mybir.dt.float32r
I32 = mybir.dt.int32
ALU = mybir.AluOpType
ACT = mybir.ActivationFunctionType
AX = mybir.AxisListType.X


class Steps:

    def __init__(self, eng, sem):
        self.eng, self.sem, self.base, self.n = eng, sem, 0, 0

    def then(self, ins):
        ins.then_inc(self.sem, 1)
        self.n += 1
        self.eng.wait_ge(self.sem, self.base + self.n)

    def loop(self, lo, hi, per, body):
        start = self.n
        with self.eng.Fori(lo, hi) as i:
            self.base = (i - lo) * per
            body(i)
        assert self.n == start + per, f"{self.n - start} steps, not {per}"
        self.base, self.n = 0, start + per * (hi - lo)


def hybrid_layer_step(nc, x_prompt, x_sample, cache_k_win, cache_v_win, state_conv, norm1_g, w_in,
                      conv_w, sinks, attn_out_g, conv_out_g, w_out, norm2_g, w_group, b_group,
                      w_fine, b_fine, w_gate, w_up, w_down, final_g,
                      y_prompt, y_sample, new_k_prompt, new_v_prompt, new_conv_prompt,
                      new_k_sample, new_v_sample, new_conv_sample):
    xp, x_smp = x_prompt[0], x_sample[:, 0, :]
    w_in_v = w_in[0].rearrange("(c p) f -> p c f", p=P)
    w_out_v = w_out[0].rearrange("(c p) f -> p c f", p=P)
    expert_parts = [w[0].rearrange("e (p c) f -> e p (c f)", p=P) for w in (w_gate, w_up, w_down)]
    xn2_d = nc.dram_tensor("xn2_rows", [NT, D], F32, kind="Internal").ap()
    y_d = nc.dram_tensor("y_slots", [SLOT_TILES * P, D], F32, kind="Internal").ap()

    ctx = ExitStack()
    with ctx:
        def sem(name):
            return ctx.enter_context(nc.semaphore(name))

        def sems(name, n):
            return [sem(f"{name}{i}") for i in range(n)]

        def alloc(stack, name, shape, dt=F32):
            return stack.enter_context(nc.sbuf_tensor("b_" + name, shape, dt))

        def sb(name, shape, dt=F32):
            return alloc(ctx, name, shape, dt)

        bank = ctx.enter_context(nc.psum_tensor("banks", [P, 8, 512], F32))

        ident = sb("ident", [P, P])
        ones = sb("ones", [P, P])
        earlier = sb("earlier", [P, P])
        group_mean = sb("group_mean", [P, 2])
        exponent = sb("exponent", [P, 2 * ALLT])
        epsilon = sb("epsilon", [P, 1])
        rev4 = sb("rev4", [P, ALLT, EG])
        valid = sb("valid", [P, ALLT])
        nowhere = sb("nowhere", [P, 2, ALLT])
        iota_row = sb("iota_row", [P, P])
        iota_p = sb("iota_p", [P, 1])
        steps128 = sb("steps128", [P, ALLT])
        token_no = sb("token_no", [P, ALLT])
        half_mask = sb("half_mask", [NH, P])
        g1 = sb("g1", [P, KC])
        ga = sb("ga", [P, AC])
        ga_s = sb("ga_s", [NH, HD])
        cwg = sb("cwg", [P, CC, 4])
        sink_in = sb("sink_in", [P, NH])
        nsink = sb("nsink", [P, NH])
        sink_in_s = sb("sink_in_s", [NH, 1])
        nsink_s = sb("nsink_s", [NH, 1])
        w_r = sb("w_r", [P, KC, NR])
        b_r = sb("b_r", [P, NR])

        mixedT = sb("mixedT", [P, KC, NT])
        w_raw = [sb(f"w_raw{i}", [P, D]) for i in range(WB)]
        ms = [sb(f"ms{i}", [P, ALLT]) for i in range(3)]
        rstd = [sb(f"rstd{i}", [P, ALLT]) for i in range(3)]
        kv_rows = sb("kv_rows", [P, 2, P])
        u_rows = sb("u_rows", [2 + NS, CONV])
        kvs_rows = u_rows[0:NS, 0:2 * P].rearrange("p (j f) -> p j f", j=2)

        first = ExitStack()
        xTh = alloc(first, "xTh", [P, KC, NT], F32R)
        xTl = alloc(first, "xTl", [P, KC, NT], F32R)
        wh = [alloc(first, f"wh{i}", [P, KC, P], F32R) for i in range(WB)]
        wl = [alloc(first, f"wl{i}", [P, KC, P], F32R) for i in range(WB)]
        hcb = alloc(first, "hcb", [P, 3, NT])
        hcb_flat = hcb[:, :, :].rearrange("p x t -> p (x t)")
        g1 = hcb_flat[:, 0:D]
        hist = hcb_flat[0:2 * NS, D:D + CONV]
        kT = alloc(first, "kT", [P, NT])
        v_tok = alloc(first, "v_tok", [P, ALLT, P])
        uT = alloc(first, "uT", [P, 2 + NT])
        zT = alloc(first, "zT", [P, NT])
        vT = zT
        sqT = alloc(first, "sqT", [P, ALLT * P])
        u_last = alloc(first, "u_last", [P, CC, 2 + NS])
        histT = alloc(first, "histT", [P, CC, 2 * NS])
        cw = alloc(first, "cw", [P, 4])
        cms = alloc(first, "cms", [P, 2 * ALLT])
        crs = alloc(first, "crs", [P, 2 * ALLT])
        crs_row = sqT
        band_mask = alloc(first, "band_mask", [P, 2, 2 * P])
        qs = alloc(first, "qs", [P, AC, P])
        kb = alloc(first, "kb", [P, 2 * P])
        prob = [alloc(first, f"prob{i}", [P, NH, 2 * P]) for i in range(2)]
        pTs = alloc(first, "pTs", [P, NH, 2, P])
        prob_flat = [b[:, :, :].rearrange("p a b -> p (a b)") for b in prob]
        x_in = [prob_flat[i // 2][:, (i % 2) * D:(i % 2 + 1) * D] for i in range(XB)]
        pTs_flat = pTs[:, :, :, :].rearrange("p a b c -> p (a b c)")
        x_sc = [pTs_flat[:, i * D:(i + 1) * D] for i in range(2)]
        mx = alloc(first, "mx", [P, NH])
        nm = [alloc(first, f"nm{i}", [P, NH]) for i in range(2)]
        sd = [alloc(first, f"sd{i}", [P, NH]) for i in range(2)]
        es = [alloc(first, f"es{i}", [P, NH]) for i in range(2)]
        den = [alloc(first, f"den{i}", [P, NH]) for i in range(2)]
        rden = alloc(first, "rden", [P, NH])
        at_o = alloc(first, "at_o", [P, ATT])
        at_n = alloc(first, "at_n", [P, ATT])
        at_sq = at_n
        at_ms = alloc(first, "at_ms", [P, NH])
        at_r = alloc(first, "at_r", [P, NH])
        conv_half = mixedT[:, AC:KC, :].rearrange("p c t -> p (c t)")
        ck, cv, kTs = [conv_half[:, i * D:(i + 1) * D].rearrange("p (n f) -> p n f", n=NS) for i in range(3)]
        squared1 = conv_half[:, 3 * D:4 * D]
        qbd = kb[:, 0:NS * NH].rearrange("p (n h) -> p n h", n=NS)
        s_sc = prob[0][0:NH, :, :].rearrange("p a b -> p (a b)")[:, 0:NS * (P + 1)].rearrange("p (n t) -> p n t", n=NS)
        s_p = prob[1][0:NH, :, :].rearrange("p a b -> p (a b)")[:, 0:NS * (P + 1)].rearrange("p (n t) -> p n t", n=NS)
        s_o2 = pTs[0:NH, :, :, :].rearrange("p a b c -> p (a b c)")[:, 0:NS * P].rearrange("p (n f) -> p n f", n=NS)
        s_o = at_o[0:NH, :].rearrange("p (n d) -> p n d", n=NS)
        s_sq = at_sq[0:NH, :].rearrange("p (n d) -> p n d", n=NS)
        s_n = at_n[0:NH, :].rearrange("p (n d) -> p n d", n=NS)
        qs_flat = qs[:, :, :].rearrange("p j t -> p (j t)")
        s_pT = qs_flat[:, 0:NS * NH].rearrange("p (n h) -> p n h", n=NS)
        s_z = qs_flat[0:NS, NS * NH:2 * NS * NH].rearrange("p (n h) -> p n h", n=NS)
        s_mx, s_nm, s_es, s_dn, s_ms, s_r = [qs_flat[0:NH, 2 * NS * NH + i * NS:2 * NS * NH + (i + 1) * NS] for i in range(6)]
        first.close()

        projecting = ExitStack()
        w_oh = alloc(projecting, "w_oh", [P, KC, D], F32R)
        w_ol = alloc(projecting, "w_ol", [P, KC, D], F32R)
        x2 = alloc(projecting, "x2", [P, ALLT, D])
        mix_h = [alloc(projecting, f"mix_h{i}", [P, KC, P], F32R) for i in range(2)]
        mix_l = [alloc(projecting, f"mix_l{i}", [P, KC, P], F32R) for i in range(2)]
        projecting.close()
        second = ExitStack()
        w_flat = alloc(second, "w_flat", [P, 2 * KC * D + ALLT * D + EW])
        ew_at = [0, EW, 2 * KC * D + ALLT * D]
        g2 = alloc(second, "g2", [P, D])
        gf = alloc(second, "gf", [P, D])
        junk = alloc(second, "junk", [P, D])
        xn2 = [alloc(second, f"xn2_{i}", [P, D]) for i in range(2)]
        xn2T = alloc(second, "xn2T", [P, KC, P])
        logits = alloc(second, "logits", [P, ALLT, NR])
        r9 = [alloc(second, f"r9_{i}", [P, ALLT]) for i in range(8)]
        r4 = [alloc(second, f"r4_{i}", [P, ALLT, EG]) for i in range(5)]
        count = alloc(second, "count", [P, NE])
        tiles_of = alloc(second, "tiles_of", [P, 2, NE])
        scan = [alloc(second, f"scan{i}", [P, 2, NE]) for i in range(2)]
        tile_j = alloc(second, "tile_j", [P, PLANNED])
        tile_j3 = alloc(second, "tile_j3", [P, PLANNED])
        tile_j3_i = alloc(second, "tile_j3_i", [P, PLANNED], I32)
        last_j = alloc(second, "last_j", [P, 1])
        plan_f = alloc(second, "plan_f", [P, PL_ALL])
        plan = alloc(second, "plan", [P, PL_ALL], I32)
        start128 = alloc(second, "start128", [P, NE])
        slot_f = alloc(second, "slot_f", [P, 2, ALLT])
        slot_i = alloc(second, "slot_i", [P, 2, ALLT], I32)
        row_i = alloc(second, "row_i", [P, 2, ALLT], I32)
        tile_i = alloc(second, "tile_i", [P, 2, ALLT], I32)
        row_f = alloc(second, "row_f", [P, 2, ALLT])
        tile_f = alloc(second, "tile_f", [P, 2, ALLT])
        gate = alloc(second, "gate", [P, 2, ALLT])
        slot_gate = alloc(second, "slot_gate", [P, PLANNED])
        slot_tok = alloc(second, "slot_tok", [P, PLANNED], I32)
        tok_i = [alloc(second, f"tok_i{i}", [P, 1], I32) for i in range(2)]
        pair_i = [[alloc(second, f"pair_i{i}_{j}", [P, 1], I32) for j in range(2)] for i in range(LB)]
        second.close()
        free_at = [0]
        mixed_flat = mixedT[:, :, :].rearrange("p c t -> p (c t)")

        def carve(n):
            free_at[0] += n
            assert free_at[0] <= KC * NT
            return mixed_flat[:, free_at[0] - n:free_at[0]]

        y_sb = [carve(D) for _ in range(2)]
        prod16 = carve(ALLT * NE).rearrange("p (t e) -> p t e", t=ALLT)
        pick = carve(2 * ALLT * NE).rearrange("p (k t e) -> p k t e", k=2, t=ALLT)
        both = carve(ALLT * NE).rearrange("p (t e) -> p t e", t=ALLT)
        before = carve((ALLT + 1) * NE).rearrange("p (t e) -> p t e", e=NE)
        place16 = carve(ALLT * NE).rearrange("p (t e) -> p t e", t=ALLT)
        cmp9 = carve(NE * ALLT).rearrange("p (e t) -> p e t", e=NE)
        row_hot = carve(2 * ALLT * P).rearrange("p (j q) -> p j q", q=P)
        tile_hot = carve(2 * ALLT * PLANNED).rearrange("p (j u) -> p j u", u=PLANNED)
        payload = carve(2 * ALLT * 2 * PLANNED).rearrange("p (j v u) -> p j v u", v=2, u=PLANNED)
        cmp16 = row_hot.rearrange("p j q -> p (j q)")[:, 0:PLANNED * NE].rearrange("p (u e) -> p u e", e=NE)
        cmp_j = row_hot.rearrange("p j q -> p (j q)")[:, PLANNED * NE:(PLANNED + NE) * NE].rearrange("p (j e) -> p j e", e=NE)
        xg = [row_hot.rearrange("p j q -> p (j q)")[:, i * D:(i + 1) * D] for i in range(2)]
        tables = mixed_flat[:, free_at[0] - 3 * 2 * ALLT * PLANNED:free_at[0]]
        silu, hid, hidT = [[tables[:, (2 * j + i) * FE:(2 * j + i + 1) * FE].rearrange("p (c t) -> p c t", c=FC) for i in range(2)] for j in range(3)]
        silu = [x.rearrange("p c t -> p (c t)") for x in silu]
        xgT = [x[:, :].rearrange("p (c t) -> p c t", c=KC) for x in xn2]
        assert 3 * LB <= 2 * KC
        pair_rows = [[w_flat[:, (2 * i + j) * D:(2 * i + j + 1) * D] for j in range(2)] for i in range(LB)]
        out_rows = [w_flat[:, (2 * LB + i) * D:(2 * LB + i + 1) * D] for i in range(LB)]

        const_made, const_in, late_const_in, sinks_ready = sem("const_made"), sem("const_in"), sem("late_const_in"), sem("sinks_ready")
        x_arrived = sems("x_arrived", XB)
        x_hi_ready, w_hi_ready, w_lo_ready = sem("x_hi_ready"), sem("w_hi_ready"), sem("w_lo_ready")
        ms1_ready, eps1_added, rstd1_ready = sem("ms1_ready"), sem("eps1_added"), sem("rstd1_ready")
        x_scaled, x_turned, xnT_ready = sem("x_scaled"), sem("x_turned"), sem("xnT_ready")
        w_arrived = sems("w_arrived", WB)
        run_done, run_out = sem("run_done"), sem("run_out")
        hist_arrived, hist_turned, hist_ready = sem("hist_arrived"), sem("hist_turned"), sem("hist_ready")
        v_turned, v_ready, kv_turned, kv_rows_ready = sem("v_turned"), sem("v_ready"), sem("kv_turned"), sem("kv_rows_ready")
        staged, scores_done, scores_read = sem("staged"), sem("scores_done"), sem("scores_read")
        nm_ready, sd_ready, exp_ready = sem("nm_ready"), sem("sd_ready"), sem("exp_ready")
        p_turned, pT_ready, pv_done = sem("p_turned"), sem("pT_ready"), sem("pv_done")
        at_ms_ready, at_r_ready, at_n_ready = sem("at_ms_ready"), sem("at_r_ready"), sem("at_n_ready")
        at_turned, atT_ready = sem("at_turned"), sem("atT_ready")
        u_ready, sq_ready, cms_done, cms_ready, crs_ready = sem("u_ready"), sem("sq_ready"), sem("cms_done"), sem("cms_ready"), sem("crs_ready")
        crs_row_ready, crs_turned, conv_ready = sem("crs_row_ready"), sem("crs_turned"), sem("conv_ready")
        u_turned, u_rows_ready = sem("u_turned"), sem("u_rows_ready")
        cache_arrived, ck_turned, kTs_ready, qbd_ready = sem("cache_arrived"), sem("ck_turned"), sem("kTs_ready"), sem("qbd_ready")
        s_scored, s_shifted, s_exp_ready, s_turned, s_pT_ready = sem("s_scored"), sem("s_shifted"), sem("s_exp_ready"), sem("s_turned"), sem("s_pT_ready")
        s_pv_done, s_ms_ready, s_r_ready, s_n_ready, s_n_turned, s_mixed = sem("s_pv_done"), sem("s_ms_ready"), sem("s_r_ready"), sem("s_n_ready"), sem("s_n_turned"), sem("s_mixed")
        g1_in, x_again, g2_in, mix_hi_ready, mix_staged, out_done, x2_ready = sem("g1_in"), sems("x_again", 2), sem("g2_in"), sem("mix_hi_ready"), sem("mix_staged"), sem("out_done"), sem("x2_ready")
        ms2_ready, eps2_added, rstd2_ready, xn2_ready = sem("ms2_ready"), sem("eps2_added"), sem("rstd2_ready"), sem("xn2_ready")
        xn2_stored = sems("xn2_stored", 2)
        xn2_turned, xn2T_ready, routed, logits_ready = sem("xn2_turned"), sem("xn2T_ready"), sem("routed"), sem("logits_ready")
        r_shifted, r_exp_ready, picks_ready, places_done = sem("r_shifted"), sem("r_exp_ready"), sem("picks_ready"), sem("places_done")
        table_in_ready, table_done, slots_ready = sem("table_in_ready"), sem("table_done"), sem("slots_ready")
        tok_staged, x_gathered, expert_arrived, plan_ready = sem("tok_staged"), sems("x_gathered", 2), sem("expert_arrived"), sem("plan_ready")
        xg_turned, xgT_ready, h_done, silu_ready, hid_ready = sem("xg_turned"), sem("xgT_ready"), sem("h_done"), sem("silu_ready"), sem("hid_ready")
        hid_turned, hidT_ready, y_done = sem("hid_turned"), sem("hidT_ready"), sem("y_done")
        y_left_ready, y_right_ready, y_stored = sem("y_left_ready"), sem("y_right_ready"), sems("y_stored", 2)
        pair_staged, pair_gathered, x3_ready = sem("pair_staged"), sems("pair_gathered", LB), sem("x3_ready")
        ms3_ready, eps3_added, rstd3_ready, out_ready = sem("ms3_ready"), sem("eps3_added"), sem("rstd3_ready"), sem("out_ready")
        out_stored, rows_stored, y_filled = sems("out_stored", LB), sem("rows_stored"), sem("y_filled")
        kvs_stored = sem("kvs_stored")
        dve_step, act_held, sp_held, pool_held = sem("dve_step"), sem("act_held"), sem("sp_held"), sem("pool_held")

        ctx.enter_context(nc.allow_non_contiguous_dma(reason="gains and sinks are a few KB"))
        block = ctx.enter_context(nc.Block())

        def rows_of(t):
            return NS if isinstance(t, int) and t == TILES else P

        def cols(t):
            return slice(t * P, t * P + rows_of(t)) if isinstance(t, int) else ds(t * P, P)

        def arrived_in(m):
            return 16 * (m // WB + 1) + 16 * sum(j <= m for j in range(m % WB, AC, WB))

        def col(t, n=1):
            return slice(t, t + n) if isinstance(t, int) else ds(t, n)

        @block.sync
        def _(sp):
            def load_x(t):
                src = x_smp if t == TILES else xp[cols(t), :]
                sp.dma_start(x_in[t % XB][0:rows_of(t), :], src).then_inc(x_arrived[t % XB], 16)

            def load_w(b, src):
                sp.dma_start(w_raw[b][:, :].rearrange("p (c f) -> p c f", c=KC), src).then_inc(w_arrived[b], 16)

            def load_wq(j):
                for g in range(NKV):
                    sp.dma_start(w_raw[j % WB][:, :].rearrange("p (c f) -> p c f", c=KC)[:, :, g * HD:(g + 1) * HD],
                                 w_in_v[:, :, (4 * g + j) * HD:(4 * g + j + 1) * HD]).then_inc(w_arrived[j % WB], 16)

            load_x(0)
            sp.dma_start(g1, norm1_g[0:1, :].broadcast_to([P, D])).then_inc(g1_in, 16)
            for t in range(1, XB):
                load_x(t)
            load_wq(0)
            for t in range(XB, ALLT):
                sp.wait_ge(x_scaled, t - XB + 1)
                load_x(t)
            for j in range(1, WB):
                load_wq(j)
            sp.dma_start(ga[:, :], attn_out_g[0].rearrange("(c p) -> p c", p=P)).then_inc(const_in, 16)
            sp.dma_start(ga_s[:, :], attn_out_g[0].rearrange("(h d) -> h d", h=NH)).then_inc(const_in, 16)
            for j in range(3):
                sp.dma_start(cwg[:, :, j], conv_w[0, j].rearrange("(c p) -> p c", p=P)).then_inc(const_in, 16)
            sp.dma_start(cwg[:, :, 3], conv_out_g[0].rearrange("(c p) -> p c", p=P)).then_inc(const_in, 16)
            for g in range(NKV):
                dst = sink_in[:, :].rearrange("p (h g j) -> p g h j", h=2, g=NKV)[:, g, :, :]
                src = sinks[0:1, 4 * g:4 * g + 4].rearrange("o (h j) -> o h j", h=2).broadcast_to([P, 2, 2])
                sp.dma_start(dst, src).then_inc(const_in, 16)
            sp.dma_start(sink_in_s[:, :], sinks[0].rearrange("(h o) -> h o", o=1)).then_inc(const_in, 16)
            sp.dma_start(w_r[:, :, 0:NG], w_group[0].rearrange("(p c) n -> p c n", p=P)).then_inc(late_const_in, 16)
            sp.dma_start(w_r[:, :, NG:NR], w_fine[0].rearrange("(p c) n -> p c n", p=P)).then_inc(late_const_in, 16)
            sp.dma_start(b_r[:, 0:NG], b_group[0:1, :].broadcast_to([P, NG])).then_inc(late_const_in, 16)
            sp.dma_start(b_r[:, NG:NR], b_fine[0:1, :].broadcast_to([P, NE])).then_inc(late_const_in, 16)
            sp.dma_start(hist, state_conv[0].rearrange("n j f -> (n j) f")).then_inc(hist_arrived, 16)
            sp.dma_start(ck, cache_k_win[0].rearrange("n t g d -> t n (g d)")).then_inc(cache_arrived, 16)
            sp.dma_start(cv, cache_v_win[0].rearrange("n t g d -> t n (g d)")).then_inc(cache_arrived, 16)
            sp.wait_ge(w_lo_ready, 1)
            load_wq(3)
            for m, off in ((4, OFF_K), (5, OFF_V), (6, OFF_H), (7, OFF_C), (8, OFF_B)):
                sp.wait_ge(w_lo_ready, m - WB + 1)
                load_w(m % WB, w_in_v[:, :, off:off + P])
            sp.wait_ge(const_made, CONST_ALL)
            sp.wait_ge(kv_rows_ready, 3)
            sp.dma_start(new_k_prompt[0, 0].rearrange("t g d -> t (g d)"), kv_rows[:, 0, :]).then_inc(rows_stored, 16)
            sp.dma_start(new_v_prompt[0, 0].rearrange("t g d -> t (g d)"), kv_rows[:, 1, :]).then_inc(rows_stored, 16)
            for j, (new, old) in enumerate(((new_k_sample, cache_k_win), (new_v_sample, cache_v_win))):
                new_v = new[0].rearrange("n t g d -> n t (g d)")
                sp.dma_start(new_v[:, P - 1, :], kvs_rows[:, j, :]).then_inc(kvs_stored, 16)
                sp.dma_start(new_v[:, 0:P - 1, :], old[0].rearrange("n t g d -> n t (g d)")[:, 1:P, :]).then_inc(rows_stored, 16)
            sp.dma_start(new_conv_sample[0, :, 0, :], state_conv[0, :, 1, :]).then_inc(rows_stored, 16)
            zeros = v_tok[:, 0, :].unsqueeze(1).broadcast_to([P, KC, P])
            with sp.Fori(0, CC - 1) as i:
                for x, off in enumerate((OFF_H, OFF_C, OFF_B)):
                    sp.wait_ge(w_lo_ready, i * 3 + (QKV + 1 + x))
                    load_w(x, w_in_v[:, :, ds(i * P + (off + P), P)])
                for x in range(FILL // 4):
                    sp.dma_start(y_d[ds((i * (FILL // 4) + (LEAST_TILES + x)) * P, P), :].rearrange("p (c f) -> p c f", c=KC), zeros).then_inc(y_filled, 16)
            for x in range(FILL // 4):
                at = (SLOT_TILES - FILL // 4 + x) * P
                sp.dma_start(y_d[at:at + P, :].rearrange("p (c f) -> p c f", c=KC), zeros).then_inc(y_filled, 16)
            for c in range(KC):
                sp.wait_ge(w_lo_ready, CHUNKS + c - WB + 1)
                sp.dma_start(w_raw[c % WB][:, :], w_out[0, c * P:(c + 1) * P, :]).then_inc(w_arrived[c % WB], 16)
            sp.wait_ge(u_rows_ready, 1)
            sp.dma_start(new_conv_prompt[0, 0], u_rows[0:2, :]).then_inc(rows_stored, 16)
            sp.dma_start(new_conv_sample[0, :, 1, :], u_rows[2:2 + NS, :]).then_inc(rows_stored, 16)
            sp.wait_ge(sq_ready, CC)
            x_tiles = xp.rearrange("(t p) d -> p t d", p=P)
            sp.dma_start(x2[:, 0:2, :], x_tiles[:, 0:2, :]).then_inc(x_again[0], 16)
            sp.wait_ge(y_filled, 16 * FILL)
            sp.wait_ge(conv_ready, 2 * CC)
            sp.wait_ge(atT_ready, TILES)
            sp.dma_start(g2[:, :], norm2_g[0:1, :].broadcast_to([P, D])).then_inc(g2_in, 16)
            sp.dma_start(x2[:, 2:TILES, :], x_tiles[:, 2:TILES, :]).then_inc(x_again[1], 16)
            sp.dma_start(x2[0:NS, TILES, :], x_smp).then_inc(x_again[1], 16)
            sp.dma_start(gf[:, :], final_g.rearrange("(o d) -> o d", o=1).broadcast_to([P, D])).then_inc(x_again[1], 16)
            def store_xn2(t, k):
                sp.wait_ge(xn2_ready, t + 1)
                sp.dma_start(xn2_d[cols(t), :], xn2[k][0:rows_of(t), :]).then_inc(xn2_stored[k], 16)
            with sp.Fori(0, TILES // 2) as i:
                for k in range(2):
                    store_xn2(i * 2 + k, k)
            store_xn2(TILES, 0)
            sp.wait_ge(plan_ready, 1)
            sp.wait_ge(out_done, ALLT)
            experts_used = sp.value_load(plan[0:1, PL_EXPERTS:PL_EXPERTS + 1], min_val=2, max_val=NE)

            def load_expert(j, b):
                if not isinstance(j, int) or j >= EB:
                    freed = sp.value_load(plan[0:1, ds(j + (PL_FREED - EB), 1)], min_val=2, max_val=2 * SLOT_TILES)
                    sp.wait_ge(y_done, freed)
                    sp.sem_inc(sp_held, 1)
                if not isinstance(j, int) or j >= 1:
                    sp.wait_ge(expert_arrived, j * 48)
                    sp.sem_inc(sp_held, 1)
                e = sp.value_load(plan[0:1, ds(j + PL_EXPERT, 1)], min_val=0, max_val=NE - 1)
                for v in range(3):
                    sp.dma_start(w_flat[:, ew_at[b] + v * KC * FE:ew_at[b] + (v + 1) * KC * FE],
                                 expert_parts[v][ds(e, 1)].rearrange("o p x -> p (o x)")).then_inc(expert_arrived, 16)

            load_expert(0, 0)
            load_expert(1, 1)
            with sp.If(experts_used > 2):
                load_expert(2, 2)
            with sp.Fori(1, NE // EB) as i:
                for b in range(EB):
                    j = i * EB + b
                    with sp.If(j < experts_used):
                        load_expert(j, b)
            with sp.If(experts_used > NE - 1):
                load_expert(NE - 1, (NE - 1) % EB)
            def store_out(t, k):
                n = rows_of(t)
                dst = y_sample[:, 0, :] if n == NS else y_prompt[0][cols(t), :]
                sp.wait_ge(out_ready, t + 1)
                sp.dma_start(dst, out_rows[k][0:n, :]).then_inc(out_stored[k], 16)
            with sp.Fori(0, ALLT // LB - 1) as i:
                for k in range(LB):
                    store_out(i * LB + k, k)
            for k in range(LB):
                store_out(ALLT - LB + k, k)
            for k in range(LB):
                sp.wait_ge(out_stored[k], 16 * (ALLT // LB))
            sp.wait_ge(rows_stored, 16 * 7)

        @block.gpsimd
        def _(pool):
            made = Steps(pool, const_made)

            def select(out, in_, pattern, base, cm, fill, op=ALU.is_ge):
                made.then(pool.affine_select(out=out, in_=in_, compare_op=op, fill=fill, base=base,
                                             pattern=pattern, channel_multiplier=cm))

            def iota(out, pattern, base, cm):
                made.then(pool.iota(out, pattern=pattern, base=base, channel_multiplier=cm,
                                    allow_small_or_imprecise_dtypes=True))

            made.then(pool.memset(ident[:, :], 0.0))
            select(ident[:, :], ident[:, :], [[-1, P]], 0, 1, 1.0, ALU.not_equal)
            made.then(pool.memset(epsilon[:, :], EPS))
            made.then(pool.memset(exponent[:, :], -0.5))

            def rsqrt(n, t, ready, added, out_ready_, rows):
                pool.wait_ge(ready, t + 1)
                pool.sem_inc(pool_held, 1)
                pool.tensor_tensor(ms[n][0:rows, col(t)], ms[n][0:rows, col(t)], epsilon[0:rows, :], ALU.add).then_inc(added, 1)
                pool.wait_ge(added, t + 1)
                pool.sem_inc(pool_held, 1)
                pool.tensor_tensor(rstd[n][0:rows, col(t)], ms[n][0:rows, col(t)], exponent[0:rows, 0:1], ALU.pow).then_inc(out_ready_, 1)

            with pool.Fori(0, TILES) as t:
                rsqrt(0, t, ms1_ready, eps1_added, rstd1_ready, P)
            rsqrt(0, TILES, ms1_ready, eps1_added, rstd1_ready, NS)

            made.then(pool.memset(ones[:, :], 1.0))
            select(earlier[:, :], ones[:, :], [[1, P]], -1, -1, 0.0)
            made.then(pool.memset(group_mean[:, :], 1.0 / HD))
            select(group_mean[:, :], group_mean[:, :], [[-HD, 2]], 0, 1, 0.0)
            select(group_mean[:, :], group_mean[:, :], [[HD, 2]], HD - 1, -1, 0.0)
            made.then(pool.memset(uT[:, 0:2], 0.0))
            made.then(pool.memset(v_tok[:, 0, :], 0.0))
            made.then(pool.memset(qbd[:, :, :], 0.0))
            made.then(pool.memset(band_mask[:, :, :], 0.0))
            select(band_mask[:, :, :], band_mask[:, :, :], [[0, 2], [1, 2 * P]], 0, -1, MASKED)
            select(band_mask[:, :, :], band_mask[:, :, :], [[0, 2], [-1, 2 * P]], P, 1, MASKED)
            made.then(pool.memset(band_mask[:, 0, 0:P], MASKED))
            made.then(pool.memset(half_mask[:, :], 1.0))
            select(half_mask[:, :].rearrange("h (g d) -> h g d", g=NKV), half_mask[:, :].rearrange("h (g d) -> h g d", g=NKV),
                   [[-4, NKV], [0, HD]], 0, 1, 0.0)
            select(half_mask[:, :].rearrange("h (g d) -> h g d", g=NKV), half_mask[:, :].rearrange("h (g d) -> h g d", g=NKV),
                   [[4, NKV], [0, HD]], 3, -1, 0.0)
            iota(rev4[:, :, :], [[0, ALLT], [-1, EG]], EG, 0)
            made.then(pool.memset(valid[:, :], 1.0))
            select(valid[:, :], valid[:, :], [[-P, ALLT]], NT - 1, -1, 0.0)
            made.then(pool.memset(nowhere[:, :, :], 0.0))
            select(nowhere[:, :, :], nowhere[:, :, :], [[0, 2], [-P, ALLT]], NT - 1, -1, NOWHERE)
            iota(iota_row[:, :], [[1, P]], 0, 0)
            iota(iota_p[:, :], [[0, 1]], 0, 1)
            iota(steps128[:, :], [[P, ALLT]], 0, 0)
            iota(token_no[:, :], [[P, ALLT]], 0, 1)
            assert made.n == CONST_ALL, made.n

            def at_power(t):
                pool.wait_ge(at_ms_ready, t + 1)
                pool.tensor_tensor(at_r[:, :], at_ms[:, :], exponent[:, 0:NH], ALU.pow).then_inc(at_r_ready, 1)

            def conv_power(i):
                pool.wait_ge(cms_ready, i + 1)
                pool.tensor_tensor(crs[:, :], cms[:, :], exponent[:, :], ALU.pow).then_inc(crs_ready, 1)

            pool.wait_ge(s_ms_ready, 1)
            pool.tensor_tensor(s_r[:, :], s_ms[:, :], exponent[0:NH, 0:NS], ALU.pow).then_inc(s_r_ready, 1)
            with pool.Fori(0, CC) as i:
                at_power(i * 2)
                conv_power(i)
                at_power(i * 2 + 1)
            with pool.Fori(0, TILES) as t:
                rsqrt(1, t, ms2_ready, eps2_added, rstd2_ready, P)
            rsqrt(1, TILES, ms2_ready, eps2_added, rstd2_ready, NS)

            def at_row(idx):
                return bass.IndirectOffsetOnAxis(ap=idx, axis=0)

            def gather_x(u, k):
                if not isinstance(u, int) or u >= 2:
                    pool.wait_ge(xg_turned, u - 1)
                    pool.sem_inc(pool_held, 1)
                pool.tensor_copy(tok_i[k][:, :], slot_tok[:, col(u)]).then_inc(tok_staged, 1)
                pool.wait_ge(tok_staged, u + 1)
                pool.sem_inc(pool_held, 1)
                pool.indirect_dma_start(xg[k], None, xn2_d, at_row(tok_i[k][:, :])).then_inc(x_gathered[k], 16)

            pool.wait_ge(plan_ready, 1)
            tiles_used = pool.value_load(plan[0:1, PL_TILES:PL_TILES + 1], min_val=LEAST_TILES, max_val=SLOT_TILES)
            pool.wait_ge(slots_ready, 1)
            pool.wait_ge(xn2_stored[0], 16 * (TILES // 2 + 1))
            pool.wait_ge(xn2_stored[1], 16 * (TILES // 2))
            for u in range(2):
                gather_x(u, u)
            with pool.Fori(0, LEAST_TILES // 2) as i:
                for k in range(2):
                    gather_x(i * 2 + (k + 2), k)
            with pool.Fori(LEAST_TILES // 2, SLOT_TILES // 2) as i:
                for k in range(2):
                    with pool.If(i * 2 + k < tiles_used):
                        gather_x(i * 2 + (k + 2), k)

            def gather_pair(t, k, rows):
                for j in range(2):
                    pool.tensor_copy(pair_i[k][j][:, :], slot_i[:, j, col(t)]).then_inc(pair_staged, 1)
                pool.wait_ge(pair_staged, t * 2 + 2)
                pool.sem_inc(pool_held, 1)
                for dst, idx in zip(pair_rows[k], pair_i[k]):
                    pool.indirect_dma_start(dst[0:rows, :], None, y_d, at_row(idx[0:rows, :])).then_inc(pair_gathered[k], 16)

            def rstd3(t, rows=P):
                rsqrt(2, t, ms3_ready, eps3_added, rstd3_ready, rows)

            pool.wait_ge(y_filled, 16 * FILL)
            for k in range(2):
                stored = pool.value_load(plan[0:1, PL_STORED + k:PL_STORED + k + 1], min_val=8 * LEAST_TILES, max_val=8 * SLOT_TILES)
                pool.wait_ge(y_stored[k], stored)
                pool.sem_inc(pool_held, 1)
            for k in range(LB):
                gather_pair(k, k, P)
            with pool.Fori(0, ALLT // LB - 2) as i:
                for k in range(LB):
                    rstd3(i * LB + k)
                    gather_pair(i * LB + (k + LB), k, P)
            for k in range(LB):
                t = ALLT - 2 * LB + k
                rstd3(t)
                gather_pair(t + LB, k, rows_of(t + LB))
            for t in range(ALLT - LB, ALLT):
                rstd3(t, rows_of(t))

        @block.scalar
        def _(act):
            def squares(n, t, src, out, ready, rows):
                if not isinstance(t, int) or t >= 1:
                    act.wait_ge(ready, t)
                    act.sem_inc(act_held, 1)
                act.activation(out[0:rows, :], src, ACT.Square, scale=D ** -0.5,
                               accum_out=ms[n][0:rows, col(t)]).then_inc(ready, 1)

            def x_hi(t):
                n = rows_of(t)
                k = t % 2
                act.wait_ge(x_turned, t + 1)
                act.copy(xTh[:, :, cols(t)], bank[:, 2 * k:2 * k + 2, :].rearrange("p b (c t) -> p (b c) t", t=P)[:, :, 0:n]).then_inc(x_hi_ready, 1)

            def w_hi(m, b, arrived):
                act.wait_ge(w_arrived[b], arrived)
                if not isinstance(m, int) or m >= WB:
                    act.wait_ge(run_done, m * NB - (WB - 1) * NB)
                act.copy(wh[b][:, :, :], w_raw[b][:, :].rearrange("p (c f) -> p c f", c=KC)).then_inc(w_hi_ready, 1)

            for t in range(ALLT):
                act.wait_ge(x_arrived[t % XB], 16 * (t // XB + 1))
                squares(0, t, x_in[t % XB][0:rows_of(t), :], squared1, ms1_ready, rows_of(t))
                if t >= 1:
                    x_hi(t - 1)
            w_hi(0, 0, 32)
            x_hi(TILES)

            def projection_out(m, dst, runs=range(NB)):
                for n in runs:
                    act.wait_ge(run_done, m * NB + (n + 1))
                    act.copy(dst[:, n * RUN:(n + 1) * RUN], bank[:, 5 + n, 0:RUN]).then_inc(run_out, 1)

            qkv_out = [mixedT[:, j, :] for j in range(AC)] + [kT[:, :], vT[:, :]]
            act.wait_ge(ms1_ready, ALLT)
            for m in range(QKV):
                w_hi(m + 1, (m + 1) % WB, arrived_in(m + 1))
                projection_out(m, qkv_out[m])
                if m == 0:
                    act.wait_ge(ck_turned, 1)
                    act.copy(kTs, bank[:, 0:2, :].rearrange("p b (n t) -> p (b n) t", t=P)).then_inc(kTs_ready, 1)

            def exps(t, k):
                act.wait_ge(nm_ready, t + 1)
                for h in range(NH):
                    act.activation(prob[k][:, h, :], prob[k][:, h, :], ACT.Exp, bias=nm[k][:, h:h + 1],
                                   accum_out=den[k][:, h:h + 1])
                act.wait_ge(sd_ready, t + 1)
                act.activation(es[k][:, :], sd[k][:, :], ACT.Exp).then_inc(exp_ready, 1)

            def probs_out(t, k):
                if not isinstance(t, int) or t >= 1:
                    act.wait_ge(pv_done, t)
                for q in range(4):
                    act.wait_ge(p_turned, t * 4 + (q + 1))
                    act.copy(pTs[:, 2 * q:2 * q + 2, :, :].rearrange("p a b c -> p (a b c)"), bank[:, 2 + q % 2, :]).then_inc(pT_ready, 1)

            w_hi(7, 1, arrived_in(7))
            act.wait_ge(hist_turned, 1)
            projection_out(6, hcb[:, 0, :])
            act.wait_ge(s_shifted, 1)
            act.activation(s_p, s_sc, ACT.Exp).then_inc(s_exp_ready, 1)
            act.activation(s_es[:, :], s_es[:, :], ACT.Exp).then_inc(s_exp_ready, 1)
            w_hi(8, 2, arrived_in(8))
            projection_out(7, hcb[:, 1, :])
            w_hi(9, 0, arrived_in(9))
            projection_out(8, hcb[:, 2, :])
            act.wait_ge(s_mixed, 2)
            exps(0, 0)

            def pair(i):
                t0 = i * 2
                m = i * 3 + (QKV + 3)
                probs_out(t0, 0)
                w_hi(m + 1, 1, i * 16 + 80)
                act.wait_ge(u_ready, i + 1)
                projection_out(m, hcb[:, 0, :])
                exps(t0 + 1, 1)
                w_hi(m + 2, 2, i * 16 + 80)
                projection_out(m + 1, hcb[:, 1, :])
                probs_out(t0 + 1, 1)
                act.wait_ge(sq_ready, i + 1)
                projection_out(m + 2, hcb[:, 2, :], range(1))
                exps(t0 + 2, 0)
                if not isinstance(i, int):
                    w_hi(m + 3, 0, i * 16 + 112)
                projection_out(m + 2, hcb[:, 2, :], range(1, NB))

            def w_out_hi(lo, hi):
                act.wait_ge(run_done, NB * CHUNKS)
                for c in range(lo, hi):
                    act.wait_ge(w_arrived[c % WB], arrived_in(CHUNKS + c))
                    act.copy(w_oh[:, c, :], w_raw[c % WB][:, :]).then_inc(w_hi_ready, 1)

            with act.Fori(0, CC - 2) as i:
                pair(i)
            pair(CC - 2)
            probs_out(TILES - 2, 0)
            exps(TILES - 1, 1)
            w_out_hi(0, 3)
            probs_out(TILES - 1, 1)
            w_out_hi(3, KC)

            def stage(t, k):
                n = rows_of(t)
                if not isinstance(t, int) or t >= 2:
                    act.wait_ge(out_done, t - 1)
                act.sem_inc(act_held, 1)
                act.copy(mix_h[k][:, :, 0:n], mixedT[:, :, cols(t)]).then_inc(mix_hi_ready, 1)

            def norm2(t, k):
                n = rows_of(t)
                act.wait_ge(x2_ready, t + 1)
                squares(1, t, x2[0:n, t, :] if isinstance(t, int) else x2[:, ds(t, 1), :].rearrange("p o d -> p (o d)"), junk, ms2_ready, n)
                if not isinstance(t, int) or t + 2 <= TILES:
                    stage(t + 2, k)
                act.wait_ge(xn2_turned, t + 1)
                act.copy(xn2T[:, :, 0:n], bank[:, 4:6, :].rearrange("p b (c t) -> p (b c) t", t=P)[:, :, 0:n]).then_inc(xn2T_ready, 1)

            act.wait_ge(conv_ready, 2 * CC)
            act.wait_ge(atT_ready, TILES)
            stage(0, 0)
            stage(1, 1)
            for t in range(2):
                norm2(t, t % 2)
            with act.Fori(1, TILES // 2 - 1) as i:
                for k in range(2):
                    norm2(i * 2 + k, k)
            for t in range(TILES - 2, ALLT):
                norm2(t, t % 2)

            act.wait_ge(r_shifted, 2)
            act.activation(r4[4][:, :, :], r4[4][:, :, :], ACT.Exp).then_inc(r_exp_ready, 1)
            act.activation(r9[5][:, :], r9[5][:, :], ACT.Exp).then_inc(r_exp_ready, 1)

            def x_out(u, k):
                act.wait_ge(xg_turned, u + 1)
                act.copy(xgT[k], bank[:, 0:2, :].rearrange("p b (c t) -> p (b c) t", t=P)).then_inc(xgT_ready, 1)

            def silus(u, k):
                act.wait_ge(h_done, u + 1)
                act.activation(silu[k], bank[:, 2 + k, 0:FE], ACT.Silu).then_inc(silu_ready, 1)

            def hid_out(u, k):
                act.wait_ge(hid_turned, u + 1)
                act.copy(hidT[k], bank[:, 4, 0:FE].rearrange("p (c t) -> p c t", c=FC)).then_inc(hidT_ready, 1)

            def y_out(u, k):
                if not isinstance(u, int) or u >= 2:
                    act.wait_ge(y_stored[k], u // 2 * 16 if isinstance(u, int) else (u - k) * 8)
                act.wait_ge(y_done, u * 2 + 1)
                act.copy(y_sb[k][:, 0:512], bank[:, 5, :]).then_inc(y_left_ready, 1)
                act.wait_ge(y_left_ready, u + 1)
                act.wait_ge(y_right_ready, u + 1)
                act.dma_start(y_d[cols(u), :], y_sb[k]).then_inc(y_stored[k], 16)

            def tile(u, k):
                hid_out(u, k)
                silus(u + 1, 1 - k)
                x_out(u + 2, k)
                y_out(u, k)

            act.wait_ge(plan_ready, 1)
            tiles_used = act.value_load(plan[0:1, PL_TILES:PL_TILES + 1], min_val=LEAST_TILES, max_val=SLOT_TILES)
            x_out(0, 0)
            silus(0, 0)
            x_out(1, 1)
            tile(0, 0)
            tile(1, 1)
            with act.Fori(1, LEAST_TILES // 2) as i:
                for k in range(2):
                    tile(i * 2 + k, k)
            with act.Fori(LEAST_TILES // 2, SLOT_TILES // 2) as i:
                for k in range(2):
                    with act.If(i * 2 + k < tiles_used):
                        tile(i * 2 + k, k)

            def norm3(t):
                n = rows_of(t)
                act.wait_ge(x3_ready, t + 1)
                squares(2, t, x2[0:n, t, :] if isinstance(t, int) else x2[:, ds(t, 1), :].rearrange("p o d -> p (o d)"), junk, ms3_ready, n)

            norm3(0)
            with act.Fori(1, TILES) as t:
                norm3(t)
            norm3(TILES)

        @block.tensor
        def _(pe):
            def late(t, least=1):
                return not isinstance(t, int) or t >= least

            def turn_x(t):
                n = rows_of(t)
                k = t % 2
                pe.wait_ge(x_scaled, t + 1)
                if t >= 2:
                    pe.wait_ge(xnT_ready, t - 1)
                for c in range(KC):
                    mm = pe.transpose(bank[:, 2 * k + c // 4, (c % 4) * P:(c % 4) * P + n], x_sc[k][0:n, c * P:(c + 1) * P], ident[0:n, 0:n])
                mm.then_inc(x_turned, 1)

            def product(out, hl, rhs_h, rhs_l, n):
                passes = [(hl[1], rhs_h), (hl[0], rhs_l), (hl[0], rhs_h)]
                for c in range(KC):
                    for x, (lhs, rhs) in enumerate(passes):
                        mm = pe.matmul(out, lhs[:, c, 0:n], rhs(c), start=c == 0 and x == 0, stop=c == KC - 1 and x == 2)
                return mm

            def project_run(m, b, n):
                if late(m):
                    pe.wait_ge(run_out, m * NB + (n + 1 - NB))
                at = slice(n * RUN, (n + 1) * RUN)
                product(bank[:, 5 + n, 0:RUN], (wh[b], wl[b]), lambda c: xTh[:, c, at], lambda c: xTl[:, c, at], P).then_inc(run_done, 1)

            def project(m, b):
                pe.wait_ge(w_lo_ready, m + 1)
                for n in range(NB):
                    project_run(m, b, n)

            pe.wait_ge(const_made, 2)
            for t in range(ALLT):
                turn_x(t)
            pe.wait_ge(hist_arrived, 16)
            for c in range(CC):
                mm = pe.transpose(bank[:, 4, c * 2 * NS:(c + 1) * 2 * NS], hist[:, c * P:(c + 1) * P], ident[0:2 * NS, 0:2 * NS])
            mm.then_inc(hist_turned, 1)
            pe.wait_ge(xnT_ready, ALLT)
            project(0, 0)
            pe.wait_ge(cache_arrived, 32)
            for n in range(NS):
                mm = pe.transpose(bank[:, n // 4, (n % 4) * P:(n % 4 + 1) * P], ck[:, n, :], ident[:, :])
            mm.then_inc(ck_turned, 1)
            for m in range(1, QKV):
                project(m, m % WB)

            pe.wait_ge(run_out, NB * QKV)
            pe.wait_ge(kTs_ready, 1)
            for b in range(TILES):
                mm = pe.transpose(bank[:, b // 4, (b % 4) * P:(b % 4 + 1) * P], vT[:, b * P:(b + 1) * P], ident[:, :])
            mm.then_inc(v_turned, 1)
            pe.wait_ge(hist_ready, 1)
            pe.transpose(bank[:, 4, 0:P], kT[:, SEQ - P:SEQ], ident[:, :])
            for j, src in enumerate((kT, vT)):
                mm = pe.transpose(bank[0:NS, 4, (1 + j) * P:(2 + j) * P], src[:, SEQ:NT], ident[:, :])
            mm.then_inc(kv_turned, 1)

            project(6, 0)
            pe.wait_ge(qbd_ready, 2)
            pe.wait_ge(kv_rows_ready, 3)
            for n in range(NS):
                pe.matmul(bank[0:NH, 2 + n // 4, (n % 4) * P:(n % 4 + 1) * P], qbd[:, n, :], kTs[:, n, :], start=True, stop=True)
                mm = pe.matmul(bank[0:NH, 4, n:n + 1], qbd[:, n, :], kT[:, SEQ + n:SEQ + n + 1], start=True, stop=True)
            mm.then_inc(s_scored, 1)
            project(7, 1)
            pe.wait_ge(s_exp_ready, 2)
            pe.wait_ge(v_ready, 1)
            for n in range(NS):
                pe.transpose(bank[:, 0, n * NH:(n + 1) * NH], s_p[:, n, 0:P], ident[0:NH, 0:NH])
            pe.transpose(bank[0:NS, 1, 0:NH], s_p[:, :, P], ident[0:NH, 0:NH]).then_inc(s_turned, 1)
            pe.wait_ge(w_lo_ready, 9)
            project_run(8, 2, 0)
            pe.wait_ge(s_pT_ready, 2)
            for n in range(NS):
                out = bank[0:NH, 2 + n // 4, (n % 4) * P:(n % 4 + 1) * P]
                pe.matmul(out, s_pT[:, n, :], cv[:, n, :], start=True, stop=False)
                mm = pe.matmul(out, s_z[:, n, :], kvs_rows[:, 1, :], start=False, stop=True)
            mm.then_inc(s_pv_done, 1)
            project_run(8, 2, 1)
            pe.wait_ge(s_n_ready, 1)
            for n in range(NS):
                mm = pe.transpose(bank[0:HD, 4, n * NH:(n + 1) * NH], s_n[:, n, :], ident[0:NH, 0:NH])
            mm.then_inc(s_n_turned, 1)

            def scores(t):
                pe.wait_ge(staged, t * 2 + 2)
                if late(t):
                    pe.wait_ge(scores_read, t * 2)
                for half in range(2):
                    for j in range(2):
                        for g in range(NKV):
                            mm = pe.matmul(bank[:, 2 * half + g, j * 2 * P:(j + 1) * 2 * P], qs[g * HD:(g + 1) * HD, 2 * half + j, :],
                                           kb[g * HD:(g + 1) * HD, :], start=True, stop=True)
                    mm.then_inc(scores_done, 1)

            def weigh(t, k):
                pe.wait_ge(exp_ready, t + 1)
                for q in range(4):
                    if late(t) or q >= 2:
                        pe.wait_ge(pT_ready, t * 4 + (q - 1))
                    for x in range(2):
                        for c in range(2):
                            mm = pe.transpose(bank[:, 2 + q % 2, (2 * x + c) * P:(2 * x + c + 1) * P],
                                              prob[k][:, 2 * q + x, c * P:(c + 1) * P], ident[:, :])
                    mm.then_inc(p_turned, 1)
                if late(t):
                    pe.wait_ge(atT_ready, t)
                pe.wait_ge(pT_ready, t * 4 + 4)
                for h in range(NH):
                    g = h // 2 % 2
                    for c in range(2):
                        v = v_tok[:, t + c, g * HD:(g + 1) * HD] if isinstance(t, int) else \
                            v_tok[:, :, :].rearrange("p b f -> p (b f)")[:, ds(t * P + (c * P + g * HD), HD)]
                        mm = pe.matmul(bank[:, 4, h * HD:(h + 1) * HD], pTs[:, h, c, :], v, start=c == 0, stop=c == 1)
                mm.then_inc(pv_done, 1)

            def turn_attention(t):
                pe.wait_ge(at_n_ready, t + 1)
                for c in range(AC):
                    first_h = (c % 2) * 4 + (c // 2) * 2
                    mm = pe.transpose(bank[:, 4, c * P:(c + 1) * P], at_n[:, first_h * HD:first_h * HD + P], ident[:, :])
                mm.then_inc(at_turned, 1)

            last_tokens = NT - P

            def conv_means(i):
                pe.wait_ge(sq_ready, i + 1)
                for t in range(ALLT):
                    at = t * P if t < TILES else last_tokens
                    mm = pe.matmul(bank[:, 2, 2 * t:2 * t + 2], sqT[:, at:at + P], group_mean[:, :], start=True, stop=True)
                mm.then_inc(cms_done, 1)

            def conv_scales(i, t1):
                pe.wait_ge(crs_row_ready, i + 1)
                pe.wait_ge(scores_read, t1 * 2 + 2)
                for t in range(ALLT):
                    out = bank[:, t // 4, (t % 4) * P:(t % 4 + 1) * P] if t < TILES else bank[:, 2, P:2 * P]
                    mm = pe.transpose(out, crs_row[:, t * P:(t + 1) * P], ident[:, :])
                mm.then_inc(crs_turned, 1)

            def pair(i, last=False):
                t0 = i * 2
                m = i * 3 + (QKV + 3)
                weigh(t0, 0)
                scores(t0 + 1)
                if not last:
                    project(m, 0)
                pe.wait_ge(scores_read, t0 * 2 + 4)
                conv_means(i)
                if not last:
                    pe.wait_ge(w_lo_ready, m + 2)
                    project_run(m + 1, 1, 0)
                    project_run(m + 1, 1, 1)
                turn_attention(t0)
                conv_scales(i, t0 + 1)
                if not last:
                    project_run(m + 1, 1, 2)
                pe.wait_ge(conv_ready, i * 2 + 2)
                weigh(t0 + 1, 1)
                if not last:
                    scores(t0 + 2)
                    project(m + 2, 2)
                turn_attention(t0 + 1)

            pe.wait_ge(const_made, CONST_ALL)
            scores(0)
            project_run(8, 2, 2)
            pe.wait_ge(s_mixed, 2)
            pair(0)
            with pe.Fori(1, CC - 1) as i:
                pair(i)
            pair(CC - 1, True)
            for c in range(CC):
                mm = pe.transpose(bank[0:2 + NS, 3, c * P:(c + 1) * P], u_last[:, c, :], ident[:, :])
            mm.then_inc(u_turned, 1)

            def project_out(t, k, halves=range(2)):
                n = rows_of(t)
                if 0 in halves:
                    pe.wait_ge(mix_staged, t + 1)
                    if late(t, 2):
                        pe.wait_ge(x2_ready, t - 1)
                for half in halves:
                    at = slice(half * 512, (half + 1) * 512)
                    mm = product(bank[0:n, 2 * k + half, :], (mix_h[k], mix_l[k]), lambda c: w_oh[:, c, at], lambda c: w_ol[:, c, at], n)
                if 1 in halves:
                    mm.then_inc(out_done, 1)

            def turn_xn2(t, k):
                n = rows_of(t)
                pe.wait_ge(xn2_ready, t + 1)
                for c in range(KC):
                    mm = pe.transpose(bank[:, 4 + c // 4, (c % 4) * P:(c % 4) * P + n], xn2[k][0:n, c * P:(c + 1) * P], ident[0:n, 0:n])
                mm.then_inc(xn2_turned, 1)

            def route(t):
                n = rows_of(t)
                pe.wait_ge(xn2T_ready, t + 1)
                if late(t):
                    pe.wait_ge(logits_ready, t)
                for c in range(KC):
                    mm = pe.matmul(bank[0:n, 7, 0:NR], xn2T[:, c, 0:n], w_r[:, c, :], start=c == 0, stop=c == KC - 1)
                mm.then_inc(routed, 1)

            pe.wait_ge(w_lo_ready, CHUNKS + KC)
            pe.wait_ge(u_rows_ready, 1)
            pe.wait_ge(late_const_in, 16 * 4)
            def tiles_out(t, k):
                project_out(t + 1, 1 - k, range(1))
                turn_xn2(t, k)
                project_out(t + 1, 1 - k, range(1, 2))
                route(t)

            project_out(0, 0)
            tiles_out(0, 0)
            tiles_out(1, 1)
            with pe.Fori(1, TILES // 2 - 1) as i:
                for k in range(2):
                    tiles_out(i * 2 + k, k)
            for t in range(TILES - 2, TILES):
                tiles_out(t, t % 2)
            turn_xn2(TILES, 0)
            route(TILES)

            pe.wait_ge(picks_ready, 1)
            pe.matmul(bank[:, 0, 0:ALLT * NE], earlier[:, :], both.rearrange("p t e -> p (t e)"), start=True, stop=False)
            pe.matmul(bank[:, 0, 0:ALLT * NE], ones[:, :], before[:, 0:ALLT, :].rearrange("p t e -> p (t e)"), start=False, stop=True)
            pe.matmul(bank[:, 1, 0:NE], ones[:, :], before[:, ALLT, :], start=True, stop=True).then_inc(places_done, 1)
            pe.wait_ge(table_in_ready, 1)
            for j in range(2 * ALLT):
                mm = pe.matmul(bank[:, 2, 0:2 * PLANNED], row_hot[:, j, :], payload[:, j, :, :].rearrange("p v u -> p (v u)"),
                               start=j == 0, stop=j == 2 * ALLT - 1)
            mm.then_inc(table_done, 1)

            def turn_tokens(u, k, arrived):
                pe.wait_ge(x_gathered[k], arrived)
                if late(u):
                    pe.wait_ge(xgT_ready, u)
                for c in range(KC):
                    mm = pe.transpose(bank[:, c // 4, (c % 4) * P:(c % 4 + 1) * P], xg[k][:, c * P:(c + 1) * P], ident[:, :])
                mm.then_inc(xg_turned, 1)

            def planned(place, u, lo, hi):
                return pe.value_load(plan[0:1, ds(u + place, 1)], min_val=lo, max_val=hi)

            def gate_and_up(u, k):
                buf = planned(PL_BUF, u, 0, ew_at[-1])
                arrived = planned(PL_ARRIVED, u, 48, 48 * NE)
                pe.wait_ge(xgT_ready, u + 1)
                if late(u, 2):
                    pe.wait_ge(hid_ready, u - 1)
                pe.wait_ge(expert_arrived, arrived)
                for c in range(KC):
                    w = w_flat[:, ds(buf, EW)].rearrange("p (v c f) -> p v c f", v=3, c=KC)[:, 0:2, c, :]
                    mm = pe.matmul(bank[:, 2 + k, :].rearrange("p (v f) -> p v f", v=2), xgT[k][:, c, :], w, start=c == 0, stop=c == KC - 1)
                mm.then_inc(h_done, 1)

            def turn_hidden(u, k):
                pe.wait_ge(hid_ready, u + 1)
                if late(u):
                    pe.wait_ge(hidT_ready, u)
                for c in range(FC):
                    mm = pe.transpose(bank[:, 4, c * P:(c + 1) * P], hid[k][:, c, :], ident[:, :])
                mm.then_inc(hid_turned, 1)

            def down(u, k):
                buf = planned(PL_BUF, u, 0, ew_at[-1])
                pe.wait_ge(hidT_ready, u + 1)
                for half in range(2):
                    if late(u):
                        pe.wait_ge((y_left_ready, y_right_ready)[half], u)
                    for c in range(FC):
                        w = w_flat[:, ds(buf + (2 * KC * FE + c * D + half * 512), 512)]
                        mm = pe.matmul(bank[:, 5 + half, :], hidT[k][:, c, :], w, start=c == 0, stop=c == FC - 1)
                    mm.then_inc(y_done, 1)

            def tile(u, i, k):
                turn_hidden(u, k)
                gate_and_up(u + 1, 1 - k)
                turn_tokens(u + 2, k, i * 16 + 32)
                down(u, k)

            pe.wait_ge(plan_ready, 1)
            tiles_used = pe.value_load(plan[0:1, PL_TILES:PL_TILES + 1], min_val=LEAST_TILES, max_val=SLOT_TILES)
            turn_tokens(0, 0, 16)
            gate_and_up(0, 0)
            turn_tokens(1, 1, 16)
            tile(0, 0, 0)
            tile(1, 0, 1)
            with pe.Fori(1, LEAST_TILES // 2) as i:
                for k in range(2):
                    tile(i * 2 + k, i, k)
            with pe.Fori(LEAST_TILES // 2, SLOT_TILES // 2) as i:
                for k in range(2):
                    with pe.If(i * 2 + k < tiles_used):
                        tile(i * 2 + k, i, k)

        @block.vector
        def _(dve):
            st = Steps(dve, dve_step)

            def bc(ap, n):
                return ap.unsqueeze(2).broadcast_to([ap.shape[0], ap.shape[1], n])

            def late(t, least=1):
                return not isinstance(t, int) or t >= least

            def scale_x(t):
                n = rows_of(t)
                if t >= 2:
                    dve.wait_ge(x_turned, t - 1)
                dve.wait_ge(rstd1_ready, t + 1)
                dve.scalar_tensor_tensor(out=x_sc[t % 2][0:n, :], in0=x_in[t % XB][0:n, :], scalar=rstd[0][0:n, col(t)], in1=g1[0:n, :],
                                         op0=ALU.mult, op1=ALU.mult).then_inc(x_scaled, 1)

            def x_lo(t):
                n = rows_of(t)
                k = t % 2
                dve.wait_ge(x_hi_ready, t + 1)
                dve.tensor_tensor(xTl[:, :, cols(t)], bank[:, 2 * k:2 * k + 2, :].rearrange("p b (c t) -> p (b c) t", t=P)[:, :, 0:n],
                                  xTh[:, :, cols(t)].bitcast(F32), ALU.subtract).then_inc(xnT_ready, 1)

            def w_lo(m, b):
                dve.wait_ge(w_hi_ready, m + 1)
                dve.tensor_tensor(wl[b][:, :, :], w_raw[b][:, :].rearrange("p (c f) -> p c f", c=KC), wh[b][:, :, :].bitcast(F32),
                                  ALU.subtract).then_inc(w_lo_ready, 1)

            dve.wait_ge(g1_in, 16)
            for t in range(ALLT):
                scale_x(t)
                if t >= 1:
                    x_lo(t - 1)
            w_lo(0, 0)
            x_lo(TILES)
            dve.wait_ge(const_in, 16 * 9)
            st.then(dve.tensor_scalar(nsink[:, :], sink_in[:, :], -1.0, None, ALU.mult))
            st.then(dve.tensor_scalar(nsink_s[:, :], sink_in_s[:, :], -1.0, None, ALU.mult))
            w_lo(1, 1)
            dve.wait_ge(hist_turned, 1)
            dve.tensor_copy(histT[:, :, :], bank[:, 4, 0:CC * 2 * NS].rearrange("p (c n) -> p c n", c=CC)).then_inc(hist_ready, 1)
            for m in range(2, QKV + 1):
                w_lo(m, m % WB)

            dve.wait_ge(v_turned, 1)
            dve.tensor_copy(kv_rows[:, 1, :], bank[:, 1, 3 * P:4 * P]).then_inc(kv_rows_ready, 1)
            dve.wait_ge(kv_turned, 1)
            dve.tensor_copy(kv_rows[:, 0, :], bank[:, 4, 0:P]).then_inc(kv_rows_ready, 1)
            dve.tensor_copy(kvs_rows, bank[0:NS, 4, P:3 * P].rearrange("p (j f) -> p j f", j=2)).then_inc(kv_rows_ready, 1)
            dve.wait_ge(const_made, CONST_ALL)
            dve.wait_ge(run_out, NB * QKV)
            for g in range(NKV):
                h = slice(g * HD, (g + 1) * HD)
                dve.tensor_scalar(qbd[h, :, 4 * g:4 * g + 4], mixedT[h, 0:AC, SEQ:NT].rearrange("p j n -> p n j"),
                                  HD ** -0.5, None, ALU.mult).then_inc(qbd_ready, 1)
            dve.tensor_copy(v_tok[:, 1:ALLT, :], bank[:, 0:2, :].rearrange("p b (c t) -> p (b c) t", t=P)).then_inc(v_ready, 1)
            w_lo(7, 1)

            dve.wait_ge(s_scored, 1)
            st.then(dve.tensor_copy(s_sc[:, :, 0:P], bank[0:NH, 2:4, :].rearrange("p b (n t) -> p (b n) t", t=P)))
            st.then(dve.tensor_copy(s_sc[:, :, P], bank[0:NH, 4, 0:NS]))
            st.then(dve.tensor_reduce(s_mx[:, :], s_sc, AX, ALU.max))
            st.then(dve.scalar_tensor_tensor(out=s_nm[:, :], in0=s_mx[:, :], scalar=-1.0, in1=nsink_s[:, :].broadcast_to([NH, NS]),
                                             op0=ALU.mult, op1=ALU.min))
            st.then(dve.tensor_tensor(s_es[:, :], s_nm[:, :], nsink_s[:, :].broadcast_to([NH, NS]), ALU.subtract))
            dve.tensor_tensor(s_sc, s_sc, bc(s_nm[:, :], P + 1), ALU.add).then_inc(s_shifted, 1)
            w_lo(8, 2)
            dve.wait_ge(s_exp_ready, 2)
            st.then(dve.tensor_reduce(s_dn[:, :], s_p, AX, ALU.add))
            st.then(dve.tensor_tensor(s_dn[:, :], s_dn[:, :], s_es[:, :], ALU.add))
            st.then(dve.reciprocal(s_dn[:, :], s_dn[:, :]))
            dve.wait_ge(s_turned, 1)
            dve.tensor_copy(s_pT[:, :, :], bank[:, 0, 0:NS * NH].rearrange("p (n h) -> p n h", h=NH)).then_inc(s_pT_ready, 1)
            dve.tensor_tensor(s_z[:, :, :], bank[0:NS, 1, 0:NH].unsqueeze(1).broadcast_to([NS, NS, NH]), bc(ident[0:NS, 0:NS], NH),
                              ALU.mult).then_inc(s_pT_ready, 1)
            dve.wait_ge(s_pv_done, 1)
            st.then(dve.tensor_tensor(s_o2, bank[0:NH, 2:4, :].rearrange("p b (n f) -> p (b n) f", f=P),
                                      half_mask[:, :].unsqueeze(1).broadcast_to([NH, NS, P]), ALU.mult))
            st.then(dve.tensor_tensor(s_o, s_o2[:, :, 0:HD], s_o2[:, :, HD:P], ALU.add))
            st.then(dve.tensor_tensor(s_o, s_o, bc(s_dn[:, :], HD), ALU.mult))
            st.then(dve.tensor_tensor(s_sq, s_o, s_o, ALU.mult))
            st.then(dve.tensor_reduce(s_ms[:, :], s_sq, AX, ALU.add))
            dve.tensor_scalar(s_ms[:, :], s_ms[:, :], 1.0 / HD, EPS, ALU.mult, ALU.add).then_inc(s_ms_ready, 1)
            dve.wait_ge(s_r_ready, 1)
            st.then(dve.tensor_tensor(s_n, s_o, bc(s_r[:, :], HD), ALU.mult))
            dve.tensor_tensor(s_n, s_n, ga_s[:, :].unsqueeze(1).broadcast_to([NH, NS, HD]), ALU.mult).then_inc(s_n_ready, 1)

            def stage(t):
                if late(t):
                    dve.wait_ge(scores_done, t * 2)
                dve.tensor_scalar(qs[:, :, :], mixedT[:, 0:AC, cols(t)], HD ** -0.5, None, ALU.mult).then_inc(staged, 1)
                if isinstance(t, int) and t == 0:
                    band, to = kT[:, 0:P].unsqueeze(1).broadcast_to([P, 2, P]), kb[:, :].rearrange("p (h c) -> p h c", h=2)
                else:
                    band, to = kT[:, ds(t * P - P, 2 * P)], kb[:, :]
                dve.tensor_scalar(to, band, 1.0, None, ALU.mult).then_inc(staged, 1)

            def soften(t, k):
                mask = band_mask[:, 0 if isinstance(t, int) and t == 0 else 1, :]
                for half in range(2):
                    dve.wait_ge(scores_done, t * 2 + (half + 1))
                    dve.tensor_tensor(prob[k][:, 4 * half:4 * half + 4, :], bank[:, 2 * half:2 * half + 2, :].rearrange("p b (x c) -> p (b x) c", x=2),
                                      mask.unsqueeze(1).broadcast_to([P, 4, 2 * P]), ALU.add).then_inc(scores_read, 1)
                dve.wait_ge(scores_read, t * 2 + 2)
                st.then(dve.tensor_reduce(mx[:, :], prob[k][:, :, :], AX, ALU.max))
                dve.scalar_tensor_tensor(out=nm[k][:, :], in0=mx[:, :], scalar=-1.0, in1=nsink[:, :], op0=ALU.mult, op1=ALU.min).then_inc(nm_ready, 1)
                dve.wait_ge(nm_ready, t + 1)
                dve.tensor_tensor(sd[k][:, :], nm[k][:, :], nsink[:, :], ALU.subtract).then_inc(sd_ready, 1)

            def norm_heads(t, k):
                dve.wait_ge(exp_ready, t + 1)
                st.then(dve.tensor_tensor(den[k][:, :], den[k][:, :], es[k][:, :], ALU.add))
                st.then(dve.reciprocal(rden[:, :], den[k][:, :]))
                dve.wait_ge(pv_done, t + 1)
                o = at_o[:, :].rearrange("p (h d) -> p h d", d=HD)
                st.then(dve.tensor_tensor(o, bank[:, 4, :].rearrange("p (h d) -> p h d", d=HD), bc(rden[:, :], HD), ALU.mult))
                st.then(dve.tensor_tensor(at_sq[:, :], at_o[:, :], at_o[:, :], ALU.mult))
                st.then(dve.tensor_reduce(at_ms[:, :], at_sq[:, :].rearrange("p (h d) -> p h d", d=HD), AX, ALU.add))
                dve.tensor_scalar(at_ms[:, :], at_ms[:, :], 1.0 / HD, EPS, ALU.mult, ALU.add).then_inc(at_ms_ready, 1)

            def scale_heads(t):
                dve.wait_ge(at_r_ready, t + 1)
                o = at_o[:, :].rearrange("p (h d) -> p h d", d=HD)
                dve.tensor_tensor(at_n[:, :].rearrange("p (h d) -> p h d", d=HD), o, bc(at_r[:, :], HD), ALU.mult).then_inc(at_n_ready, 1)

            def attention_out(t):
                dve.wait_ge(at_turned, t + 1)
                dve.tensor_tensor(mixedT[:, 0:AC, cols(t)], bank[:, 4, :].rearrange("p (c t) -> p c t", t=P), bc(ga[:, :], P), ALU.mult).then_inc(atT_ready, 1)

            def taps(i):
                dve.wait_ge(run_out, i * (3 * NB) + NB * (QKV + 2))
                cwi = cwg[:, i, :] if isinstance(i, int) else cwg[:, ds(i, 1), :].rearrange("p o j -> p (o j)")
                st.then(dve.tensor_scalar(cw[:, :], cwi, 1.0, None, ALU.mult))
                dve.tensor_tensor(uT[:, 2:2 + NT], hcb[:, 0, :], hcb[:, 1, :], ALU.mult).then_inc(u_ready, 1)
                dve.wait_ge(u_ready, i + 1)
                st.then(dve.tensor_scalar(zT[:, 0:SEQ], uT[:, 0:SEQ], cw[:, 0:1], None, ALU.mult))
                for j in (1, 2):
                    st.then(dve.scalar_tensor_tensor(out=zT[:, 0:SEQ], in0=uT[:, j:j + SEQ], scalar=cw[:, j:j + 1], in1=zT[:, 0:SEQ],
                                                     op0=ALU.mult, op1=ALU.add))
                h = (histT[:, i, :] if isinstance(i, int) else histT[:, ds(i, 1), :].rearrange("p o n -> p (o n)")).rearrange("p (n j) -> p n j", j=2)
                z = zT[:, SEQ:NT]
                st.then(dve.tensor_scalar(z, h[:, :, 0], cw[:, 0:1], None, ALU.mult))
                st.then(dve.scalar_tensor_tensor(out=z, in0=h[:, :, 1], scalar=cw[:, 1:2], in1=z, op0=ALU.mult, op1=ALU.add))
                st.then(dve.scalar_tensor_tensor(out=z, in0=uT[:, 2 + SEQ:2 + NT], scalar=cw[:, 2:3], in1=z, op0=ALU.mult, op1=ALU.add))
                last = u_last[:, i, :] if isinstance(i, int) else u_last[:, ds(i, 1), :].rearrange("p o n -> p (o n)")
                st.then(dve.tensor_scalar(last, uT[:, SEQ:2 + NT], 1.0, None, ALU.mult))

            def gated(i):
                dve.wait_ge(run_out, i * (3 * NB) + NB * (QKV + 3))
                st.then(dve.tensor_tensor(zT[:, :], zT[:, :], hcb[:, 2, :], ALU.mult))
                dve.tensor_tensor(sqT[:, 0:NT], zT[:, :], zT[:, :], ALU.mult).then_inc(sq_ready, 1)

            def conv_means_out(i):
                dve.wait_ge(cms_done, i + 1)
                dve.tensor_scalar(cms[:, :], bank[:, 2, 0:2 * ALLT], EPS, None, ALU.add).then_inc(cms_ready, 1)

            def spread_rstd(i):
                dve.wait_ge(crs_ready, i + 1)
                dve.tensor_copy(crs_row[:, :].rearrange("p (m d) -> p m d", d=HD), bc(crs[:, :], HD)).then_inc(crs_row_ready, 1)

            def conv_out(i):
                dve.wait_ge(crs_turned, i + 1)
                at = mixedT[:, AC + i, :] if isinstance(i, int) else mixedT[:, ds(i + AC, 1), :].rearrange("p o t -> p (o t)")
                dve.scalar_tensor_tensor(out=at[:, 0:SEQ].rearrange("p (b t) -> p b t", b=2), in0=bank[:, 0:2, :], scalar=cw[:, 3:4],
                                         in1=zT[:, 0:SEQ].rearrange("p (b t) -> p b t", b=2), op0=ALU.mult, op1=ALU.mult).then_inc(conv_ready, 1)
                dve.scalar_tensor_tensor(out=at[:, SEQ:NT], in0=bank[:, 2, 2 * P - NS:2 * P], scalar=cw[:, 3:4], in1=zT[:, SEQ:NT],
                                         op0=ALU.mult, op1=ALU.mult).then_inc(conv_ready, 1)

            def pair(i, last=False):
                t0 = i * 2
                m = i * 3 + (QKV + 3)
                stage(t0 + 1)
                taps(i)
                if not last:
                    w_lo(m + 1, 1)
                gated(i)
                soften(t0 + 1, 1)
                norm_heads(t0, 0)
                conv_means_out(i)
                scale_heads(t0)
                spread_rstd(i)
                if not last:
                    w_lo(m + 2, 2)
                    stage(t0 + 2)
                attention_out(t0)
                conv_out(i)
                if last:
                    w_out_lo(0, 3)
                norm_heads(t0 + 1, 1)
                if not last:
                    soften(t0 + 2, 0)
                scale_heads(t0 + 1)
                if not last and (not isinstance(i, int) or i < CC - 2):
                    w_lo(m + 3, 0)
                attention_out(t0 + 1)
                if last:
                    w_out_lo(3, KC)

            def w_out_lo(lo, hi):
                dve.wait_ge(run_done, NB * CHUNKS)
                for c in range(lo, hi):
                    dve.wait_ge(w_hi_ready, CHUNKS + c + 1)
                    dve.tensor_tensor(w_ol[:, c, :], w_raw[c % WB][:, :], w_oh[:, c, :].bitcast(F32), ALU.subtract).then_inc(w_lo_ready, 1)

            stage(0)
            soften(0, 0)
            w_lo(9, 0)
            dve.wait_ge(s_n_turned, 1)
            turned = bank[0:HD, 4, 0:NS * NH].rearrange("p (n c x) -> p c n x", n=NS, x=2)
            for x in range(2):
                dve.tensor_copy(mixedT[x * HD:(x + 1) * HD, 0:AC, SEQ:NT], turned[:, :, :, x]).then_inc(s_mixed, 1)
            pair(0)
            st.loop(1, CC - 2, 2 + 10 + 8 + 1, pair)
            pair(CC - 2)
            pair(CC - 1, True)
            dve.wait_ge(u_turned, 1)
            dve.wait_ge(kvs_stored, 32)
            dve.tensor_copy(u_rows[:, :], bank[0:2 + NS, 3, :]).then_inc(u_rows_ready, 1)
            st.then(dve.memset(logits[:, :, :], 0.0))

            def x2_of(t):
                return x2[0:rows_of(t), t, :] if isinstance(t, int) else x2[:, ds(t, 1), :].rearrange("p o d -> p (o d)")

            def mix_lo(t, k):
                n = rows_of(t)
                dve.wait_ge(mix_hi_ready, t + 1)
                dve.tensor_tensor(mix_l[k][:, :, 0:n], mixedT[:, :, cols(t)], mix_h[k][:, :, 0:n].bitcast(F32), ALU.subtract).then_inc(mix_staged, 1)

            def residual(t, k, free):
                n = rows_of(t)
                dve.wait_ge(out_done, t + 1)
                dve.tensor_tensor(x2_of(t), bank[0:n, 2 * k:2 * k + 2, :].rearrange("p b d -> p (b d)"), x2_of(t), ALU.add).then_inc(x2_ready, 1)
                if not isinstance(t, int) or t + 2 <= TILES:
                    mix_lo(t + 2, k)
                dve.wait_ge(rstd2_ready, t + 1)
                if late(t, 2):
                    dve.wait_ge(xn2_stored[k], free)
                dve.scalar_tensor_tensor(out=xn2[k][0:n, :].rearrange("p (c q) -> p q c", c=KC), in0=x2_of(t).rearrange("p (q c) -> p q c", c=KC),
                                         scalar=rstd[1][0:n, col(t)], in1=g2[0:n, :].rearrange("p (q c) -> p q c", c=KC),
                                         op0=ALU.mult, op1=ALU.mult).then_inc(xn2_ready, 1)
                dve.wait_ge(routed, t + 1)
                lt = logits[0:n, t, :] if isinstance(t, int) else logits[:, ds(t, 1), :].rearrange("p o r -> p (o r)")
                dve.tensor_tensor(lt, bank[0:n, 7, 0:NR], b_r[0:n, :], ALU.add).then_inc(logits_ready, 1)

            mix_lo(0, 0)
            mix_lo(1, 1)
            dve.wait_ge(x_again[0], 16)
            dve.wait_ge(g2_in, 16)
            dve.wait_ge(late_const_in, 16 * 4)
            residual(0, 0, 0)
            residual(1, 1, 0)
            dve.wait_ge(x_again[1], 16 * 3)
            with dve.Fori(1, TILES // 2 - 1) as i:
                for k in range(2):
                    residual(i * 2 + k, k, i * 16)
            for t in range(TILES - 2, TILES):
                residual(t, t % 2, 16 * (t // 2))
            residual(TILES, 0, 16 * (TILES // 2))

            dve.wait_ge(logits_ready, ALLT)

            def first_of_max(vals, top, hot, a, b):
                st.then(dve.tensor_reduce(top, vals, AX, ALU.max))
                st.then(dve.tensor_tensor(a, vals, bc(top, EG), ALU.is_equal))
                st.then(dve.tensor_tensor(a, a, rev4[:, :, :], ALU.mult))
                st.then(dve.tensor_reduce(b, a, AX, ALU.max))
                st.then(dve.tensor_tensor(hot, a, bc(b, EG), ALU.is_equal))

            top_c, tmp9, top1, top2, denom, ratio, psel, one_r = [r[:, :] for r in r9]
            hot_g, hot_1, fine, tmp4, shifted = [r[:, :, :] for r in r4]
            coarse = logits[:, :, 0:NG]
            first_of_max(coarse, top_c, hot_g, tmp4, tmp9)
            dve.tensor_tensor(shifted, coarse, bc(top_c, NG), ALU.subtract).then_inc(r_shifted, 1)
            g_e = "p t (g j) -> p t g j"
            st.then(dve.tensor_tensor(prod16.rearrange(g_e, g=NG), logits[:, :, NG:NR].rearrange(g_e, g=NG),
                                      hot_g.unsqueeze(3).broadcast_to([P, ALLT, NG, EG]), ALU.mult))
            st.then(dve.tensor_reduce(fine, prod16.rearrange("p t (g j) -> p t j g", g=NG), AX, ALU.add))
            first_of_max(fine, top1, hot_1, tmp4, tmp9)

            def picked(k, hot):
                st.then(dve.tensor_tensor(pick[:, k, :, :].rearrange(g_e, g=NG), hot_g.unsqueeze(3).broadcast_to([P, ALLT, NG, EG]),
                                          hot.unsqueeze(2).broadcast_to([P, ALLT, NG, EG]), ALU.mult))
                st.then(dve.tensor_tensor(pick[:, k, :, :], pick[:, k, :, :], bc(valid[:, :], NE), ALU.mult))

            picked(0, hot_1)
            st.then(dve.scalar_tensor_tensor(out=fine, in0=hot_1, scalar=LOWEST, in1=fine, op0=ALU.mult, op1=ALU.add))
            first_of_max(fine, top2, hot_1, tmp4, tmp9)
            dve.tensor_tensor(ratio, top2, top1, ALU.subtract).then_inc(r_shifted, 1)
            picked(1, hot_1)
            st.then(dve.tensor_tensor(both, pick[:, 0, :, :], pick[:, 1, :, :], ALU.add))
            st.then(dve.memset(before[:, 0, :], 0.0))
            for t in range(ALLT):
                ins = dve.tensor_tensor(before[:, t + 1, :], before[:, t, :], both[:, t, :], ALU.add)
                if t < ALLT - 1:
                    st.then(ins)
            ins.then_inc(picks_ready, 1)
            dve.wait_ge(r_exp_ready, 2)
            st.then(dve.tensor_reduce(denom, shifted, AX, ALU.add))
            st.then(dve.tensor_scalar(one_r, ratio, 1.0, None, ALU.add))
            st.then(dve.tensor_tensor(denom, denom, one_r, ALU.mult))
            st.then(dve.reciprocal(gate[:, 0, :], denom))
            st.then(dve.tensor_tensor(gate[:, 1, :], gate[:, 0, :], ratio, ALU.mult))

            dve.wait_ge(places_done, 1)
            st.then(dve.tensor_copy(count[:, :], bank[:, 1, 0:NE]))
            st.then(dve.tensor_tensor(cmp9, bc(count[:, :], ALLT), steps128[:, :].unsqueeze(1).broadcast_to([P, NE, ALLT]), ALU.is_gt))
            st.then(dve.tensor_reduce(tiles_of[:, 0, :], cmp9, AX, ALU.add))
            st.then(dve.tensor_scalar(tiles_of[:, 1, :], tiles_of[:, 0, :], 0.0, None, ALU.is_gt))
            src = tiles_of
            for n, sh in enumerate((1, 2, 4, 8)):
                dst = scan[n % 2]
                st.then(dve.tensor_copy(dst[:, :, 0:sh], src[:, :, 0:sh]))
                st.then(dve.tensor_tensor(dst[:, :, sh:NE], src[:, :, sh:NE], src[:, :, 0:NE - sh], ALU.add))
                src = dst
            ends, order = src[:, 0, :], src[:, 1, :]
            st.then(dve.tensor_tensor(cmp16, ends.unsqueeze(1).broadcast_to([P, PLANNED, NE]), bc(iota_row[:, 0:PLANNED], NE), ALU.is_le))
            st.then(dve.tensor_tensor(cmp16, cmp16, tiles_of[:, 1, :].unsqueeze(1).broadcast_to([P, PLANNED, NE]), ALU.mult))
            st.then(dve.tensor_reduce(tile_j[:, :], cmp16, AX, ALU.add))
            st.then(dve.tensor_scalar(last_j[:, :], order[:, NE - 1:NE], -1.0, None, ALU.add))
            st.then(dve.tensor_scalar(tile_j[:, :], tile_j[:, :], last_j[:, 0:1], None, ALU.min))
            st.then(dve.tensor_scalar(tile_j3_i[:, :], tile_j[:, :], 11.0, None, ALU.mult))
            st.then(dve.tensor_scalar(tile_j3_i[:, :], tile_j3_i[:, :], 5, None, ALU.logical_shift_right))
            st.then(dve.tensor_copy(tile_j3[:, :], tile_j3_i[:, :]))
            st.then(dve.scalar_tensor_tensor(out=tile_j3[:, :], in0=tile_j3[:, :], scalar=-float(EB), in1=tile_j[:, :],
                                             op0=ALU.mult, op1=ALU.add))
            at_buf = plan_f[:, PL_BUF:PL_BUF + PLANNED]
            st.then(dve.tensor_scalar(at_buf, tile_j3[:, :], float(EB - 1), float(ew_at[2] - 2 * EW), ALU.is_ge, ALU.mult))
            st.then(dve.scalar_tensor_tensor(out=at_buf, in0=tile_j3[:, :], scalar=float(EW), in1=at_buf, op0=ALU.mult, op1=ALU.add))
            st.then(dve.tensor_scalar(plan_f[:, PL_ARRIVED:PL_ARRIVED + PLANNED], tile_j[:, :], 1.0, 48.0, ALU.add, ALU.mult))
            by_place = [P, NE, NE]
            st.then(dve.tensor_tensor(cmp_j, order.unsqueeze(1).broadcast_to(by_place), bc(iota_row[:, 0:NE], NE), ALU.is_le))
            st.then(dve.tensor_reduce(plan_f[:, PL_EXPERT:PL_EXPERT + NE], cmp_j, AX, ALU.add))
            st.then(dve.tensor_tensor(cmp_j, order.unsqueeze(1).broadcast_to(by_place), bc(iota_row[:, 1:NE + 1], NE), ALU.is_le))
            st.then(dve.tensor_tensor(cmp_j, cmp_j, tiles_of[:, 0, :].unsqueeze(1).broadcast_to(by_place), ALU.mult))
            st.then(dve.tensor_reduce(plan_f[:, PL_FREED:PL_FREED + NE], cmp_j, AX, ALU.add))
            st.then(dve.tensor_scalar(plan_f[:, PL_FREED:PL_FREED + NE], plan_f[:, PL_FREED:PL_FREED + NE], 2.0, None, ALU.mult))
            st.then(dve.tensor_copy(plan_f[:, PL_TILES:PL_TILES + 1], ends[:, NE - 1:NE]))
            st.then(dve.tensor_copy(plan_f[:, PL_EXPERTS:PL_EXPERTS + 1], order[:, NE - 1:NE]))
            for k in range(2):
                st.then(dve.tensor_scalar(plan_f[:, PL_STORED + k:PL_STORED + k + 1], ends[:, NE - 1:NE], float(1 - k), None, ALU.add))
            st.then(dve.tensor_copy(plan[:, :], plan_f[:, :]))
            st.then(dve.tensor_scalar(plan[:, PL_STORED:PL_ALL], plan[:, PL_STORED:PL_ALL], 1, None, ALU.logical_shift_right))
            dve.tensor_scalar(plan[:, PL_STORED:PL_ALL], plan[:, PL_STORED:PL_ALL], 4, None, ALU.logical_shift_left).then_inc(plan_ready, 1)

            st.then(dve.tensor_tensor(start128[:, :], ends, tiles_of[:, 0, :], ALU.subtract))
            st.then(dve.tensor_scalar(start128[:, :], start128[:, :], float(P), None, ALU.mult))
            st.then(dve.tensor_tensor(place16, bank[:, 0, 0:ALLT * NE].rearrange("p (t e) -> p t e", e=NE),
                                      start128[:, :].unsqueeze(1).broadcast_to([P, ALLT, NE]), ALU.add))
            for k in range(2):
                st.then(dve.tensor_tensor(prod16, pick[:, k, :, :], place16, ALU.mult))
                st.then(dve.tensor_reduce(slot_f[:, k, :], prod16, AX, ALU.add))
            st.then(dve.tensor_copy(slot_i[:, :, :], slot_f[:, :, :]))
            st.then(dve.tensor_scalar(row_i[:, :, :], slot_i[:, :, :], P - 1, None, ALU.bitwise_and))
            st.then(dve.tensor_scalar(tile_i[:, :, :], slot_i[:, :, :], 7, None, ALU.logical_shift_right))
            st.then(dve.tensor_copy(tile_f[:, :, :], tile_i[:, :, :]))
            st.then(dve.tensor_tensor(row_f[:, :, :], row_i[:, :, :], nowhere[:, :, :], ALU.add))
            kt = "p k t -> p (k t)"
            st.then(dve.tensor_tensor(row_hot, bc(row_f[:, :, :].rearrange(kt), P), iota_row[:, :].unsqueeze(1).broadcast_to([P, 2 * ALLT, P]), ALU.is_equal))
            st.then(dve.tensor_tensor(tile_hot, bc(tile_f[:, :, :].rearrange(kt), PLANNED),
                                      iota_row[:, 0:PLANNED].unsqueeze(1).broadcast_to([P, 2 * ALLT, PLANNED]), ALU.is_equal))
            st.then(dve.tensor_tensor(payload[:, :, 1, :], tile_hot, bc(gate[:, :, :].rearrange(kt), PLANNED), ALU.mult))
            for k in range(2):
                j = slice(k * ALLT, (k + 1) * ALLT)
                ins = dve.tensor_tensor(payload[:, j, 0, :], tile_hot[:, j, :], bc(token_no[:, :], PLANNED), ALU.mult)
                if k == 0:
                    st.then(ins)
            ins.then_inc(table_in_ready, 1)
            dve.wait_ge(table_done, 1)
            st.then(dve.tensor_copy(slot_gate[:, :], bank[:, 2, PLANNED:2 * PLANNED]))
            dve.tensor_copy(slot_tok[:, :], bank[:, 2, 0:PLANNED]).then_inc(slots_ready, 1)

            def hidden(u, k):
                dve.wait_ge(silu_ready, u + 1)
                qc = "p (q c) -> p q c"
                dve.scalar_tensor_tensor(out=hid[k].rearrange("p c q -> p q c"), in0=bank[:, 2 + k, FE:2 * FE].rearrange(qc, c=FC),
                                         scalar=slot_gate[:, col(u)], in1=silu[k].rearrange(qc, c=FC), op0=ALU.mult, op1=ALU.mult).then_inc(hid_ready, 1)

            def y_out(u, k):
                if late(u, 2):
                    dve.wait_ge(y_stored[k], u // 2 * 16 if isinstance(u, int) else (u - k) * 8)
                dve.wait_ge(y_done, u * 2 + 2)
                dve.tensor_copy(y_sb[k][:, 512:D], bank[:, 6, :]).then_inc(y_right_ready, 1)

            def tile(u, k):
                hidden(u + 1, 1 - k)
                y_out(u, k)

            dve.wait_ge(plan_ready, 1)
            tiles_used = dve.value_load(plan[0:1, PL_TILES:PL_TILES + 1], min_val=LEAST_TILES, max_val=SLOT_TILES)
            hidden(0, 0)
            tile(0, 0)
            tile(1, 1)
            with dve.Fori(1, LEAST_TILES // 2) as i:
                for k in range(2):
                    tile(i * 2 + k, k)
            with dve.Fori(LEAST_TILES // 2, SLOT_TILES // 2) as i:
                for k in range(2):
                    with dve.If(i * 2 + k < tiles_used):
                        tile(i * 2 + k, k)

            def add_pair(t, k, arrived):
                n = rows_of(t)
                dve.wait_ge(pair_gathered[k], arrived)
                st.then(dve.tensor_tensor(x2_of(t), x2_of(t), pair_rows[k][0][0:n, :], ALU.add))
                dve.tensor_tensor(x2_of(t), x2_of(t), pair_rows[k][1][0:n, :], ALU.add).then_inc(x3_ready, 1)

            def last_norm(t, k, free):
                n = rows_of(t)
                dve.wait_ge(rstd3_ready, t + 1)
                if late(t, LB):
                    dve.wait_ge(out_stored[k], free)
                dve.scalar_tensor_tensor(out=out_rows[k][0:n, :], in0=x2_of(t), scalar=rstd[2][0:n, col(t)], in1=gf[0:n, :],
                                         op0=ALU.mult, op1=ALU.mult).then_inc(out_ready, 1)

            add_pair(0, 0, 32)
            add_pair(1, 1, 32)
            last_norm(0, 0, 0)
            add_pair(2, 2, 32)
            last_norm(1, 1, 0)

            for i in range(1, ALLT // LB):
                for k in range(LB):
                    t = i * LB + k
                    add_pair(t, k, i * 32 + 32)
                    last_norm(t - 1, (t - 1) % LB, (t - 1) // LB * 16)
            last_norm(ALLT - 1, LB - 1, (ALLT - 1) // LB * 16)


CONST_ALL = 28


_INS = ["x_prompt", "x_sample", "cache_k_win", "cache_v_win", "state_conv", "norm1_g", "w_in", "conv_w", "sinks",
        "attn_out_g", "conv_out_g", "w_out", "norm2_g", "w_group", "b_group", "w_fine", "b_fine", "w_gate", "w_up",
        "w_down", "final_g"]
_OUTS = [(1, SEQ, D), (NS, 1, D), (1, 1, P, NKV, HD), (1, 1, P, NKV, HD), (1, 1, 2, CONV),
         (1, NS, P, NKV, HD), (1, NS, P, NKV, HD), (1, NS, 2, CONV)]


def kernel(**inputs):
    import numpy as _np
    import concourse.bacc as _bacc
    from concourse import mybir as _mybir
    from concourse.bass_utils import run_bass_kernel_spmd as _run

    nc = _bacc.Bacc("TRN2", target_bir_lowering=False, num_devices=1)
    arrays, args = {}, []
    for name in _INS:
        a = _np.ascontiguousarray(inputs[name])
        arrays[f"in_{name}_dram"] = a
        args.append(nc.dram_tensor(f"in_{name}_dram", a.shape, _mybir.dt.from_np(a.dtype), kind="ExternalInput").ap())
    for i, shape in enumerate(_OUTS):
        args.append(nc.dram_tensor(f"out_{i}_dram", shape, _mybir.dt.float32, kind="ExternalOutput").ap())
    hybrid_layer_step(nc, *args)
    r = _run(nc, [arrays], core_ids=[0])
    return tuple(r.results[0][f"out_{i}_dram"] for i in range(len(_OUTS)))
```

```python
from contextlib import ExitStack

import concourse.bass as bass
from concourse import mybir
from concourse.bass import ds

P = 128
D = 1024
KC = D // P
SEQ = 1024
NS = 8
NT = SEQ + NS
TILES = SEQ // P
ALLT = TILES + 1
HD = 64
NH = 8
NKV = 2
ATT = NH * HD
AC = ATT // P
CONV = D - ATT
CC = CONV // P
OFF_K = ATT
OFF_V = OFF_K + NKV * HD
OFF_B = OFF_V + NKV * HD
OFF_C = OFF_B + CONV
OFF_H = OFF_C + CONV
QKV = 6
NG = 4
EG = 4
NE = NG * EG
FE = 256
FC = FE // P
NR = NG + NE
SLOT_TILES = (2 * NT + NE * (P - 1)) // P
LEAST_TILES = 2 * NT // P
FILL = SLOT_TILES - LEAST_TILES
PLANNED = SLOT_TILES + 2
EW = 3 * KC * FE
PIECES = EW // D
GU = 4
GU_FIRST = GU - 1
PL_TILE = 0
J_BITS = 4
DOWN_TOO = 1 << 2 * J_BITS
GATE_UP_TOO = 2 << 2 * J_BITS
PL_TILES = PL_TILE + PLANNED
PL_STORED = PL_TILES + 1
PL_ALL = PL_STORED + 2
NB = 3
RUN = NT // NB
WB = 3
CHUNKS = QKV + 3 * CC
XB = 4
LB = 3
EPS = 1e-5
MASKED = -1e30
LOWEST = -3e38
NOWHERE = 999.0

F32 = mybir.dt.float32
F32R = mybir.dt.float32r
I32 = mybir.dt.int32
ALU = mybir.AluOpType
ACT = mybir.ActivationFunctionType
AX = mybir.AxisListType.X


class Steps:

    def __init__(self, eng, sem):
        self.eng, self.sem, self.base, self.n = eng, sem, 0, 0

    def then(self, ins):
        ins.then_inc(self.sem, 1)
        self.n += 1
        self.eng.wait_ge(self.sem, self.base + self.n)

    def along(self, ins):
        ins.then_inc(self.sem, 1)
        self.n += 1

    def loop(self, lo, hi, per, body):
        start = self.n
        with self.eng.Fori(lo, hi) as i:
            self.base = (i - lo) * per
            body(i)
        assert self.n == start + per, f"{self.n - start} steps, not {per}"
        self.base, self.n = 0, start + per * (hi - lo)


def hybrid_layer_step(nc, x_prompt, x_sample, cache_k_win, cache_v_win, state_conv, norm1_g, w_in,
                      conv_w, sinks, attn_out_g, conv_out_g, w_out, norm2_g, w_group, b_group,
                      w_fine, b_fine, w_gate, w_up, w_down, final_g,
                      y_prompt, y_sample, new_k_prompt, new_v_prompt, new_conv_prompt,
                      new_k_sample, new_v_sample, new_conv_sample):
    xp, x_smp = x_prompt[0], x_sample[:, 0, :]
    w_in_v = w_in[0].rearrange("(c p) f -> p c f", p=P)
    expert_parts = [w[0].rearrange("e (p c) f -> e p (c f)", p=P) for w in (w_gate, w_up, w_down)]
    xn2_d = nc.dram_tensor("xn2_rows", [NT, D], F32, kind="Internal").ap()
    y_d = nc.dram_tensor("y_slots", [SLOT_TILES * P, D], F32, kind="Internal").ap()

    ctx = ExitStack()
    with ctx:
        def sem(name):
            return ctx.enter_context(nc.semaphore(name))

        def sems(name, n):
            return [sem(f"{name}{i}") for i in range(n)]

        def alloc(stack, name, shape, dt=F32):
            return stack.enter_context(nc.sbuf_tensor("b_" + name, shape, dt))

        def sb(name, shape, dt=F32):
            return alloc(ctx, name, shape, dt)

        bank = ctx.enter_context(nc.psum_tensor("banks", [P, 8, 512], F32))

        ident = sb("ident", [P, P])
        ones = sb("ones", [P, P])
        earlier = sb("earlier", [P, P])
        group_mean = sb("group_mean", [P, 2])
        exponent = sb("exponent", [P, 2 * ALLT])
        epsilon = sb("epsilon", [P, 1])
        rev4 = sb("rev4", [P, ALLT, EG])
        valid = sb("valid", [P, ALLT])
        nowhere = sb("nowhere", [P, 2, ALLT])
        iota_row = sb("iota_row", [P, P])
        iota_p = sb("iota_p", [P, 1])
        steps128 = sb("steps128", [P, ALLT])
        token_no = sb("token_no", [P, ALLT])
        half_mask = sb("half_mask", [NH, P])
        g1 = sb("g1", [P, KC])
        ga = sb("ga", [P, AC])
        ga_s = sb("ga_s", [NH, HD])
        cwg = sb("cwg", [P, CC, 4])
        sink_in = sb("sink_in", [P, NH])
        nsink = sb("nsink", [P, NH])
        sink_in_s = sb("sink_in_s", [NH, 1])
        nsink_s = sb("nsink_s", [NH, 1])
        w_r = sb("w_r", [P, KC, NR])
        b_r = sb("b_r", [P, NR])

        mixedT = sb("mixedT", [P, KC, NT])
        w_raw = [sb(f"w_raw{i}", [P, D]) for i in range(WB)]
        ms = [sb(f"ms{i}", [P, ALLT]) for i in range(3)]
        rstd = [sb(f"rstd{i}", [P, ALLT]) for i in range(3)]
        kv_rows = sb("kv_rows", [P, 2, P])
        u_rows = sb("u_rows", [2 + NS, CONV])
        kvs_rows = u_rows[0:NS, 0:2 * P].rearrange("p (j f) -> p j f", j=2)

        first = ExitStack()
        xTh = alloc(first, "xTh", [P, KC, NT], F32R)
        xTl = alloc(first, "xTl", [P, KC, NT], F32R)
        wh = [alloc(first, f"wh{i}", [P, KC, P], F32R) for i in range(WB)]
        wl = [alloc(first, f"wl{i}", [P, KC, P], F32R) for i in range(WB)]
        hcb = alloc(first, "hcb", [P, 3, NT])
        hcb_flat = hcb[:, :, :].rearrange("p x t -> p (x t)")
        g1 = hcb_flat[:, 0:D]
        hist = hcb_flat[0:2 * NS, D:D + CONV]
        kT = alloc(first, "kT", [P, NT])
        v_tok = alloc(first, "v_tok", [P, ALLT, P])
        uT = alloc(first, "uT", [P, 2 + NT])
        zT = alloc(first, "zT", [P, NT])
        vT = zT
        sqT = alloc(first, "sqT", [P, ALLT * P])
        u_last = alloc(first, "u_last", [P, CC, 2 + NS])
        histT = alloc(first, "histT", [P, CC, 2 * NS])
        cw = alloc(first, "cw", [P, 4])
        cms = alloc(first, "cms", [P, 2 * ALLT])
        crs = alloc(first, "crs", [P, 2 * ALLT])
        crs_row = sqT
        band_mask = alloc(first, "band_mask", [P, 2, 2 * P])
        qs = alloc(first, "qs", [P, AC, P])
        kb = alloc(first, "kb", [P, 2 * P])
        prob = [alloc(first, f"prob{i}", [P, NH, 2 * P]) for i in range(2)]
        pTs = alloc(first, "pTs", [P, NH, 2, P])
        prob_flat = [b[:, :, :].rearrange("p a b -> p (a b)") for b in prob]
        x_in = [prob_flat[i // 2][:, (i % 2) * D:(i % 2 + 1) * D] for i in range(XB)]
        pTs_flat = pTs[:, :, :, :].rearrange("p a b c -> p (a b c)")
        x_sc = [pTs_flat[:, i * D:(i + 1) * D] for i in range(2)]
        mx = alloc(first, "mx", [P, NH])
        nm = [alloc(first, f"nm{i}", [P, NH]) for i in range(2)]
        sd = [alloc(first, f"sd{i}", [P, NH]) for i in range(2)]
        es = [alloc(first, f"es{i}", [P, NH]) for i in range(2)]
        den = [alloc(first, f"den{i}", [P, NH]) for i in range(2)]
        rden = alloc(first, "rden", [P, NH])
        at_o = alloc(first, "at_o", [P, ATT])
        at_n = alloc(first, "at_n", [P, ATT])
        at_sq = at_n
        at_ms = alloc(first, "at_ms", [P, NH])
        at_r = alloc(first, "at_r", [P, NH])
        conv_half = mixedT[:, AC:KC, :].rearrange("p c t -> p (c t)")
        ck, cv, kTs = [conv_half[:, i * D:(i + 1) * D].rearrange("p (n f) -> p n f", n=NS) for i in range(3)]
        squared1 = conv_half[:, 3 * D:4 * D]
        qbd = kb[:, 0:NS * NH].rearrange("p (n h) -> p n h", n=NS)
        s_sc = prob[0][0:NH, :, :].rearrange("p a b -> p (a b)")[:, 0:NS * (P + 1)].rearrange("p (n t) -> p n t", n=NS)
        s_p = prob[1][0:NH, :, :].rearrange("p a b -> p (a b)")[:, 0:NS * (P + 1)].rearrange("p (n t) -> p n t", n=NS)
        s_o2 = pTs[0:NH, :, :, :].rearrange("p a b c -> p (a b c)")[:, 0:NS * P].rearrange("p (n f) -> p n f", n=NS)
        s_o = at_o[0:NH, :].rearrange("p (n d) -> p n d", n=NS)
        s_sq = at_sq[0:NH, :].rearrange("p (n d) -> p n d", n=NS)
        s_n = at_n[0:NH, :].rearrange("p (n d) -> p n d", n=NS)
        qs_flat = qs[:, :, :].rearrange("p j t -> p (j t)")
        s_pT = qs_flat[:, 0:NS * NH].rearrange("p (n h) -> p n h", n=NS)
        s_z = qs_flat[0:NS, NS * NH:2 * NS * NH].rearrange("p (n h) -> p n h", n=NS)
        s_mx, s_nm, s_es, s_dn, s_ms, s_r = [qs_flat[0:NH, 2 * NS * NH + i * NS:2 * NS * NH + (i + 1) * NS] for i in range(6)]
        first.close()

        projecting = ExitStack()
        w_oh = alloc(projecting, "w_oh", [P, KC, D], F32R)
        w_ol = alloc(projecting, "w_ol", [P, KC, D], F32R)
        mix_h = [alloc(projecting, f"mix_h{i}", [P, KC, P], F32R) for i in range(2)]
        mix_l = [alloc(projecting, f"mix_l{i}", [P, KC, P], F32R) for i in range(2)]
        xn2 = [alloc(projecting, f"xn2_{i}", [P, D]) for i in range(2)]
        xn2T = alloc(projecting, "xn2T", [P, KC, P])
        g2 = alloc(projecting, "g2", [P, D])
        projecting.close()
        last = ExitStack()
        last_flat = alloc(last, "last_flat", [P, 3 * LB * D])
        last.close()
        table = ExitStack()
        alloc(table, "table_pad", [P, EW])
        row_hot = alloc(table, "row_hot", [P, 2 * ALLT, P], F32R)
        payload = alloc(table, "payload", [P, 2 * ALLT, 3, PLANNED], F32R)
        table.close()
        second = ExitStack()
        eh = alloc(second, "eh", [P, 2 * EW], F32R)
        el = alloc(second, "el", [P, 2 * EW], F32R)
        x2 = alloc(second, "x2", [P, ALLT, D])
        xgh = alloc(second, "xgh", [P, KC, P], F32R)
        xgl = alloc(second, "xgl", [P, KC, P], F32R)
        hTh = alloc(second, "hTh", [P, FC, P], F32R)
        hTl = alloc(second, "hTl", [P, FC, P], F32R)
        gf = alloc(second, "gf", [P, D])
        junk = alloc(second, "junk", [P, D])
        logits = alloc(second, "logits", [P, ALLT, NR])
        r9 = [alloc(second, f"r9_{i}", [P, ALLT]) for i in range(7)]
        r4 = [alloc(second, f"r4_{i}", [P, ALLT, EG]) for i in range(5)]
        count = alloc(second, "count", [P, NE])
        tiles_of = alloc(second, "tiles_of", [P, 2, NE])
        scan = [alloc(second, f"scan{i}", [P, 2, NE]) for i in range(2)]
        tile_j = alloc(second, "tile_j", [P, PLANNED])
        two_on = alloc(second, "two_on", [P, PLANNED])
        flag = alloc(second, "flag", [P, PLANNED])
        last_j = alloc(second, "last_j", [P, 1])
        plan_f = alloc(second, "plan_f", [P, PL_ALL])
        plan = alloc(second, "plan", [P, PL_ALL], I32)
        order_f = alloc(second, "order_f", [P, NE + 1])
        order_i = alloc(second, "order_i", [P, NE + 1], I32)
        gate_h = alloc(second, "gate_h", [P, 2 * ALLT], F32R)
        start128 = alloc(second, "start128", [P, NE])
        slot_f = alloc(second, "slot_f", [P, 2, ALLT])
        slot_i = alloc(second, "slot_i", [P, 2, ALLT], I32)
        row_i = alloc(second, "row_i", [P, 2, ALLT], I32)
        tile_i = alloc(second, "tile_i", [P, 2, ALLT], I32)
        row_f = alloc(second, "row_f", [P, 2, ALLT])
        tile_f = alloc(second, "tile_f", [P, 2, ALLT])
        gate = alloc(second, "gate", [P, 2, ALLT])
        slot_gate = alloc(second, "slot_gate", [P, PLANNED])
        slot_tok = alloc(second, "slot_tok", [P, PLANNED + 1], I32)
        tok_i = [alloc(second, f"tok_i{i}", [P, 1], I32) for i in range(2)]
        pair_i = [[alloc(second, f"pair_i{i}_{j}", [P, 1], I32) for j in range(2)] for i in range(LB)]
        second.close()
        free_at = [0]
        mixed_flat = mixedT[:, :, :].rearrange("p c t -> p (c t)")

        def carve(n):
            free_at[0] += n
            assert free_at[0] <= KC * NT, free_at[0]
            return mixed_flat[:, free_at[0] - n:free_at[0]]

        y_sb = [carve(D) for _ in range(2)]
        prod16 = carve(ALLT * NE).rearrange("p (t e) -> p t e", t=ALLT)
        pick = carve(2 * ALLT * NE).rearrange("p (k t e) -> p k t e", k=2, t=ALLT)
        both = carve(ALLT * NE).rearrange("p (t e) -> p t e", t=ALLT)
        before = carve((ALLT + 1) * NE).rearrange("p (t e) -> p t e", e=NE)
        place16 = carve(ALLT * NE).rearrange("p (t e) -> p t e", t=ALLT)
        cmp9 = carve(NE * ALLT).rearrange("p (e t) -> p e t", e=NE)
        tile_hot = carve(2 * ALLT * PLANNED).rearrange("p (j u) -> p j u", u=PLANNED)
        cmp16 = y_sb[0][:, 0:PLANNED * NE].rearrange("p (u e) -> p u e", e=NE)
        cmp_j = y_sb[0][:, PLANNED * NE:(PLANNED + NE) * NE].rearrange("p (j e) -> p j e", e=NE)
        xg = [carve(D) for _ in range(2)]
        silu = [carve(FE) for _ in range(2)]
        hid = [carve(FE).rearrange("p (c t) -> p c t", c=FC) for _ in range(2)]
        spare = carve(D)
        pair_rows = [[last_flat[:, (2 * i + j) * D:(2 * i + j + 1) * D] for j in range(2)] for i in range(LB)]
        out_rows = [last_flat[:, (2 * LB + i) * D:(2 * LB + i + 1) * D] for i in range(LB)]

        const_made, const_in, late_const_in = sem("const_made"), sem("const_in"), sem("late_const_in")
        x_arrived = sems("x_arrived", XB)
        x_hi_ready, w_hi_ready, w_lo_ready = sem("x_hi_ready"), sem("w_hi_ready"), sem("w_lo_ready")
        ms1_ready, eps1_added, rstd1_ready = sem("ms1_ready"), sem("eps1_added"), sem("rstd1_ready")
        x_scaled, x_turned, xnT_ready = sem("x_scaled"), sem("x_turned"), sem("xnT_ready")
        w_arrived = sems("w_arrived", PIECES)
        run_done, run_out = sem("run_done"), sem("run_out")
        hist_arrived, hist_turned, hist_ready = sem("hist_arrived"), sem("hist_turned"), sem("hist_ready")
        v_turned, v_ready, kv_turned, kv_rows_ready = sem("v_turned"), sem("v_ready"), sem("kv_turned"), sem("kv_rows_ready")
        staged, scores_done, scores_read = sem("staged"), sem("scores_done"), sem("scores_read")
        nm_ready, sd_ready, exp_ready = sem("nm_ready"), sem("sd_ready"), sem("exp_ready")
        p_turned, pT_ready, pv_done = sem("p_turned"), sem("pT_ready"), sem("pv_done")
        at_ms_ready, at_r_ready, at_n_ready = sem("at_ms_ready"), sem("at_r_ready"), sem("at_n_ready")
        at_turned, atT_ready = sem("at_turned"), sem("atT_ready")
        u_ready, sq_ready, cms_done, cms_ready, crs_ready = sem("u_ready"), sem("sq_ready"), sem("cms_done"), sem("cms_ready"), sem("crs_ready")
        crs_row_ready, crs_turned, conv_ready = sem("crs_row_ready"), sem("crs_turned"), sem("conv_ready")
        u_turned, u_rows_ready = sem("u_turned"), sem("u_rows_ready")
        cache_arrived, ck_turned, kTs_ready, qbd_ready = sem("cache_arrived"), sem("ck_turned"), sem("kTs_ready"), sem("qbd_ready")
        s_scored, s_shifted, s_exp_ready, s_turned, s_pT_ready = sem("s_scored"), sem("s_shifted"), sem("s_exp_ready"), sem("s_turned"), sem("s_pT_ready")
        s_pv_done, s_ms_ready, s_r_ready, s_n_ready, s_n_turned, s_mixed = sem("s_pv_done"), sem("s_ms_ready"), sem("s_r_ready"), sem("s_n_ready"), sem("s_n_turned"), sem("s_mixed")
        g1_in, x_again, gf_in, g2_in, mix_hi_ready, mix_staged, out_done, x2_ready = sem("g1_in"), sems("x_again", 2), sem("gf_in"), sem("g2_in"), sem("mix_hi_ready"), sem("mix_staged"), sem("out_done"), sem("x2_ready")
        ms2_ready, eps2_added, rstd2_ready, xn2_ready = sem("ms2_ready"), sem("eps2_added"), sem("rstd2_ready"), sem("xn2_ready")
        xn2_stored = sems("xn2_stored", 2)
        xn2_turned, xn2T_ready, routed, logits_ready = sem("xn2_turned"), sem("xn2T_ready"), sem("routed"), sem("logits_ready")
        r_shifted, r_exp_ready, picks_ready, places_done = sem("r_shifted"), sem("r_exp_ready"), sem("picks_ready"), sem("places_done")
        tile_hot_ready, tokens_in_ready = sem("tile_hot_ready"), sem("tokens_in_ready")
        table_in_ready, table_done, slots_ready = sem("table_in_ready"), sem("table_done"), sem("slots_ready")
        tok_staged, x_gathered, order_ready, plan_ready = sem("tok_staged"), sems("x_gathered", 2), sem("order_ready"), sem("plan_ready")
        xg_hi_ready, hid_hi_ready = sem("xg_hi_ready"), sem("hid_hi_ready")
        xg_turned, xgT_ready, h_done, silu_ready, hid_ready = sem("xg_turned"), sem("xgT_ready"), sem("h_done"), sem("silu_ready"), sem("hid_ready")
        hid_turned, hidT_ready, y_done = sem("hid_turned"), sem("hidT_ready"), sem("y_done")
        y_left_ready, y_right_ready, y_stored = sem("y_left_ready"), sem("y_right_ready"), sems("y_stored", 2)
        pair_staged, pair_gathered, x3_ready = sem("pair_staged"), sems("pair_gathered", LB), sem("x3_ready")
        ms3_ready, eps3_added, rstd3_ready, out_ready = sem("ms3_ready"), sem("eps3_added"), sem("rstd3_ready"), sem("out_ready")
        out_stored, rows_stored, y_filled = sems("out_stored", LB), sem("rows_stored"), sem("y_filled")
        kvs_stored = sem("kvs_stored")
        dve_step, dve_held, act_held, sp_held, pool_held = sem("dve_step"), sem("dve_held"), sem("act_held"), sem("sp_held"), sem("pool_held")

        ctx.enter_context(nc.allow_non_contiguous_dma(reason="gains and sinks are a few KB"))
        block = ctx.enter_context(nc.Block())

        def rows_of(t):
            return NS if isinstance(t, int) and t == TILES else P

        def cols(t):
            return slice(t * P, t * P + rows_of(t)) if isinstance(t, int) else ds(t * P, P)

        def arrived_in(m):
            return 16 * (m // WB + 1) + 16 * sum(j <= m for j in range(m % WB, AC, WB))

        PRIOR = CHUNKS + KC

        def piece_buf(q):
            return (PRIOR + q) % WB if q < WB else q

        piece_in = w_raw + [junk, gf, spare]

        def piece_arrived(j, q):
            prior = arrived_in(max(m for m in range(PRIOR) if m % WB == piece_buf(q))) if q < WB else 0
            return j * 16 + (prior + 16)

        def piece_no(j, q):
            return j * PIECES + (PRIOR + q)

        def col(t, n=1):
            return slice(t, t + n) if isinstance(t, int) else ds(t, n)

        @block.sync
        def _(sp):
            def load_x(t):
                src = x_smp if t == TILES else xp[cols(t), :]
                sp.dma_start(x_in[t % XB][0:rows_of(t), :], src).then_inc(x_arrived[t % XB], 16)

            def load_w(b, src):
                sp.dma_start(w_raw[b][:, :].rearrange("p (c f) -> p c f", c=KC), src).then_inc(w_arrived[b], 16)

            def load_wq(j):
                for g in range(NKV):
                    sp.dma_start(w_raw[j % WB][:, :].rearrange("p (c f) -> p c f", c=KC)[:, :, g * HD:(g + 1) * HD],
                                 w_in_v[:, :, (4 * g + j) * HD:(4 * g + j + 1) * HD]).then_inc(w_arrived[j % WB], 16)

            load_x(0)
            sp.dma_start(g1, norm1_g[0:1, :].broadcast_to([P, D])).then_inc(g1_in, 16)
            for t in range(1, XB):
                load_x(t)
            load_wq(0)
            for t in range(XB, ALLT):
                sp.wait_ge(x_scaled, t - XB + 1)
                load_x(t)
            for j in range(1, WB):
                load_wq(j)
            sp.dma_start(ga[:, :], attn_out_g[0].rearrange("(c p) -> p c", p=P)).then_inc(const_in, 16)
            sp.dma_start(ga_s[:, :], attn_out_g[0].rearrange("(h d) -> h d", h=NH)).then_inc(const_in, 16)
            for j in range(3):
                sp.dma_start(cwg[:, :, j], conv_w[0, j].rearrange("(c p) -> p c", p=P)).then_inc(const_in, 16)
            sp.dma_start(cwg[:, :, 3], conv_out_g[0].rearrange("(c p) -> p c", p=P)).then_inc(const_in, 16)
            for g in range(NKV):
                dst = sink_in[:, :].rearrange("p (h g j) -> p g h j", h=2, g=NKV)[:, g, :, :]
                src = sinks[0:1, 4 * g:4 * g + 4].rearrange("o (h j) -> o h j", h=2).broadcast_to([P, 2, 2])
                sp.dma_start(dst, src).then_inc(const_in, 16)
            sp.dma_start(sink_in_s[:, :], sinks[0].rearrange("(h o) -> h o", o=1)).then_inc(const_in, 16)
            sp.dma_start(w_r[:, :, 0:NG], w_group[0].rearrange("(p c) n -> p c n", p=P)).then_inc(late_const_in, 16)
            sp.dma_start(w_r[:, :, NG:NR], w_fine[0].rearrange("(p c) n -> p c n", p=P)).then_inc(late_const_in, 16)
            sp.dma_start(b_r[:, 0:NG], b_group[0:1, :].broadcast_to([P, NG])).then_inc(late_const_in, 16)
            sp.dma_start(b_r[:, NG:NR], b_fine[0:1, :].broadcast_to([P, NE])).then_inc(late_const_in, 16)
            sp.dma_start(hist, state_conv[0].rearrange("n j f -> (n j) f")).then_inc(hist_arrived, 16)
            sp.dma_start(ck, cache_k_win[0].rearrange("n t g d -> t n (g d)")).then_inc(cache_arrived, 16)
            sp.dma_start(cv, cache_v_win[0].rearrange("n t g d -> t n (g d)")).then_inc(cache_arrived, 16)
            sp.wait_ge(w_lo_ready, 1)
            load_wq(3)
            for m, off in ((4, OFF_K), (5, OFF_V), (6, OFF_H), (7, OFF_C), (8, OFF_B)):
                sp.wait_ge(w_lo_ready, m - WB + 1)
                load_w(m % WB, w_in_v[:, :, off:off + P])
            sp.wait_ge(const_made, CONST_ALL)
            sp.wait_ge(kv_rows_ready, 3)
            sp.dma_start(new_k_prompt[0, 0].rearrange("t g d -> t (g d)"), kv_rows[:, 0, :]).then_inc(rows_stored, 16)
            sp.dma_start(new_v_prompt[0, 0].rearrange("t g d -> t (g d)"), kv_rows[:, 1, :]).then_inc(rows_stored, 16)
            for j, (new, old) in enumerate(((new_k_sample, cache_k_win), (new_v_sample, cache_v_win))):
                new_v = new[0].rearrange("n t g d -> n t (g d)")
                sp.dma_start(new_v[:, P - 1, :], kvs_rows[:, j, :]).then_inc(kvs_stored, 16)
                sp.dma_start(new_v[:, 0:P - 1, :], old[0].rearrange("n t g d -> n t (g d)")[:, 1:P, :]).then_inc(rows_stored, 16)
            sp.dma_start(new_conv_sample[0, :, 0, :], state_conv[0, :, 1, :]).then_inc(rows_stored, 16)
            zeros = v_tok[:, 0, :].unsqueeze(1).broadcast_to([P, KC, P])
            with sp.Fori(0, CC - 1) as i:
                for x, off in enumerate((OFF_H, OFF_C, OFF_B)):
                    sp.wait_ge(w_lo_ready, i * 3 + (QKV + 1 + x))
                    load_w(x, w_in_v[:, :, ds(i * P + (off + P), P)])
                for x in range(FILL // 4):
                    sp.dma_start(y_d[ds((i * (FILL // 4) + (LEAST_TILES + x)) * P, P), :].rearrange("p (c f) -> p c f", c=KC), zeros).then_inc(y_filled, 16)
            for x in range(FILL // 4):
                at = (SLOT_TILES - FILL // 4 + x) * P
                sp.dma_start(y_d[at:at + P, :].rearrange("p (c f) -> p c f", c=KC), zeros).then_inc(y_filled, 16)
            for c in range(KC):
                sp.wait_ge(w_lo_ready, CHUNKS + c - WB + 1)
                sp.dma_start(w_raw[c % WB][:, :], w_out[0, c * P:(c + 1) * P, :]).then_inc(w_arrived[c % WB], 16)
            sp.wait_ge(u_rows_ready, 1)
            sp.dma_start(new_conv_prompt[0, 0], u_rows[0:2, :]).then_inc(rows_stored, 16)
            sp.dma_start(new_conv_sample[0, :, 1, :], u_rows[2:2 + NS, :]).then_inc(rows_stored, 16)
            sp.wait_ge(y_filled, 16 * FILL)
            sp.wait_ge(conv_ready, 2 * CC)
            sp.wait_ge(atT_ready, TILES)
            x_tiles = xp.rearrange("(t p) d -> p t d", p=P)
            sp.dma_start(x2[:, 0:2, :], x_tiles[:, 0:2, :]).then_inc(x_again[0], 16)
            sp.dma_start(g2[:, :], norm2_g[0:1, :].broadcast_to([P, D])).then_inc(g2_in, 16)
            sp.dma_start(x2[:, 2:TILES, :], x_tiles[:, 2:TILES, :]).then_inc(x_again[1], 16)
            sp.dma_start(x2[0:NS, TILES, :], x_smp).then_inc(x_again[1], 16)
            def store_xn2(t, k):
                sp.wait_ge(xn2_ready, t + 1)
                sp.dma_start(xn2_d[cols(t), :], xn2[k][0:rows_of(t), :]).then_inc(xn2_stored[k], 16)
            with sp.Fori(0, TILES // 2) as i:
                for k in range(2):
                    store_xn2(i * 2 + k, k)
            store_xn2(TILES, 0)
            sp.wait_ge(order_ready, 1)
            experts_used = sp.value_load(order_i[0:1, NE:NE + 1], min_val=2, max_val=NE)

            def load_expert(j):
                e = sp.value_load(order_i[0:1, ds(j, 1)], min_val=0, max_val=NE - 1)
                for q in range(PIECES):
                    if not isinstance(j, int) or j > 0:
                        sp.wait_ge(w_lo_ready, piece_no(j, q) - (PIECES - 1))
                        sp.sem_inc(sp_held, 1)
                    src = expert_parts[q // 2][ds(e, 1), :, (q % 2) * D:(q % 2 + 1) * D].rearrange("o p x -> p (o x)")
                    sp.dma_start(piece_in[piece_buf(q)][:, :], src).then_inc(w_arrived[piece_buf(q)], 16)

            sp.wait_ge(w_lo_ready, PRIOR)
            sp.wait_ge(ms2_ready, ALLT)
            load_expert(0)
            load_expert(1)
            with sp.Fori(2, NE) as j:
                with sp.If(j < experts_used):
                    load_expert(j)
            sp.sem_inc(sp_held, 1)
            sp.wait_ge(w_lo_ready, experts_used * PIECES + PRIOR)
            sp.sem_inc(sp_held, 1)
            sp.dma_start(gf[:, :], final_g.rearrange("(o d) -> o d", o=1).broadcast_to([P, D])).then_inc(gf_in, 16)
            def store_out(t, k):
                n = rows_of(t)
                dst = y_sample[:, 0, :] if n == NS else y_prompt[0][cols(t), :]
                sp.wait_ge(out_ready, t + 1)
                sp.dma_start(dst, out_rows[k][0:n, :]).then_inc(out_stored[k], 16)
            with sp.Fori(0, ALLT // LB - 1) as i:
                for k in range(LB):
                    store_out(i * LB + k, k)
            for k in range(LB):
                store_out(ALLT - LB + k, k)
            for k in range(LB):
                sp.wait_ge(out_stored[k], 16 * (ALLT // LB))
            sp.wait_ge(rows_stored, 16 * 7)

        @block.gpsimd
        def _(pool):
            made = Steps(pool, const_made)

            def select(out, in_, pattern, base, cm, fill, op=ALU.is_ge):
                made.then(pool.affine_select(out=out, in_=in_, compare_op=op, fill=fill, base=base,
                                             pattern=pattern, channel_multiplier=cm))

            def iota(out, pattern, base, cm):
                made.then(pool.iota(out, pattern=pattern, base=base, channel_multiplier=cm,
                                    allow_small_or_imprecise_dtypes=True))

            made.then(pool.memset(ident[:, :], 0.0))
            select(ident[:, :], ident[:, :], [[-1, P]], 0, 1, 1.0, ALU.not_equal)
            made.then(pool.memset(epsilon[:, :], EPS))
            made.then(pool.memset(exponent[:, :], -0.5))

            def rsqrt(n, t, ready, added, out_ready_, rows):
                pool.wait_ge(ready, t + 1)
                pool.sem_inc(pool_held, 1)
                pool.tensor_tensor(ms[n][0:rows, col(t)], ms[n][0:rows, col(t)], epsilon[0:rows, :], ALU.add).then_inc(added, 1)
                pool.wait_ge(added, t + 1)
                pool.sem_inc(pool_held, 1)
                pool.tensor_tensor(rstd[n][0:rows, col(t)], ms[n][0:rows, col(t)], exponent[0:rows, 0:1], ALU.pow).then_inc(out_ready_, 1)

            with pool.Fori(0, TILES) as t:
                rsqrt(0, t, ms1_ready, eps1_added, rstd1_ready, P)
            rsqrt(0, TILES, ms1_ready, eps1_added, rstd1_ready, NS)

            made.then(pool.memset(ones[:, :], 1.0))
            select(earlier[:, :], ones[:, :], [[1, P]], -1, -1, 0.0)
            made.then(pool.memset(group_mean[:, :], 1.0 / HD))
            select(group_mean[:, :], group_mean[:, :], [[-HD, 2]], 0, 1, 0.0)
            select(group_mean[:, :], group_mean[:, :], [[HD, 2]], HD - 1, -1, 0.0)
            made.then(pool.memset(uT[:, 0:2], 0.0))
            made.then(pool.memset(v_tok[:, 0, :], 0.0))
            made.then(pool.memset(qbd[:, :, :], 0.0))
            made.then(pool.memset(band_mask[:, :, :], 0.0))
            select(band_mask[:, :, :], band_mask[:, :, :], [[0, 2], [1, 2 * P]], 0, -1, MASKED)
            select(band_mask[:, :, :], band_mask[:, :, :], [[0, 2], [-1, 2 * P]], P, 1, MASKED)
            made.then(pool.memset(band_mask[:, 0, 0:P], MASKED))
            made.then(pool.memset(half_mask[:, :], 1.0))
            select(half_mask[:, :].rearrange("h (g d) -> h g d", g=NKV), half_mask[:, :].rearrange("h (g d) -> h g d", g=NKV),
                   [[-4, NKV], [0, HD]], 0, 1, 0.0)
            select(half_mask[:, :].rearrange("h (g d) -> h g d", g=NKV), half_mask[:, :].rearrange("h (g d) -> h g d", g=NKV),
                   [[4, NKV], [0, HD]], 3, -1, 0.0)
            iota(rev4[:, :, :], [[0, ALLT], [-1, EG]], EG, 0)
            made.then(pool.memset(valid[:, :], 1.0))
            select(valid[:, :], valid[:, :], [[-P, ALLT]], NT - 1, -1, 0.0)
            made.then(pool.memset(nowhere[:, :, :], 0.0))
            select(nowhere[:, :, :], nowhere[:, :, :], [[0, 2], [-P, ALLT]], NT - 1, -1, NOWHERE)
            iota(iota_row[:, :], [[1, P]], 0, 0)
            iota(iota_p[:, :], [[0, 1]], 0, 1)
            iota(steps128[:, :], [[P, ALLT]], 0, 0)
            iota(token_no[:, :], [[P, ALLT]], 0, 1)
            assert made.n == CONST_ALL, made.n

            def at_power(t):
                pool.wait_ge(at_ms_ready, t + 1)
                pool.tensor_tensor(at_r[:, :], at_ms[:, :], exponent[:, 0:NH], ALU.pow).then_inc(at_r_ready, 1)

            def conv_power(i):
                pool.wait_ge(cms_ready, i + 1)
                pool.tensor_tensor(crs[:, :], cms[:, :], exponent[:, :], ALU.pow).then_inc(crs_ready, 1)

            pool.wait_ge(s_ms_ready, 1)
            pool.tensor_tensor(s_r[:, :], s_ms[:, :], exponent[0:NH, 0:NS], ALU.pow).then_inc(s_r_ready, 1)
            with pool.Fori(0, CC) as i:
                at_power(i * 2)
                conv_power(i)
                at_power(i * 2 + 1)
            with pool.Fori(0, TILES) as t:
                rsqrt(1, t, ms2_ready, eps2_added, rstd2_ready, P)
            rsqrt(1, TILES, ms2_ready, eps2_added, rstd2_ready, NS)

            def at_row(idx):
                return bass.IndirectOffsetOnAxis(ap=idx, axis=0)

            def gather_x(u, k):
                if not isinstance(u, int) or u >= 2:
                    pool.wait_ge(xg_turned, u - 1)
                    pool.sem_inc(pool_held, 1)
                pool.tensor_copy(tok_i[k][:, :], slot_tok[:, col(u)]).then_inc(tok_staged, 1)
                pool.wait_ge(tok_staged, u + 1)
                pool.sem_inc(pool_held, 1)
                pool.indirect_dma_start(xg[k], None, xn2_d, at_row(tok_i[k][:, :])).then_inc(x_gathered[k], 16)

            def tile(u, k):
                gather_x(u + 3, 1 - k)
                pool.wait_ge(y_left_ready, u + 1)
                pool.wait_ge(y_right_ready, u + 1)
                pool.sem_inc(pool_held, 1)
                pool.dma_start(y_d[cols(u), :], y_sb[k]).then_inc(y_stored[k], 16)

            pool.wait_ge(out_done, ALLT)
            pool.wait_ge(tile_hot_ready, 1)
            for k in range(2):
                j = slice(k * ALLT, (k + 1) * ALLT)
                pool.tensor_tensor(payload[:, j, 0, :], tile_hot[:, j, :],
                                   token_no[:, :].unsqueeze(2).broadcast_to([P, ALLT, PLANNED]), ALU.mult).then_inc(tokens_in_ready, 1)
            pool.wait_ge(slots_ready, 1)
            pool.wait_ge(xn2_stored[0], 16 * (TILES // 2 + 1))
            pool.wait_ge(xn2_stored[1], 16 * (TILES // 2))
            for u in range(3):
                gather_x(u, u % 2)
            pool.wait_ge(plan_ready, 1)
            tiles_used = pool.value_load(plan[0:1, PL_TILES:PL_TILES + 1], min_val=LEAST_TILES, max_val=SLOT_TILES)
            with pool.Fori(0, LEAST_TILES // 2) as i:
                for k in range(2):
                    tile(i * 2 + k, k)
            with pool.Fori(LEAST_TILES // 2, SLOT_TILES // 2) as i:
                for k in range(2):
                    with pool.If(i * 2 + k < tiles_used):
                        tile(i * 2 + k, k)
                        pool.sem_inc(pool_held, 1)

            def gather_pair(t, k, rows):
                for j in range(2):
                    pool.tensor_copy(pair_i[k][j][:, :], slot_i[:, j, col(t)]).then_inc(pair_staged, 1)
                pool.wait_ge(pair_staged, t * 2 + 2)
                pool.sem_inc(pool_held, 1)
                for dst, idx in zip(pair_rows[k], pair_i[k]):
                    pool.indirect_dma_start(dst[0:rows, :], None, y_d, at_row(idx[0:rows, :])).then_inc(pair_gathered[k], 16)

            def rstd3(t, rows=P):
                rsqrt(2, t, ms3_ready, eps3_added, rstd3_ready, rows)

            pool.wait_ge(y_filled, 16 * FILL)
            for k in range(2):
                stored = pool.value_load(plan[0:1, PL_STORED + k:PL_STORED + k + 1], min_val=8 * LEAST_TILES, max_val=8 * SLOT_TILES)
                pool.wait_ge(y_stored[k], stored)
                pool.sem_inc(pool_held, 1)
            for k in range(LB):
                gather_pair(k, k, P)
            with pool.Fori(0, ALLT // LB - 2) as i:
                for k in range(LB):
                    rstd3(i * LB + k)
                    gather_pair(i * LB + (k + LB), k, P)
            for k in range(LB):
                t = ALLT - 2 * LB + k
                rstd3(t)
                gather_pair(t + LB, k, rows_of(t + LB))
            for t in range(ALLT - LB, ALLT):
                rstd3(t, rows_of(t))

        @block.scalar
        def _(act):
            def squares(n, t, src, out, ready, rows):
                if not isinstance(t, int) or t >= 1:
                    act.wait_ge(ready, t)
                    act.sem_inc(act_held, 1)
                act.activation(out[0:rows, :], src, ACT.Square, scale=D ** -0.5,
                               accum_out=ms[n][0:rows, col(t)]).then_inc(ready, 1)

            def x_hi(t):
                n = rows_of(t)
                k = t % 2
                act.wait_ge(x_turned, t + 1)
                act.copy(xTh[:, :, cols(t)], bank[:, 2 * k:2 * k + 2, :].rearrange("p b (c t) -> p (b c) t", t=P)[:, :, 0:n]).then_inc(x_hi_ready, 1)

            def w_hi(m, b, arrived):
                act.wait_ge(w_arrived[b], arrived)
                if not isinstance(m, int) or m >= WB:
                    act.wait_ge(run_done, m * NB - (WB - 1) * NB)
                act.copy(wh[b][:, :, :], w_raw[b][:, :].rearrange("p (c f) -> p c f", c=KC)).then_inc(w_hi_ready, 1)

            for t in range(ALLT):
                act.wait_ge(x_arrived[t % XB], 16 * (t // XB + 1))
                squares(0, t, x_in[t % XB][0:rows_of(t), :], squared1, ms1_ready, rows_of(t))
                if t >= 1:
                    x_hi(t - 1)
                if t == 5:
                    w_hi(0, 0, 32)
            x_hi(TILES)

            def projection_out(m, dst, runs=range(NB)):
                for n in runs:
                    act.wait_ge(run_done, m * NB + (n + 1))
                    act.copy(dst[:, n * RUN:(n + 1) * RUN], bank[:, 5 + n, 0:RUN]).then_inc(run_out, 1)

            qkv_out = [mixedT[:, j, :] for j in range(AC)] + [kT[:, :], vT[:, :]]
            act.wait_ge(ms1_ready, ALLT)
            for m in range(QKV):
                w_hi(m + 1, (m + 1) % WB, arrived_in(m + 1))
                projection_out(m, qkv_out[m])
                if m == 0:
                    act.wait_ge(ck_turned, 1)
                    act.copy(kTs, bank[:, 0:2, :].rearrange("p b (n t) -> p (b n) t", t=P)).then_inc(kTs_ready, 1)

            def exps(t, k):
                act.wait_ge(nm_ready, t + 1)
                for h in range(NH):
                    act.activation(prob[k][:, h, :], prob[k][:, h, :], ACT.Exp, bias=nm[k][:, h:h + 1],
                                   accum_out=den[k][:, h:h + 1])
                act.wait_ge(sd_ready, t + 1)
                act.activation(es[k][:, :], sd[k][:, :], ACT.Exp).then_inc(exp_ready, 1)

            def probs_out(t, k):
                if not isinstance(t, int) or t >= 1:
                    act.wait_ge(pv_done, t)
                for q in range(4):
                    act.wait_ge(p_turned, t * 4 + (q + 1))
                    act.copy(pTs[:, 2 * q:2 * q + 2, :, :].rearrange("p a b c -> p (a b c)"), bank[:, 2 + q % 2, :]).then_inc(pT_ready, 1)

            w_hi(7, 1, arrived_in(7))
            act.wait_ge(hist_turned, 1)
            projection_out(6, hcb[:, 0, :])
            act.wait_ge(s_shifted, 1)
            act.activation(s_p, s_sc, ACT.Exp).then_inc(s_exp_ready, 1)
            act.activation(s_es[:, :], s_es[:, :], ACT.Exp).then_inc(s_exp_ready, 1)
            w_hi(8, 2, arrived_in(8))
            projection_out(7, hcb[:, 1, :])
            w_hi(9, 0, arrived_in(9))
            projection_out(8, hcb[:, 2, :])
            act.wait_ge(s_mixed, 2)
            exps(0, 0)

            def pair(i):
                t0 = i * 2
                m = i * 3 + (QKV + 3)
                probs_out(t0, 0)
                w_hi(m + 1, 1, i * 16 + 80)
                act.wait_ge(u_ready, i + 1)
                projection_out(m, hcb[:, 0, :])
                exps(t0 + 1, 1)
                w_hi(m + 2, 2, i * 16 + 80)
                projection_out(m + 1, hcb[:, 1, :])
                probs_out(t0 + 1, 1)
                act.wait_ge(sq_ready, i + 1)
                projection_out(m + 2, hcb[:, 2, :], range(1))
                exps(t0 + 2, 0)
                if not isinstance(i, int):
                    w_hi(m + 3, 0, i * 16 + 112)
                projection_out(m + 2, hcb[:, 2, :], range(1, NB))

            def w_out_hi(lo, hi):
                act.wait_ge(run_done, NB * CHUNKS)
                for c in range(lo, hi):
                    act.wait_ge(w_arrived[c % WB], arrived_in(CHUNKS + c))
                    act.copy(w_oh[:, c, :], w_raw[c % WB][:, :]).then_inc(w_hi_ready, 1)

            with act.Fori(0, CC - 2) as i:
                pair(i)
            pair(CC - 2)
            probs_out(TILES - 2, 0)
            exps(TILES - 1, 1)
            w_out_hi(0, 3)
            probs_out(TILES - 1, 1)
            w_out_hi(3, 6)

            def stage(t, k):
                n = rows_of(t)
                if not isinstance(t, int) or t >= 2:
                    act.wait_ge(out_done, t - 1)
                act.sem_inc(act_held, 1)
                act.copy(mix_h[k][:, :, 0:n], mixedT[:, :, cols(t)]).then_inc(mix_hi_ready, 1)

            def norm2(t, k):
                n = rows_of(t)
                act.wait_ge(x2_ready, t + 1)
                squares(1, t, x2[0:n, t, :] if isinstance(t, int) else x2[:, ds(t, 1), :].rearrange("p o d -> p (o d)"), junk, ms2_ready, n)
                if not isinstance(t, int) or t + 2 <= TILES:
                    stage(t + 2, k)
                act.wait_ge(xn2_turned, t + 1)
                act.copy(xn2T[:, :, 0:n], bank[:, 4:6, :].rearrange("p b (c t) -> p (b c) t", t=P)[:, :, 0:n]).then_inc(xn2T_ready, 1)

            act.wait_ge(conv_ready, 2 * CC)
            act.wait_ge(atT_ready, TILES)
            stage(0, 0)
            w_out_hi(6, KC)
            stage(1, 1)
            for t in range(2):
                norm2(t, t % 2)
            with act.Fori(1, TILES // 2 - 1) as i:
                for k in range(2):
                    norm2(i * 2 + k, k)
            for t in range(TILES - 2, ALLT):
                norm2(t, t % 2)

            act.wait_ge(r_shifted, 2)
            act.activation(r4[4][:, :, :], r4[4][:, :, :], ACT.Exp).then_inc(r_exp_ready, 1)
            act.activation(r9[5][:, :], r9[5][:, :], ACT.Exp).then_inc(r_exp_ready, 1)

            def w_piece_hi(j, q, at):
                act.wait_ge(w_arrived[piece_buf(q)], piece_arrived(j, q))
                act.sem_inc(act_held, 1)
                act.copy(eh[:, ds(at + q * D, D)], piece_in[piece_buf(q)][:, :]).then_inc(w_hi_ready, 1)

            def x_hi(u):
                if not isinstance(u, int) or u >= 1:
                    act.wait_ge(h_done, u)
                act.wait_ge(xg_turned, u + 1)
                act.copy(xgh[:, :, :], bank[:, 0:2, :].rearrange("p b (c t) -> p (b c) t", t=P)).then_inc(xg_hi_ready, 1)

            def silus(u, k):
                act.wait_ge(h_done, u + 1)
                act.activation(silu[k], bank[:, 2 + k, 0:FE], ACT.Silu).then_inc(silu_ready, 1)

            def hid_hi(u):
                if not isinstance(u, int) or u >= 1:
                    act.wait_ge(y_done, u * 2)
                act.wait_ge(hid_turned, u + 1)
                act.copy(hTh[:, :, :], bank[:, 4, 0:FE].rearrange("p (c t) -> p c t", c=FC)).then_inc(hid_hi_ready, 1)

            def y_out(u, k):
                if not isinstance(u, int) or u >= 2:
                    act.wait_ge(y_stored[k], u // 2 * 16 if isinstance(u, int) else (u - k) * 8)
                act.wait_ge(y_done, u * 2 + 1)
                act.copy(y_sb[k][:, 0:512], bank[:, 5, :]).then_inc(y_left_ready, 1)

            def tile(u, k):
                packed = act.value_load(plan[0:1, ds(u + PL_TILE, 1)], min_val=0, max_val=2 * GATE_UP_TOO - 1)
                j = packed & (NE - 1)
                at = (packed & 1) * EW
                hid_hi(u)
                with act.If((packed & DOWN_TOO) > 0):
                    if not isinstance(u, int) or u >= 1:
                        act.wait_ge(y_done, u * 2)
                        act.sem_inc(act_held, 1)
                    for q in range(GU, PIECES):
                        w_piece_hi(j + 1, q, at * -1 + EW)
                with act.If((packed & GATE_UP_TOO) > 0):
                    act.wait_ge(h_done, u + 1)
                    act.sem_inc(act_held, 1)
                    for q in range(GU_FIRST):
                        w_piece_hi(j + 2, q, at)
                silus(u + 1, 1 - k)
                x_hi(u + 2)
                with act.If((packed & GATE_UP_TOO) > 0):
                    for q in range(GU_FIRST, GU):
                        w_piece_hi(j + 2, q, at)
                y_out(u, k)

            act.wait_ge(out_done, ALLT)
            for q in range(PIECES):
                w_piece_hi(0, q, 0)
            x_hi(0)
            act.wait_ge(table_done, 1)
            for q in range(GU):
                w_piece_hi(1, q, EW)
            silus(0, 0)
            x_hi(1)
            act.wait_ge(plan_ready, 1)
            tiles_used = act.value_load(plan[0:1, PL_TILES:PL_TILES + 1], min_val=LEAST_TILES, max_val=SLOT_TILES)
            tile(0, 0)
            tile(1, 1)
            with act.Fori(1, LEAST_TILES // 2) as i:
                for k in range(2):
                    tile(i * 2 + k, k)
            with act.Fori(LEAST_TILES // 2, SLOT_TILES // 2) as i:
                for k in range(2):
                    with act.If(i * 2 + k < tiles_used):
                        tile(i * 2 + k, k)
                        act.sem_inc(act_held, 1)

            def norm3(t):
                n = rows_of(t)
                act.wait_ge(x3_ready, t + 1)
                squares(2, t, x2[0:n, t, :] if isinstance(t, int) else x2[:, ds(t, 1), :].rearrange("p o d -> p (o d)"), junk, ms3_ready, n)

            norm3(0)
            with act.Fori(1, TILES) as t:
                norm3(t)
            norm3(TILES)

        @block.tensor
        def _(pe):
            def late(t, least=1):
                return not isinstance(t, int) or t >= least

            def turn_x(t):
                n = rows_of(t)
                k = t % 2
                pe.wait_ge(x_scaled, t + 1)
                if t >= 2:
                    pe.wait_ge(xnT_ready, t - 1)
                for c in range(KC):
                    mm = pe.transpose(bank[:, 2 * k + c // 4, (c % 4) * P:(c % 4) * P + n], x_sc[k][0:n, c * P:(c + 1) * P], ident[0:n, 0:n])
                mm.then_inc(x_turned, 1)

            def product(out, hl, rhs_h, rhs_l, n, chunks=KC, first_chunk=None):
                passes = [(hl[1], rhs_h), (hl[0], rhs_l), (hl[0], rhs_h)]
                for c in range(chunks):
                    if first_chunk is not None:
                        pe.wait_ge(w_lo_ready, first_chunk + c + 1)
                    for x, (lhs, rhs) in enumerate(passes):
                        mm = pe.matmul(out, lhs[:, c, 0:n], rhs(c), start=c == 0 and x == 0, stop=c == chunks - 1 and x == 2)
                return mm

            def project_run(m, b, n):
                if late(m):
                    pe.wait_ge(run_out, m * NB + (n + 1 - NB))
                at = slice(n * RUN, (n + 1) * RUN)
                product(bank[:, 5 + n, 0:RUN], (wh[b], wl[b]), lambda c: xTh[:, c, at], lambda c: xTl[:, c, at], P).then_inc(run_done, 1)

            def project(m, b):
                pe.wait_ge(w_lo_ready, m + 1)
                for n in range(NB):
                    project_run(m, b, n)

            pe.wait_ge(const_made, 2)
            for t in range(7):
                turn_x(t)
            pe.wait_ge(xnT_ready, -(-RUN // P))
            pe.wait_ge(w_lo_ready, 1)
            project_run(0, 0, 0)
            for t in range(7, ALLT):
                turn_x(t)
            pe.wait_ge(hist_arrived, 16)
            for c in range(CC):
                mm = pe.transpose(bank[:, 4, c * 2 * NS:(c + 1) * 2 * NS], hist[:, c * P:(c + 1) * P], ident[0:2 * NS, 0:2 * NS])
            mm.then_inc(hist_turned, 1)
            pe.wait_ge(xnT_ready, ALLT)
            project_run(0, 0, 1)
            project_run(0, 0, 2)
            pe.wait_ge(cache_arrived, 32)
            for n in range(NS):
                mm = pe.transpose(bank[:, n // 4, (n % 4) * P:(n % 4 + 1) * P], ck[:, n, :], ident[:, :])
            mm.then_inc(ck_turned, 1)
            for m in range(1, QKV):
                project(m, m % WB)

            pe.wait_ge(run_out, NB * QKV)
            pe.wait_ge(kTs_ready, 1)
            for b in range(TILES):
                mm = pe.transpose(bank[:, b // 4, (b % 4) * P:(b % 4 + 1) * P], vT[:, b * P:(b + 1) * P], ident[:, :])
            mm.then_inc(v_turned, 1)
            pe.wait_ge(hist_ready, 1)
            pe.transpose(bank[:, 4, 0:P], kT[:, SEQ - P:SEQ], ident[:, :])
            for j, src in enumerate((kT, vT)):
                mm = pe.transpose(bank[0:NS, 4, (1 + j) * P:(2 + j) * P], src[:, SEQ:NT], ident[:, :])
            mm.then_inc(kv_turned, 1)

            project(6, 0)
            pe.wait_ge(qbd_ready, 2)
            pe.wait_ge(kv_rows_ready, 3)
            for n in range(NS):
                pe.matmul(bank[0:NH, 2 + n // 4, (n % 4) * P:(n % 4 + 1) * P], qbd[:, n, :], kTs[:, n, :], start=True, stop=True)
                mm = pe.matmul(bank[0:NH, 4, n:n + 1], qbd[:, n, :], kT[:, SEQ + n:SEQ + n + 1], start=True, stop=True)
            mm.then_inc(s_scored, 1)
            project(7, 1)
            pe.wait_ge(s_exp_ready, 2)
            pe.wait_ge(v_ready, 1)
            for n in range(NS):
                pe.transpose(bank[:, 0, n * NH:(n + 1) * NH], s_p[:, n, 0:P], ident[0:NH, 0:NH])
            pe.transpose(bank[0:NS, 1, 0:NH], s_p[:, :, P], ident[0:NH, 0:NH]).then_inc(s_turned, 1)
            pe.wait_ge(w_lo_ready, 9)
            project_run(8, 2, 0)
            pe.wait_ge(s_pT_ready, 2)
            for n in range(NS):
                out = bank[0:NH, 2 + n // 4, (n % 4) * P:(n % 4 + 1) * P]
                pe.matmul(out, s_pT[:, n, :], cv[:, n, :], start=True, stop=False)
                mm = pe.matmul(out, s_z[:, n, :], kvs_rows[:, 1, :], start=False, stop=True)
            mm.then_inc(s_pv_done, 1)
            project_run(8, 2, 1)
            pe.wait_ge(s_n_ready, 1)
            for n in range(NS):
                mm = pe.transpose(bank[0:HD, 4, n * NH:(n + 1) * NH], s_n[:, n, :], ident[0:NH, 0:NH])
            mm.then_inc(s_n_turned, 1)

            def scores(t):
                pe.wait_ge(staged, t * 2 + 2)
                if late(t):
                    pe.wait_ge(scores_read, t * 2)
                for half in range(2):
                    for j in range(2):
                        for g in range(NKV):
                            mm = pe.matmul(bank[:, 2 * half + g, j * 2 * P:(j + 1) * 2 * P], qs[g * HD:(g + 1) * HD, 2 * half + j, :],
                                           kb[g * HD:(g + 1) * HD, :], start=True, stop=True)
                    mm.then_inc(scores_done, 1)

            def weigh(t, k):
                pe.wait_ge(exp_ready, t + 1)
                for q in range(4):
                    if late(t) or q >= 2:
                        pe.wait_ge(pT_ready, t * 4 + (q - 1))
                    for x in range(2):
                        for c in range(2):
                            mm = pe.transpose(bank[:, 2 + q % 2, (2 * x + c) * P:(2 * x + c + 1) * P],
                                              prob[k][:, 2 * q + x, c * P:(c + 1) * P], ident[:, :])
                    mm.then_inc(p_turned, 1)
                if late(t):
                    pe.wait_ge(atT_ready, t)
                pe.wait_ge(pT_ready, t * 4 + 4)
                for h in range(NH):
                    g = h // 2 % 2
                    for c in range(2):
                        v = v_tok[:, t + c, g * HD:(g + 1) * HD] if isinstance(t, int) else \
                            v_tok[:, :, :].rearrange("p b f -> p (b f)")[:, ds(t * P + (c * P + g * HD), HD)]
                        mm = pe.matmul(bank[:, 4, h * HD:(h + 1) * HD], pTs[:, h, c, :], v, start=c == 0, stop=c == 1)
                mm.then_inc(pv_done, 1)

            def turn_attention(t):
                pe.wait_ge(at_n_ready, t + 1)
                for c in range(AC):
                    first_h = (c % 2) * 4 + (c // 2) * 2
                    mm = pe.transpose(bank[:, 4, c * P:(c + 1) * P], at_n[:, first_h * HD:first_h * HD + P], ident[:, :])
                mm.then_inc(at_turned, 1)

            last_tokens = NT - P

            def conv_means(i):
                pe.wait_ge(sq_ready, i + 1)
                for t in range(ALLT):
                    at = t * P if t < TILES else last_tokens
                    mm = pe.matmul(bank[:, 2, 2 * t:2 * t + 2], sqT[:, at:at + P], group_mean[:, :], start=True, stop=True)
                mm.then_inc(cms_done, 1)

            def conv_scales(i, t1):
                pe.wait_ge(crs_row_ready, i + 1)
                pe.wait_ge(scores_read, t1 * 2 + 2)
                for t in range(ALLT):
                    out = bank[:, t // 4, (t % 4) * P:(t % 4 + 1) * P] if t < TILES else bank[:, 2, P:2 * P]
                    mm = pe.transpose(out, crs_row[:, t * P:(t + 1) * P], ident[:, :])
                mm.then_inc(crs_turned, 1)

            def pair(i, last=False):
                t0 = i * 2
                m = i * 3 + (QKV + 3)
                weigh(t0, 0)
                scores(t0 + 1)
                if last:
                    turn_attention(t0)
                    pe.wait_ge(scores_read, t0 * 2 + 4)
                    conv_means(i)
                    pe.wait_ge(cms_ready, i + 1)
                    weigh(t0 + 1, 1)
                    pe.wait_ge(pT_ready, t0 * 4 + 8)
                    conv_scales(i, t0 + 1)
                    turn_attention(t0 + 1)
                    return
                project(m, 0)
                pe.wait_ge(scores_read, t0 * 2 + 4)
                conv_means(i)
                pe.wait_ge(w_lo_ready, m + 2)
                project_run(m + 1, 1, 0)
                project_run(m + 1, 1, 1)
                turn_attention(t0)
                conv_scales(i, t0 + 1)
                project_run(m + 1, 1, 2)
                pe.wait_ge(conv_ready, i * 2 + 2)
                weigh(t0 + 1, 1)
                scores(t0 + 2)
                project(m + 2, 2)
                turn_attention(t0 + 1)

            pe.wait_ge(const_made, CONST_ALL)
            scores(0)
            project_run(8, 2, 2)
            pe.wait_ge(s_mixed, 2)
            pair(0)
            with pe.Fori(1, CC - 1) as i:
                pair(i)
            pair(CC - 1, True)
            for c in range(CC):
                mm = pe.transpose(bank[0:2 + NS, 3, c * P:(c + 1) * P], u_last[:, c, :], ident[:, :])
            mm.then_inc(u_turned, 1)

            def project_out(t, k, halves=range(2)):
                n = rows_of(t)
                if 0 in halves:
                    pe.wait_ge(mix_staged, t + 1)
                    if late(t, 2):
                        pe.wait_ge(x2_ready, t - 1)
                for half in halves:
                    at = slice(half * 512, (half + 1) * 512)
                    mm = product(bank[0:n, 2 * k + half, :], (mix_h[k], mix_l[k]), lambda c: w_oh[:, c, at], lambda c: w_ol[:, c, at], n,
                                 first_chunk=None if late(t) else CHUNKS)
                if 1 in halves:
                    mm.then_inc(out_done, 1)

            def turn_xn2(t, k):
                n = rows_of(t)
                pe.wait_ge(xn2_ready, t + 1)
                for c in range(KC):
                    mm = pe.transpose(bank[:, 4 + c // 4, (c % 4) * P:(c % 4) * P + n], xn2[k][0:n, c * P:(c + 1) * P], ident[0:n, 0:n])
                mm.then_inc(xn2_turned, 1)

            def route(t):
                n = rows_of(t)
                pe.wait_ge(xn2T_ready, t + 1)
                if late(t):
                    pe.wait_ge(logits_ready, t)
                for c in range(KC):
                    mm = pe.matmul(bank[0:n, 7, 0:NR], xn2T[:, c, 0:n], w_r[:, c, :], start=c == 0, stop=c == KC - 1)
                mm.then_inc(routed, 1)

            pe.wait_ge(u_rows_ready, 1)
            pe.wait_ge(late_const_in, 16 * 4)
            def tiles_out(t, k):
                project_out(t + 1, 1 - k, range(1))
                if late(t):
                    route(t - 1)
                project_out(t + 1, 1 - k, range(1, 2))
                turn_xn2(t, k)

            project_out(0, 0)
            tiles_out(0, 0)
            tiles_out(1, 1)
            with pe.Fori(1, TILES // 2) as i:
                for k in range(2):
                    tiles_out(i * 2 + k, k)
            route(TILES - 1)
            turn_xn2(TILES, 0)
            route(TILES)

            pe.wait_ge(picks_ready, 1)
            pe.matmul(bank[:, 0, 0:ALLT * NE], earlier[:, :], both.rearrange("p t e -> p (t e)"), start=True, stop=False)
            pe.matmul(bank[:, 0, 0:ALLT * NE], ones[:, :], before[:, 0:ALLT, :].rearrange("p t e -> p (t e)"), start=False, stop=True)
            pe.matmul(bank[:, 1, 0:NE], ones[:, :], before[:, ALLT, :], start=True, stop=True).then_inc(places_done, 1)
            for j in range(2 * ALLT):
                if j % ALLT == 0:
                    pe.wait_ge(table_in_ready, j // ALLT + 1)
                    pe.wait_ge(tokens_in_ready, j // ALLT + 1)
                mm = pe.matmul(bank[:, 2, 0:3 * PLANNED], row_hot[:, j, :], payload[:, j, :, :].rearrange("p v u -> p (v u)"),
                               start=j == 0, stop=j == 2 * ALLT - 1)
            mm.then_inc(table_done, 1)

            def turn_tokens(u, k, arrived):
                pe.wait_ge(x_gathered[k], arrived)
                if late(u):
                    pe.wait_ge(xgT_ready, u)
                for c in range(KC):
                    mm = pe.transpose(bank[:, c // 4, (c % 4) * P:(c % 4 + 1) * P], xg[k][:, c * P:(c + 1) * P], ident[:, :])
                mm.then_inc(xg_turned, 1)

            def gate_and_up(u, k, j, at):
                pe.wait_ge(xgT_ready, u + 1)
                if late(u, 2):
                    pe.wait_ge(hid_ready, u - 1)
                pe.wait_ge(w_lo_ready, j * PIECES + (PRIOR + GU))
                gu = [lambda c, w=w: w[:, ds(at, EW)].rearrange("p (v c f) -> p v c f", v=3, c=KC)[:, 0:2, c, :] for w in (eh, el)]
                product(bank[:, 2 + k, :].rearrange("p (v f) -> p v f", v=2), (xgh, xgl), gu[0], gu[1], P).then_inc(h_done, 1)

            def turn_hidden(u, k):
                pe.wait_ge(hid_ready, u + 1)
                if late(u):
                    pe.wait_ge(hidT_ready, u)
                for c in range(FC):
                    mm = pe.transpose(bank[:, 4, c * P:(c + 1) * P], hid[k][:, c, :], ident[:, :])
                mm.then_inc(hid_turned, 1)

            def down(u, j, at):
                pe.wait_ge(hidT_ready, u + 1)
                pe.wait_ge(w_lo_ready, j * PIECES + (PRIOR + PIECES))
                for half in range(2):
                    if late(u):
                        pe.wait_ge((y_left_ready, y_right_ready)[half], u)
                    dn = [lambda c, w=w: w[:, ds(at + ((GU + c) * D + half * 512), 512)] for w in (eh, el)]
                    product(bank[:, 5 + half, :], (hTh, hTl), dn[0], dn[1], P, FC).then_inc(y_done, 1)

            def tile(u, i, k):
                packed = pe.value_load(plan[0:1, ds(u + PL_TILE, 1)], min_val=0, max_val=2 * GATE_UP_TOO - 1)
                j = packed & (NE - 1)
                j_next = (packed >> J_BITS) & (NE - 1)
                turn_hidden(u, k)
                gate_and_up(u + 1, 1 - k, j_next, (j_next & 1) * EW)
                turn_tokens(u + 2, k, i * 16 + 32)
                down(u, j, (j & 1) * EW)

            turn_tokens(0, 0, 16)
            gate_and_up(0, 0, 0, 0)
            pe.wait_ge(plan_ready, 1)
            tiles_used = pe.value_load(plan[0:1, PL_TILES:PL_TILES + 1], min_val=LEAST_TILES, max_val=SLOT_TILES)
            turn_tokens(1, 1, 16)
            tile(0, 0, 0)
            tile(1, 0, 1)
            with pe.Fori(1, LEAST_TILES // 2) as i:
                for k in range(2):
                    tile(i * 2 + k, i, k)
            with pe.Fori(LEAST_TILES // 2, SLOT_TILES // 2) as i:
                for k in range(2):
                    with pe.If(i * 2 + k < tiles_used):
                        tile(i * 2 + k, i, k)

        @block.vector
        def _(dve):
            st = Steps(dve, dve_step)

            def bc(ap, n):
                return ap.unsqueeze(2).broadcast_to([ap.shape[0], ap.shape[1], n])

            def late(t, least=1):
                return not isinstance(t, int) or t >= least

            def scale_x(t):
                n = rows_of(t)
                if t >= 2:
                    dve.wait_ge(x_turned, t - 1)
                dve.wait_ge(rstd1_ready, t + 1)
                dve.scalar_tensor_tensor(out=x_sc[t % 2][0:n, :], in0=x_in[t % XB][0:n, :], scalar=rstd[0][0:n, col(t)], in1=g1[0:n, :],
                                         op0=ALU.mult, op1=ALU.mult).then_inc(x_scaled, 1)

            def x_lo(t):
                n = rows_of(t)
                k = t % 2
                dve.wait_ge(x_hi_ready, t + 1)
                dve.tensor_tensor(xTl[:, :, cols(t)], bank[:, 2 * k:2 * k + 2, :].rearrange("p b (c t) -> p (b c) t", t=P)[:, :, 0:n],
                                  xTh[:, :, cols(t)].bitcast(F32), ALU.subtract).then_inc(xnT_ready, 1)

            def w_lo(m, b):
                dve.wait_ge(w_hi_ready, m + 1)
                dve.tensor_tensor(wl[b][:, :, :], w_raw[b][:, :].rearrange("p (c f) -> p c f", c=KC), wh[b][:, :, :].bitcast(F32),
                                  ALU.subtract).then_inc(w_lo_ready, 1)

            dve.wait_ge(g1_in, 16)
            for t in range(ALLT):
                scale_x(t)
                if t >= 1:
                    x_lo(t - 1)
                if t == 5:
                    w_lo(0, 0)
            x_lo(TILES)
            dve.wait_ge(const_in, 16 * 9)
            st.then(dve.tensor_scalar(nsink[:, :], sink_in[:, :], -1.0, None, ALU.mult))
            st.then(dve.tensor_scalar(nsink_s[:, :], sink_in_s[:, :], -1.0, None, ALU.mult))
            w_lo(1, 1)
            dve.wait_ge(hist_turned, 1)
            dve.tensor_copy(histT[:, :, :], bank[:, 4, 0:CC * 2 * NS].rearrange("p (c n) -> p c n", c=CC)).then_inc(hist_ready, 1)
            for m in range(2, QKV + 1):
                w_lo(m, m % WB)

            dve.wait_ge(v_turned, 1)
            dve.tensor_copy(kv_rows[:, 1, :], bank[:, 1, 3 * P:4 * P]).then_inc(kv_rows_ready, 1)
            dve.wait_ge(kv_turned, 1)
            dve.tensor_copy(kv_rows[:, 0, :], bank[:, 4, 0:P]).then_inc(kv_rows_ready, 1)
            dve.tensor_copy(kvs_rows, bank[0:NS, 4, P:3 * P].rearrange("p (j f) -> p j f", j=2)).then_inc(kv_rows_ready, 1)
            dve.wait_ge(const_made, CONST_ALL)
            dve.wait_ge(run_out, NB * QKV)
            for g in range(NKV):
                h = slice(g * HD, (g + 1) * HD)
                dve.tensor_scalar(qbd[h, :, 4 * g:4 * g + 4], mixedT[h, 0:AC, SEQ:NT].rearrange("p j n -> p n j"),
                                  HD ** -0.5, None, ALU.mult).then_inc(qbd_ready, 1)
            dve.tensor_copy(v_tok[:, 1:ALLT, :], bank[:, 0:2, :].rearrange("p b (c t) -> p (b c) t", t=P)).then_inc(v_ready, 1)
            w_lo(7, 1)

            dve.wait_ge(s_scored, 1)
            st.then(dve.tensor_copy(s_sc[:, :, 0:P], bank[0:NH, 2:4, :].rearrange("p b (n t) -> p (b n) t", t=P)))
            st.then(dve.tensor_copy(s_sc[:, :, P], bank[0:NH, 4, 0:NS]))
            st.then(dve.tensor_reduce(s_mx[:, :], s_sc, AX, ALU.max))
            st.then(dve.scalar_tensor_tensor(out=s_nm[:, :], in0=s_mx[:, :], scalar=-1.0, in1=nsink_s[:, :].broadcast_to([NH, NS]),
                                             op0=ALU.mult, op1=ALU.min))
            st.then(dve.tensor_tensor(s_es[:, :], s_nm[:, :], nsink_s[:, :].broadcast_to([NH, NS]), ALU.subtract))
            dve.tensor_tensor(s_sc, s_sc, bc(s_nm[:, :], P + 1), ALU.add).then_inc(s_shifted, 1)
            w_lo(8, 2)
            dve.wait_ge(s_exp_ready, 2)
            st.then(dve.tensor_reduce(s_dn[:, :], s_p, AX, ALU.add))
            st.then(dve.tensor_tensor(s_dn[:, :], s_dn[:, :], s_es[:, :], ALU.add))
            st.then(dve.reciprocal(s_dn[:, :], s_dn[:, :]))
            dve.wait_ge(s_turned, 1)
            dve.tensor_copy(s_pT[:, :, :], bank[:, 0, 0:NS * NH].rearrange("p (n h) -> p n h", h=NH)).then_inc(s_pT_ready, 1)
            dve.tensor_tensor(s_z[:, :, :], bank[0:NS, 1, 0:NH].unsqueeze(1).broadcast_to([NS, NS, NH]), bc(ident[0:NS, 0:NS], NH),
                              ALU.mult).then_inc(s_pT_ready, 1)
            dve.wait_ge(s_pv_done, 1)
            st.then(dve.tensor_tensor(s_o2, bank[0:NH, 2:4, :].rearrange("p b (n f) -> p (b n) f", f=P),
                                      half_mask[:, :].unsqueeze(1).broadcast_to([NH, NS, P]), ALU.mult))
            st.then(dve.tensor_tensor(s_o, s_o2[:, :, 0:HD], s_o2[:, :, HD:P], ALU.add))
            st.then(dve.tensor_tensor(s_o, s_o, bc(s_dn[:, :], HD), ALU.mult))
            st.then(dve.tensor_tensor(s_sq, s_o, s_o, ALU.mult))
            st.then(dve.tensor_reduce(s_ms[:, :], s_sq, AX, ALU.add))
            dve.tensor_scalar(s_ms[:, :], s_ms[:, :], 1.0 / HD, EPS, ALU.mult, ALU.add).then_inc(s_ms_ready, 1)
            dve.wait_ge(s_r_ready, 1)
            st.then(dve.tensor_tensor(s_n, s_o, bc(s_r[:, :], HD), ALU.mult))
            dve.tensor_tensor(s_n, s_n, ga_s[:, :].unsqueeze(1).broadcast_to([NH, NS, HD]), ALU.mult).then_inc(s_n_ready, 1)

            def stage(t):
                if late(t):
                    dve.wait_ge(scores_done, t * 2)
                dve.tensor_scalar(qs[:, :, :], mixedT[:, 0:AC, cols(t)], HD ** -0.5, None, ALU.mult).then_inc(staged, 1)
                if isinstance(t, int) and t == 0:
                    band, to = kT[:, 0:P].unsqueeze(1).broadcast_to([P, 2, P]), kb[:, :].rearrange("p (h c) -> p h c", h=2)
                else:
                    band, to = kT[:, ds(t * P - P, 2 * P)], kb[:, :]
                dve.tensor_scalar(to, band, 1.0, None, ALU.mult).then_inc(staged, 1)

            def soften(t, k):
                mask = band_mask[:, 0 if isinstance(t, int) and t == 0 else 1, :]
                for half in range(2):
                    dve.wait_ge(scores_done, t * 2 + (half + 1))
                    dve.tensor_tensor(prob[k][:, 4 * half:4 * half + 4, :], bank[:, 2 * half:2 * half + 2, :].rearrange("p b (x c) -> p (b x) c", x=2),
                                      mask.unsqueeze(1).broadcast_to([P, 4, 2 * P]), ALU.add).then_inc(scores_read, 1)
                dve.wait_ge(scores_read, t * 2 + 2)
                st.then(dve.tensor_reduce(mx[:, :], prob[k][:, :, :], AX, ALU.max))
                dve.scalar_tensor_tensor(out=nm[k][:, :], in0=mx[:, :], scalar=-1.0, in1=nsink[:, :], op0=ALU.mult, op1=ALU.min).then_inc(nm_ready, 1)
                dve.wait_ge(nm_ready, t + 1)
                dve.tensor_tensor(sd[k][:, :], nm[k][:, :], nsink[:, :], ALU.subtract).then_inc(sd_ready, 1)

            def norm_heads(t, k):
                dve.wait_ge(exp_ready, t + 1)
                st.then(dve.tensor_tensor(den[k][:, :], den[k][:, :], es[k][:, :], ALU.add))
                st.then(dve.reciprocal(rden[:, :], den[k][:, :]))
                dve.wait_ge(pv_done, t + 1)
                o = at_o[:, :].rearrange("p (h d) -> p h d", d=HD)
                st.then(dve.tensor_tensor(o, bank[:, 4, :].rearrange("p (h d) -> p h d", d=HD), bc(rden[:, :], HD), ALU.mult))
                st.then(dve.tensor_tensor(at_sq[:, :], at_o[:, :], at_o[:, :], ALU.mult))
                st.then(dve.tensor_reduce(at_ms[:, :], at_sq[:, :].rearrange("p (h d) -> p h d", d=HD), AX, ALU.add))
                dve.tensor_scalar(at_ms[:, :], at_ms[:, :], 1.0 / HD, EPS, ALU.mult, ALU.add).then_inc(at_ms_ready, 1)

            def scale_heads(t):
                dve.wait_ge(at_r_ready, t + 1)
                o = at_o[:, :].rearrange("p (h d) -> p h d", d=HD)
                dve.tensor_tensor(at_n[:, :].rearrange("p (h d) -> p h d", d=HD), o, bc(at_r[:, :], HD), ALU.mult).then_inc(at_n_ready, 1)

            def attention_out(t):
                dve.wait_ge(at_turned, t + 1)
                dve.tensor_tensor(mixedT[:, 0:AC, cols(t)], bank[:, 4, :].rearrange("p (c t) -> p c t", t=P), bc(ga[:, :], P), ALU.mult).then_inc(atT_ready, 1)

            def taps(i):
                dve.wait_ge(run_out, i * (3 * NB) + NB * (QKV + 2))
                cwi = cwg[:, i, :] if isinstance(i, int) else cwg[:, ds(i, 1), :].rearrange("p o j -> p (o j)")
                st.then(dve.tensor_scalar(cw[:, :], cwi, 1.0, None, ALU.mult))
                dve.tensor_tensor(uT[:, 2:2 + NT], hcb[:, 0, :], hcb[:, 1, :], ALU.mult).then_inc(u_ready, 1)
                dve.wait_ge(u_ready, i + 1)
                st.then(dve.tensor_scalar(zT[:, 0:SEQ], uT[:, 0:SEQ], cw[:, 0:1], None, ALU.mult))
                for j in (1, 2):
                    st.then(dve.scalar_tensor_tensor(out=zT[:, 0:SEQ], in0=uT[:, j:j + SEQ], scalar=cw[:, j:j + 1], in1=zT[:, 0:SEQ],
                                                     op0=ALU.mult, op1=ALU.add))
                h = (histT[:, i, :] if isinstance(i, int) else histT[:, ds(i, 1), :].rearrange("p o n -> p (o n)")).rearrange("p (n j) -> p n j", j=2)
                z = zT[:, SEQ:NT]
                st.then(dve.tensor_scalar(z, h[:, :, 0], cw[:, 0:1], None, ALU.mult))
                st.then(dve.scalar_tensor_tensor(out=z, in0=h[:, :, 1], scalar=cw[:, 1:2], in1=z, op0=ALU.mult, op1=ALU.add))
                st.then(dve.scalar_tensor_tensor(out=z, in0=uT[:, 2 + SEQ:2 + NT], scalar=cw[:, 2:3], in1=z, op0=ALU.mult, op1=ALU.add))
                last = u_last[:, i, :] if isinstance(i, int) else u_last[:, ds(i, 1), :].rearrange("p o n -> p (o n)")
                st.then(dve.tensor_scalar(last, uT[:, SEQ:2 + NT], 1.0, None, ALU.mult))

            def gated(i):
                dve.wait_ge(run_out, i * (3 * NB) + NB * (QKV + 3))
                st.then(dve.tensor_tensor(zT[:, :], zT[:, :], hcb[:, 2, :], ALU.mult))
                dve.tensor_tensor(sqT[:, 0:NT], zT[:, :], zT[:, :], ALU.mult).then_inc(sq_ready, 1)

            def conv_means_out(i):
                dve.wait_ge(cms_done, i + 1)
                dve.tensor_scalar(cms[:, :], bank[:, 2, 0:2 * ALLT], EPS, None, ALU.add).then_inc(cms_ready, 1)

            def spread_rstd(i):
                dve.wait_ge(crs_ready, i + 1)
                dve.tensor_copy(crs_row[:, :].rearrange("p (m d) -> p m d", d=HD), bc(crs[:, :], HD)).then_inc(crs_row_ready, 1)

            def conv_out(i):
                dve.wait_ge(crs_turned, i + 1)
                at = mixedT[:, AC + i, :] if isinstance(i, int) else mixedT[:, ds(i + AC, 1), :].rearrange("p o t -> p (o t)")
                dve.scalar_tensor_tensor(out=at[:, 0:SEQ].rearrange("p (b t) -> p b t", b=2), in0=bank[:, 0:2, :], scalar=cw[:, 3:4],
                                         in1=zT[:, 0:SEQ].rearrange("p (b t) -> p b t", b=2), op0=ALU.mult, op1=ALU.mult).then_inc(conv_ready, 1)
                dve.scalar_tensor_tensor(out=at[:, SEQ:NT], in0=bank[:, 2, 2 * P - NS:2 * P], scalar=cw[:, 3:4], in1=zT[:, SEQ:NT],
                                         op0=ALU.mult, op1=ALU.mult).then_inc(conv_ready, 1)

            def pair(i):
                t0 = i * 2
                m = i * 3 + (QKV + 3)
                stage(t0 + 1)
                taps(i)
                w_lo(m + 1, 1)
                gated(i)
                soften(t0 + 1, 1)
                norm_heads(t0, 0)
                conv_means_out(i)
                scale_heads(t0)
                spread_rstd(i)
                w_lo(m + 2, 2)
                stage(t0 + 2)
                attention_out(t0)
                conv_out(i)
                norm_heads(t0 + 1, 1)
                soften(t0 + 2, 0)
                scale_heads(t0 + 1)
                if not isinstance(i, int) or i < CC - 2:
                    w_lo(m + 3, 0)
                attention_out(t0 + 1)

            def last_pair(i):
                t0 = i * 2
                stage(t0 + 1)
                taps(i)
                norm_heads(t0, 0)
                soften(t0 + 1, 1)
                scale_heads(t0)
                gated(i)
                conv_means_out(i)
                attention_out(t0)
                w_out_lo(0, 3)
                spread_rstd(i)
                norm_heads(t0 + 1, 1)
                conv_out(i)
                scale_heads(t0 + 1)
                attention_out(t0 + 1)

            def w_out_lo(lo, hi):
                dve.wait_ge(run_done, NB * CHUNKS)
                for c in range(lo, hi):
                    dve.wait_ge(w_hi_ready, CHUNKS + c + 1)
                    dve.tensor_tensor(w_ol[:, c, :], w_raw[c % WB][:, :], w_oh[:, c, :].bitcast(F32), ALU.subtract).then_inc(w_lo_ready, 1)

            stage(0)
            soften(0, 0)
            w_lo(9, 0)
            dve.wait_ge(s_n_turned, 1)
            turned = bank[0:HD, 4, 0:NS * NH].rearrange("p (n c x) -> p c n x", n=NS, x=2)
            for x in range(2):
                dve.tensor_copy(mixedT[x * HD:(x + 1) * HD, 0:AC, SEQ:NT], turned[:, :, :, x]).then_inc(s_mixed, 1)
            pair(0)
            st.loop(1, CC - 2, 2 + 10 + 8 + 1, pair)
            pair(CC - 2)
            last_pair(CC - 1)
            dve.wait_ge(u_turned, 1)
            dve.wait_ge(kvs_stored, 32)
            dve.tensor_copy(u_rows[:, :], bank[0:2 + NS, 3, :]).then_inc(u_rows_ready, 1)
            st.then(dve.memset(logits[:, :, :], 0.0))

            def x2_of(t):
                return x2[0:rows_of(t), t, :] if isinstance(t, int) else x2[:, ds(t, 1), :].rearrange("p o d -> p (o d)")

            def mix_lo(t, k):
                n = rows_of(t)
                dve.wait_ge(mix_hi_ready, t + 1)
                dve.tensor_tensor(mix_l[k][:, :, 0:n], mixedT[:, :, cols(t)], mix_h[k][:, :, 0:n].bitcast(F32), ALU.subtract).then_inc(mix_staged, 1)

            def residual(t, k, free):
                n = rows_of(t)
                dve.wait_ge(out_done, t + 1)
                dve.tensor_tensor(x2_of(t), bank[0:n, 2 * k:2 * k + 2, :].rearrange("p b d -> p (b d)"), x2_of(t), ALU.add).then_inc(x2_ready, 1)
                if not isinstance(t, int) or t + 2 <= TILES:
                    mix_lo(t + 2, k)
                dve.wait_ge(rstd2_ready, t + 1)
                if late(t, 2):
                    dve.wait_ge(xn2_stored[k], free)
                dve.scalar_tensor_tensor(out=xn2[k][0:n, :].rearrange("p (c q) -> p q c", c=KC), in0=x2_of(t).rearrange("p (q c) -> p q c", c=KC),
                                         scalar=rstd[1][0:n, col(t)], in1=g2[0:n, :].rearrange("p (q c) -> p q c", c=KC),
                                         op0=ALU.mult, op1=ALU.mult).then_inc(xn2_ready, 1)

            def logits_out(t):
                n = rows_of(t)
                dve.wait_ge(routed, t + 1)
                lt = logits[0:n, t, :] if isinstance(t, int) else logits[:, ds(t, 1), :].rearrange("p o r -> p (o r)")
                dve.tensor_tensor(lt, bank[0:n, 7, 0:NR], b_r[0:n, :], ALU.add).then_inc(logits_ready, 1)

            mix_lo(0, 0)
            w_out_lo(3, KC)
            mix_lo(1, 1)
            dve.wait_ge(x_again[0], 16)
            dve.wait_ge(g2_in, 16)
            dve.wait_ge(late_const_in, 16 * 4)
            residual(0, 0, 0)
            residual(1, 1, 0)
            logits_out(0)
            dve.wait_ge(x_again[1], 16 * 2)
            with dve.Fori(1, TILES // 2 - 1) as i:
                for k in range(2):
                    residual(i * 2 + k, k, i * 16)
                    logits_out(i * 2 + (k - 1))
            for t in range(TILES - 2, ALLT):
                residual(t, t % 2, 16 * (t // 2))
                logits_out(t - 1)
            logits_out(TILES)

            dve.wait_ge(logits_ready, ALLT)

            def first_of_max(vals, top, hot, a, b):
                st.then(dve.tensor_reduce(top, vals, AX, ALU.max))
                st.then(dve.tensor_tensor(a, vals, bc(top, EG), ALU.is_equal))
                st.then(dve.tensor_tensor(a, a, rev4[:, :, :], ALU.mult))
                st.then(dve.tensor_reduce(b, a, AX, ALU.max))
                st.then(dve.tensor_tensor(hot, a, bc(b, EG), ALU.is_equal))

            top_c, tmp9, top1, top2, denom, ratio, one_r = [r[:, :] for r in r9]
            hot_g, hot_1, fine, tmp4, shifted = [r[:, :, :] for r in r4]
            coarse = logits[:, :, 0:NG]
            first_of_max(coarse, top_c, hot_g, tmp4, tmp9)
            dve.tensor_tensor(shifted, coarse, bc(top_c, NG), ALU.subtract).then_inc(r_shifted, 1)
            g_e = "p t (g j) -> p t g j"
            st.then(dve.tensor_tensor(prod16.rearrange(g_e, g=NG), logits[:, :, NG:NR].rearrange(g_e, g=NG),
                                      hot_g.unsqueeze(3).broadcast_to([P, ALLT, NG, EG]), ALU.mult))
            st.then(dve.tensor_reduce(fine, prod16.rearrange("p t (g j) -> p t j g", g=NG), AX, ALU.add))
            first_of_max(fine, top1, hot_1, tmp4, tmp9)

            def picked(k, hot):
                st.then(dve.tensor_tensor(pick[:, k, :, :].rearrange(g_e, g=NG), hot_g.unsqueeze(3).broadcast_to([P, ALLT, NG, EG]),
                                          hot.unsqueeze(2).broadcast_to([P, ALLT, NG, EG]), ALU.mult))
                st.then(dve.tensor_tensor(pick[:, k, :, :], pick[:, k, :, :], bc(valid[:, :], NE), ALU.mult))

            picked(0, hot_1)
            st.then(dve.scalar_tensor_tensor(out=fine, in0=hot_1, scalar=LOWEST, in1=fine, op0=ALU.mult, op1=ALU.add))
            first_of_max(fine, top2, hot_1, tmp4, tmp9)
            dve.tensor_tensor(ratio, top2, top1, ALU.subtract).then_inc(r_shifted, 1)
            picked(1, hot_1)
            st.then(dve.tensor_tensor(both, pick[:, 0, :, :], pick[:, 1, :, :], ALU.add))
            st.along(dve.memset(before[:, 0, :], 0.0))
            src = both
            for n, sh in enumerate((1, 2, 4, 8)):
                dst = (place16, before[:, 1:ALLT + 1, :])[n % 2]
                st.along(dve.tensor_copy(dst[:, 0:sh, :], src[:, 0:sh, :]))
                ins = dve.tensor_tensor(dst[:, sh:ALLT, :], src[:, sh:ALLT, :], src[:, 0:ALLT - sh, :], ALU.add)
                if sh < 8:
                    st.then(ins)
                src = dst
            ins.then_inc(picks_ready, 1)
            dve.wait_ge(r_exp_ready, 2)
            st.then(dve.tensor_reduce(denom, shifted, AX, ALU.add))
            st.then(dve.tensor_scalar(one_r, ratio, 1.0, None, ALU.add))
            st.then(dve.tensor_tensor(denom, denom, one_r, ALU.mult))
            st.then(dve.reciprocal(gate[:, 0, :], denom))
            st.then(dve.tensor_tensor(gate[:, 1, :], gate[:, 0, :], ratio, ALU.mult))

            dve.wait_ge(places_done, 1)
            st.then(dve.tensor_copy(count[:, :], bank[:, 1, 0:NE]))
            st.then(dve.tensor_tensor(cmp9, bc(count[:, :], ALLT), steps128[:, :].unsqueeze(1).broadcast_to([P, NE, ALLT]), ALU.is_gt))
            st.then(dve.tensor_reduce(tiles_of[:, 0, :], cmp9, AX, ALU.add))
            st.then(dve.tensor_scalar(tiles_of[:, 1, :], tiles_of[:, 0, :], 0.0, None, ALU.is_gt))
            src = tiles_of
            for n, sh in enumerate((1, 2, 4, 8)):
                dst = scan[n % 2]
                st.along(dve.tensor_copy(dst[:, :, 0:sh], src[:, :, 0:sh]))
                st.then(dve.tensor_tensor(dst[:, :, sh:NE], src[:, :, sh:NE], src[:, :, 0:NE - sh], ALU.add))
                src = dst
            ends, order = src[:, 0, :], src[:, 1, :]
            by_place = [P, NE, NE]
            st.then(dve.tensor_tensor(cmp_j, order.unsqueeze(1).broadcast_to(by_place), bc(iota_row[:, 0:NE], NE), ALU.is_le))
            st.along(dve.tensor_copy(order_f[:, NE:NE + 1], order[:, NE - 1:NE]))
            st.then(dve.tensor_reduce(order_f[:, 0:NE], cmp_j, AX, ALU.add))
            dve.tensor_copy(order_i[:, :], order_f[:, :]).then_inc(order_ready, 1)

            st.then(dve.tensor_tensor(start128[:, :], ends, tiles_of[:, 0, :], ALU.subtract))
            st.then(dve.tensor_scalar(start128[:, :], start128[:, :], float(P), None, ALU.mult))
            st.then(dve.tensor_tensor(place16, bank[:, 0, 0:ALLT * NE].rearrange("p (t e) -> p t e", e=NE),
                                      start128[:, :].unsqueeze(1).broadcast_to([P, ALLT, NE]), ALU.add))
            st.along(dve.tensor_tensor(prod16, pick[:, 0, :, :], place16, ALU.mult))
            st.then(dve.tensor_tensor(both, pick[:, 1, :, :], place16, ALU.mult))
            st.along(dve.tensor_reduce(slot_f[:, 0, :], prod16, AX, ALU.add))
            st.then(dve.tensor_reduce(slot_f[:, 1, :], both, AX, ALU.add))
            st.then(dve.tensor_copy(slot_i[:, :, :], slot_f[:, :, :]))
            st.along(dve.tensor_scalar(row_i[:, :, :], slot_i[:, :, :], P - 1, None, ALU.bitwise_and))
            st.then(dve.tensor_scalar(tile_i[:, :, :], slot_i[:, :, :], 7, None, ALU.logical_shift_right))
            kt = "p k t -> p (k t)"
            dve.wait_ge(out_done, ALLT)
            st.along(dve.tensor_tensor(row_f[:, :, :], row_i[:, :, :], nowhere[:, :, :], ALU.add))
            st.then(dve.tensor_copy(tile_f[:, :, :], tile_i[:, :, :]))
            gates = gate[:, :, :].rearrange(kt)
            dve.tensor_tensor(tile_hot, bc(tile_f[:, :, :].rearrange(kt), PLANNED),
                              iota_row[:, 0:PLANNED].unsqueeze(1).broadcast_to([P, 2 * ALLT, PLANNED]), ALU.is_equal).then_inc(tile_hot_ready, 1)
            st.along(dve.tensor_copy(gate_h[:, :], gates))
            halves = [slice(k * ALLT, (k + 1) * ALLT) for k in range(2)]
            def hot_rows(j):
                return dve.tensor_tensor(row_hot[:, j, :], bc(row_f[:, :, :].rearrange(kt)[:, j], P),
                                         iota_row[:, :].unsqueeze(1).broadcast_to([P, ALLT, P]), ALU.is_equal)
            st.then(hot_rows(halves[0]))
            st.then(dve.tensor_tensor(gates, gates, gate_h[:, :].bitcast(F32), ALU.subtract))
            dve.wait_ge(tile_hot_ready, 1)
            for k, j in enumerate(halves):
                st.along(dve.tensor_tensor(payload[:, j, 1, :], tile_hot[:, j, :], bc(gate_h[:, j].bitcast(F32), PLANNED), ALU.mult))
                dve.tensor_tensor(payload[:, j, 2, :], tile_hot[:, j, :], bc(gates[:, j], PLANNED), ALU.mult).then_inc(table_in_ready, 1)
                if k == 0:
                    st.then(hot_rows(halves[1]))

            def w_piece_lo(j, q, at):
                dve.wait_ge(w_hi_ready, piece_no(j, q) + 1)
                dve.tensor_tensor(el[:, ds(at + q * D, D)], piece_in[piece_buf(q)][:, :], eh[:, ds(at + q * D, D)].bitcast(F32),
                                  ALU.subtract).then_inc(w_lo_ready, 1)

            for k in range(2):
                dve.wait_ge(xn2_stored[k], 16 * (TILES // 2 + 1 - k))
            w_piece_lo(0, 0, 0)
            st.along(dve.memset(slot_tok[:, PLANNED:PLANNED + 1], 0))
            st.along(dve.tensor_scalar(last_j[:, :], order[:, NE - 1:NE], -1.0, None, ALU.add))
            ends_used = count[:, :]
            st.then(dve.tensor_scalar(ends_used, tiles_of[:, 0, :], 0.0, float(PLANNED), ALU.is_equal, ALU.mult))
            st.then(dve.tensor_tensor(ends_used, ends_used, ends, ALU.add))
            dve.wait_ge(table_done, 1)
            dve.tensor_copy(slot_tok[:, 0:PLANNED], bank[:, 2, 0:PLANNED]).then_inc(slots_ready, 1)
            st.then(dve.tensor_copy(slot_gate[:, :], bank[:, 2, PLANNED:2 * PLANNED]))
            st.then(dve.tensor_tensor(slot_gate[:, :], slot_gate[:, :], bank[:, 2, 2 * PLANNED:3 * PLANNED], ALU.add))
            for q in range(1, GU):
                w_piece_lo(0, q, 0)

            def x_lo(u):
                dve.wait_ge(xg_hi_ready, u + 1)
                dve.tensor_tensor(xgl[:, :, :], bank[:, 0:2, :].rearrange("p b (c t) -> p (b c) t", t=P), xgh[:, :, :].bitcast(F32),
                                  ALU.subtract).then_inc(xgT_ready, 1)

            st.then(dve.tensor_tensor(cmp16, ends_used.unsqueeze(1).broadcast_to([P, PLANNED, NE]), bc(iota_row[:, 0:PLANNED], NE), ALU.is_le))
            st.then(dve.tensor_reduce(tile_j[:, :], cmp16, AX, ALU.add))
            st.then(dve.tensor_scalar(tile_j[:, :], tile_j[:, :], last_j[:, 0:1], None, ALU.min))
            n = PLANNED - 1
            st.then(dve.tensor_scalar(two_on[:, :], tile_j[:, :], 2.0, None, ALU.add))
            st.along(dve.memset(flag[:, 0:1], 1.0))
            st.along(dve.tensor_scalar(two_on[:, :], two_on[:, :], last_j[:, 0:1], None, ALU.is_le))
            st.then(dve.tensor_tensor(flag[:, 1:PLANNED], tile_j[:, 1:PLANNED], tile_j[:, 0:n], ALU.subtract))
            st.then(dve.tensor_tensor(flag[:, 1:PLANNED], flag[:, 1:PLANNED], two_on[:, 0:n], ALU.mult))
            x_lo(0)
            for q in range(GU, PIECES):
                w_piece_lo(0, q, 0)
            packed = plan_f[:, PL_TILE:PL_TILE + n]
            st.along(dve.memset(plan_f[:, PL_TILE + n:PL_TILE + PLANNED], 0.0))
            st.along(dve.tensor_copy(plan_f[:, PL_TILES:PL_TILES + 1], ends[:, NE - 1:NE]))
            for k in range(2):
                st.along(dve.tensor_scalar(plan_f[:, PL_STORED + k:PL_STORED + k + 1], ends[:, NE - 1:NE], float(1 - k), None, ALU.add))
            st.then(dve.scalar_tensor_tensor(out=packed, in0=tile_j[:, 1:PLANNED], scalar=float(1 << J_BITS), in1=tile_j[:, 0:n],
                                             op0=ALU.mult, op1=ALU.add))
            for which, bit in ((flag[:, 0:n], DOWN_TOO), (flag[:, 1:PLANNED], GATE_UP_TOO)):
                st.then(dve.scalar_tensor_tensor(out=packed, in0=which, scalar=float(bit), in1=packed, op0=ALU.mult, op1=ALU.add))
            st.then(dve.tensor_copy(plan[:, :], plan_f[:, :]))
            st.then(dve.tensor_scalar(plan[:, PL_STORED:PL_ALL], plan[:, PL_STORED:PL_ALL], 1, None, ALU.logical_shift_right))
            dve.tensor_scalar(plan[:, PL_STORED:PL_ALL], plan[:, PL_STORED:PL_ALL], 4, None, ALU.logical_shift_left).then_inc(plan_ready, 1)

            def hidden(u, k):
                dve.wait_ge(silu_ready, u + 1)
                qc = "p (q c) -> p q c"
                dve.scalar_tensor_tensor(out=hid[k].rearrange("p c q -> p q c"), in0=bank[:, 2 + k, FE:2 * FE].rearrange(qc, c=FC),
                                         scalar=slot_gate[:, col(u)], in1=silu[k].rearrange(qc, c=FC), op0=ALU.mult, op1=ALU.mult).then_inc(hid_ready, 1)

            def y_out(u, k):
                if late(u, 2):
                    dve.wait_ge(y_stored[k], u // 2 * 16 if isinstance(u, int) else (u - k) * 8)
                dve.wait_ge(y_done, u * 2 + 2)
                dve.tensor_copy(y_sb[k][:, 512:D], bank[:, 6, :]).then_inc(y_right_ready, 1)

            def hid_lo(u):
                dve.wait_ge(hid_hi_ready, u + 1)
                dve.tensor_tensor(hTl[:, :, :], bank[:, 4, 0:FE].rearrange("p (c t) -> p c t", c=FC), hTh[:, :, :].bitcast(F32),
                                  ALU.subtract).then_inc(hidT_ready, 1)

            def tile(u, k):
                packed = dve.value_load(plan[0:1, ds(u + PL_TILE, 1)], min_val=0, max_val=2 * GATE_UP_TOO - 1)
                j = packed & (NE - 1)
                at = (packed & 1) * EW
                hid_lo(u)
                with dve.If((packed & DOWN_TOO) > 0):
                    for q in range(GU, PIECES):
                        w_piece_lo(j + 1, q, at * -1 + EW)
                with dve.If((packed & GATE_UP_TOO) > 0):
                    for q in range(GU_FIRST):
                        w_piece_lo(j + 2, q, at)
                hidden(u + 1, 1 - k)
                x_lo(u + 2)
                with dve.If((packed & GATE_UP_TOO) > 0):
                    for q in range(GU_FIRST, GU):
                        w_piece_lo(j + 2, q, at)
                y_out(u, k)

            dve.wait_ge(plan_ready, 1)
            tiles_used = dve.value_load(plan[0:1, PL_TILES:PL_TILES + 1], min_val=LEAST_TILES, max_val=SLOT_TILES)
            for q in range(GU):
                w_piece_lo(1, q, EW)
            hidden(0, 0)
            x_lo(1)
            tile(0, 0)
            tile(1, 1)
            with dve.Fori(1, LEAST_TILES // 2) as i:
                for k in range(2):
                    tile(i * 2 + k, k)
            with dve.Fori(LEAST_TILES // 2, SLOT_TILES // 2) as i:
                for k in range(2):
                    with dve.If(i * 2 + k < tiles_used):
                        tile(i * 2 + k, k)
                        dve.sem_inc(dve_held, 1)

            def add_pair(t, k, arrived):
                n = rows_of(t)
                dve.wait_ge(pair_gathered[k], arrived)
                st.then(dve.tensor_tensor(x2_of(t), x2_of(t), pair_rows[k][0][0:n, :], ALU.add))
                dve.tensor_tensor(x2_of(t), x2_of(t), pair_rows[k][1][0:n, :], ALU.add).then_inc(x3_ready, 1)

            def last_norm(t, k, free):
                n = rows_of(t)
                dve.wait_ge(rstd3_ready, t + 1)
                if late(t, LB):
                    dve.wait_ge(out_stored[k], free)
                dve.scalar_tensor_tensor(out=out_rows[k][0:n, :], in0=x2_of(t), scalar=rstd[2][0:n, col(t)], in1=gf[0:n, :],
                                         op0=ALU.mult, op1=ALU.mult).then_inc(out_ready, 1)

            dve.wait_ge(gf_in, 16)
            add_pair(0, 0, 32)
            add_pair(1, 1, 32)
            last_norm(0, 0, 0)
            add_pair(2, 2, 32)
            last_norm(1, 1, 0)

            for i in range(1, ALLT // LB):
                for k in range(LB):
                    t = i * LB + k
                    add_pair(t, k, i * 32 + 32)
                    last_norm(t - 1, (t - 1) % LB, (t - 1) // LB * 16)
            last_norm(ALLT - 1, LB - 1, (ALLT - 1) // LB * 16)


CONST_ALL = 28


_INS = ["x_prompt", "x_sample", "cache_k_win", "cache_v_win", "state_conv", "norm1_g", "w_in", "conv_w", "sinks",
        "attn_out_g", "conv_out_g", "w_out", "norm2_g", "w_group", "b_group", "w_fine", "b_fine", "w_gate", "w_up",
        "w_down", "final_g"]
_OUTS = [(1, SEQ, D), (NS, 1, D), (1, 1, P, NKV, HD), (1, 1, P, NKV, HD), (1, 1, 2, CONV),
         (1, NS, P, NKV, HD), (1, NS, P, NKV, HD), (1, NS, 2, CONV)]


def kernel(**inputs):
    import numpy as _np
    import concourse.bacc as _bacc
    from concourse import mybir as _mybir
    from concourse.bass_utils import run_bass_kernel_spmd as _run

    nc = _bacc.Bacc("TRN2", target_bir_lowering=False, num_devices=1)
    arrays, args = {}, []
    for name in _INS:
        a = _np.ascontiguousarray(inputs[name])
        arrays[f"in_{name}_dram"] = a
        args.append(nc.dram_tensor(f"in_{name}_dram", a.shape, _mybir.dt.from_np(a.dtype), kind="ExternalInput").ap())
    for i, shape in enumerate(_OUTS):
        args.append(nc.dram_tensor(f"out_{i}_dram", shape, _mybir.dt.float32, kind="ExternalOutput").ap())
    hybrid_layer_step(nc, *args)
    r = _run(nc, [arrays], core_ids=[0])
    return tuple(r.results[0][f"out_{i}_dram"] for i in range(len(_OUTS)))
```
